# Optimizing a Trainium2 kernel written in Bass

```python
import jax, jax.numpy as jnp
from jax import lax
import numpy as np

D_MODEL = 2048
BATCH = 1
SEQ = 512
DEPTH = 1

PLE_DIM = 256
MLA_HEADS = 8
QK_NOPE = 128
QK_ROPE = 64
V_HEAD = 128
Q_LORA = 512
KV_LORA = 256
ROPE_THETA = 10000.0
Q_BLOCK = 128
SGU_GROUPS = 8
SGU_GROUP_DIM = 128
CHUNK = 128
MLA_WIDTH = MLA_HEADS * V_HEAD
SGU_WIDTH = SGU_GROUPS * SGU_GROUP_DIM
MIX_WIDTH = MLA_WIDTH + SGU_WIDTH
OFF_CKV = Q_LORA
OFF_KR = Q_LORA + KV_LORA
OFF_U = OFF_KR + QK_ROPE
OFF_V = OFF_U + SGU_WIDTH
IN_COLS = OFF_V + SGU_WIDTH
PEER_HEADS = 8
PEER_KEYS = 128
PEER_QDIM = 256
PEER_TOPK = 16
N_EXPERTS = PEER_KEYS * PEER_KEYS
EPS = 1e-6

kernel_name = "hymba_mla_sgu_peer_ple_block"

def rmsnorm(x, g):
    xf = x.astype(jnp.float32)
    y = xf * lax.rsqrt(jnp.mean(xf * xf, axis=-1, keepdims=True) + EPS)
    return (y * g.astype(jnp.float32)).astype(x.dtype)

def layernorm(x, g, b):
    xf = x.astype(jnp.float32)
    mu = jnp.mean(xf, axis=-1, keepdims=True)
    xc = xf - mu
    y = xc * lax.rsqrt(jnp.mean(xc * xc, axis=-1, keepdims=True) + EPS)
    return (y * g.astype(jnp.float32) + b.astype(jnp.float32)).astype(x.dtype)

def rope(x, pos):
    half = x.shape[-1] // 2
    freqs = ROPE_THETA ** (-jnp.arange(half, dtype=jnp.float32) / half)
    ang = pos.astype(jnp.float32)[..., None] * freqs
    cos = jnp.cos(ang)[:, :, None, :]
    sin = jnp.sin(ang)[:, :, None, :]
    xf = x.astype(jnp.float32)
    x1, x2 = xf[..., :half], xf[..., half:]
    out = jnp.concatenate([x1 * cos - x2 * sin, x2 * cos + x1 * sin], axis=-1)
    return out.astype(x.dtype)

def causal_block_attention(q, k, v):
    B, S, H, Dq = q.shape
    nb = S // Q_BLOCK
    scale = Dq ** -0.5
    qb = jnp.moveaxis(q.reshape(B, nb, Q_BLOCK, H, Dq), 1, 0)
    k_pos = jnp.arange(S)

    def one(args):
        q_blk, start = args
        s = jnp.einsum('bqhd,bkhd->bhqk', q_blk, k, preferred_element_type=jnp.float32) * scale
        q_pos = start + jnp.arange(Q_BLOCK)
        mask = k_pos[None, :] <= q_pos[:, None]
        s = jnp.where(mask[None, None], s, -jnp.inf)
        pr = jax.nn.softmax(s, axis=-1)
        return jnp.einsum('bhqk,bkhd->bqhd', pr.astype(v.dtype), v)

    starts = jnp.arange(nb) * Q_BLOCK
    out = lax.map(one, (qb, starts))
    return jnp.moveaxis(out, 0, 1).reshape(B, S, H, v.shape[-1])

def mla(c_q, c_kv, k_r, pos, g_cq, w_uq, g_ckv, w_ukv):
    B, S, _ = c_q.shape
    q = (rmsnorm(c_q, g_cq) @ w_uq).reshape(B, S, MLA_HEADS, QK_NOPE + QK_ROPE)
    kv = (rmsnorm(c_kv, g_ckv) @ w_ukv).reshape(B, S, MLA_HEADS, QK_NOPE + V_HEAD)
    q_nope, q_rope = q[..., :QK_NOPE], rope(q[..., QK_NOPE:], pos)
    k_nope, v = kv[..., :QK_NOPE], kv[..., QK_NOPE:]
    k_rope = rope(k_r[:, :, None, :], pos)
    q = jnp.concatenate([q_nope, q_rope], axis=-1)
    k = jnp.concatenate([k_nope, jnp.broadcast_to(k_rope, (B, S, MLA_HEADS, QK_ROPE))], axis=-1)
    o = causal_block_attention(q, k, v)
    return o.reshape(B, S, MLA_WIDTH)

def chunked_sgu(u, v, g_ln, b_ln, w_s, b_s):
    B, S, _ = u.shape
    nc = S // CHUNK
    u = jax.nn.gelu(u).reshape(B, nc, CHUNK, SGU_GROUPS, SGU_GROUP_DIM)
    v = layernorm(jax.nn.gelu(v).reshape(B, S, SGU_GROUPS, SGU_GROUP_DIM), g_ln, b_ln)
    v = v.reshape(B, nc, CHUNK, SGU_GROUPS, SGU_GROUP_DIM)
    w = w_s * jnp.tril(jnp.ones((CHUNK, CHUNK), dtype=w_s.dtype))[None]
    mixed = jnp.einsum('gts,bcsgd->bctgd', w, v) + jnp.transpose(b_s)[None, None, :, :, None]
    return (u * mixed).reshape(B, S, SGU_WIDTH)

def peer(a, w_q, k1, k2, u_exp, v_exp):
    B, S, D = a.shape
    half = PEER_QDIM // 2
    q = (a @ w_q).reshape(B, S, PEER_HEADS, PEER_QDIM)
    s1 = jnp.einsum('bshd,hnd->bshn', q[..., :half], k1, preferred_element_type=jnp.float32)
    s2 = jnp.einsum('bshd,hnd->bshn', q[..., half:], k2, preferred_element_type=jnp.float32)
    t1, i1 = lax.top_k(s1, PEER_TOPK)
    t2, i2 = lax.top_k(s2, PEER_TOPK)
    cand = (t1[..., :, None] + t2[..., None, :]).reshape(B, S, PEER_HEADS, PEER_TOPK * PEER_TOPK)
    cand_idx = (i1[..., :, None] * PEER_KEYS + i2[..., None, :]).reshape(B, S, PEER_HEADS, PEER_TOPK * PEER_TOPK)
    top, sel = lax.top_k(cand, PEER_TOPK)
    experts = jnp.take_along_axis(cand_idx, sel, axis=-1)
    gates = jax.nn.softmax(top, axis=-1)
    nc = S // CHUNK

    def to_chunks(t):
        return jnp.moveaxis(t.reshape((B, nc, CHUNK) + t.shape[2:]), 1, 0)

    def one(args):
        a_c, e_c, g_c = args
        u_sel = jnp.take(u_exp, e_c, axis=0)
        h = jnp.einsum('bthkd,btd->bthk', u_sel, a_c, preferred_element_type=jnp.float32)
        w = (g_c * jax.nn.gelu(h)).astype(a_c.dtype)
        v_sel = jnp.take(v_exp, e_c, axis=0)
        return jnp.einsum('bthk,bthkd->btd', w, v_sel)

    out = lax.map(one, (to_chunks(a), to_chunks(experts), to_chunks(gates)))
    return jnp.moveaxis(out, 0, 1).reshape(B, S, D)

def setup_inputs(seed: int = 0) -> dict:
    key = jax.random.key(seed)
    ks = iter(jax.random.split(key, 40))

    def nrm(shape, scale):
        return jax.random.normal(next(ks), shape, dtype=jnp.float32) * scale

    def gain(shape):
        return 1.0 + nrm(shape, 0.02)

    L = DEPTH
    x = nrm((BATCH, SEQ, D_MODEL), 1.0)
    p = nrm((DEPTH, BATCH, SEQ, PLE_DIM), 1.0)
    positions = (jax.random.randint(next(ks), (BATCH, 1), 0, 4096, dtype=jnp.int32)
                 + jnp.arange(SEQ, dtype=jnp.int32)[None, :])
    return {
        "x": x,
        "p": p,
        "positions": positions,
        "g_mix": gain((L, D_MODEL)),
        "w_in": nrm((L, D_MODEL, IN_COLS), D_MODEL ** -0.5),
        "g_cq": gain((L, Q_LORA)),
        "w_uq": nrm((L, Q_LORA, MLA_HEADS * (QK_NOPE + QK_ROPE)), Q_LORA ** -0.5),
        "g_ckv": gain((L, KV_LORA)),
        "w_ukv": nrm((L, KV_LORA, MLA_HEADS * (QK_NOPE + V_HEAD)), KV_LORA ** -0.5),
        "g_ln_sgu": gain((L, SGU_GROUPS, SGU_GROUP_DIM)),
        "b_ln_sgu": nrm((L, SGU_GROUPS, SGU_GROUP_DIM), 0.02),
        "w_sgu": nrm((L, SGU_GROUPS, CHUNK, CHUNK), CHUNK ** -0.5),
        "b_sgu": gain((L, SGU_GROUPS, CHUNK)),
        "g_out_attn": gain((L, MLA_WIDTH)),
        "g_out_sgu": gain((L, SGU_WIDTH)),
        "w_out": nrm((L, MIX_WIDTH, D_MODEL), MIX_WIDTH ** -0.5),
        "g_ffn": gain((L, D_MODEL)),
        "w_peer_q": nrm((L, D_MODEL, PEER_HEADS * PEER_QDIM), D_MODEL ** -0.5),
        "peer_k1": nrm((L, PEER_HEADS, PEER_KEYS, PEER_QDIM // 2), (PEER_QDIM // 2) ** -0.5),
        "peer_k2": nrm((L, PEER_HEADS, PEER_KEYS, PEER_QDIM // 2), (PEER_QDIM // 2) ** -0.5),
        "peer_u": nrm((L, N_EXPERTS, D_MODEL), D_MODEL ** -0.5),
        "peer_v": nrm((L, N_EXPERTS, D_MODEL), PEER_HEADS ** -0.5),
        "g_ple": gain((L, D_MODEL)),
        "w_ple_gate": nrm((L, D_MODEL, D_MODEL), D_MODEL ** -0.5),
        "w_ple_proj": nrm((L, PLE_DIM, D_MODEL), PLE_DIM ** -0.5),
        "g_final": gain((D_MODEL,)),
    }

def reference(x, p, positions, g_mix, w_in, g_cq, w_uq, g_ckv, w_ukv, g_ln_sgu, b_ln_sgu,
              w_sgu, b_sgu, g_out_attn, g_out_sgu, w_out, g_ffn, w_peer_q, peer_k1, peer_k2,
              peer_u, peer_v, g_ple, w_ple_gate, w_ple_proj, g_final):
    h = x
    for i in range(DEPTH):
        z = rmsnorm(h, g_mix[i]) @ w_in[i]
        c_q = z[..., :OFF_CKV]
        c_kv = z[..., OFF_CKV:OFF_KR]
        k_r = z[..., OFF_KR:OFF_U]
        u = z[..., OFF_U:OFF_V]
        v = z[..., OFF_V:]
        o_attn = rmsnorm(mla(c_q, c_kv, k_r, positions, g_cq[i], w_uq[i], g_ckv[i], w_ukv[i]),
                         g_out_attn[i])
        o_sgu = rmsnorm(chunked_sgu(u, v, g_ln_sgu[i], b_ln_sgu[i], w_sgu[i], b_sgu[i]),
                        g_out_sgu[i])
        h = h + jnp.concatenate([o_attn, o_sgu], axis=-1) @ w_out[i]
        h = h + peer(rmsnorm(h, g_ffn[i]), w_peer_q[i], peer_k1[i], peer_k2[i], peer_u[i], peer_v[i])
        gate = jax.nn.sigmoid(rmsnorm(h, g_ple[i]) @ w_ple_gate[i])
        h = h + gate * (p[i] @ w_ple_proj[i])
    return rmsnorm(h, g_final)


_drawn_inputs = setup_inputs


def setup_inputs(seed=0):
    import zlib

    import numpy as np

    out = dict(_drawn_inputs(seed))
    spreads = {}
    factors = {'g_cq': 3.633,
     'g_ckv': 2.765,
     'g_ln_sgu': 23.554,
     'b_ln_sgu': 25.01,
     'b_sgu': 16.718,
     'g_out_attn': 10.805,
     'g_out_sgu': 11.006,
     'g_ffn': 10.756,
     'g_ple': 64.0,
     'g_final': 7.494}
    for name, (base, spread) in spreads.items():
        noise = np.random.default_rng([zlib.crc32(name.encode()), seed]).standard_normal(out[name].shape)
        drawn = base * np.exp(spread * noise) if base else spread * noise
        out[name] = __import__('jax').numpy.asarray(drawn.astype(out[name].dtype))
    for name, factor in factors.items():
        out[name] = (out[name] * factor).astype(out[name].dtype)
    return out
```

```python
import math

import concourse.bass as bass
from concourse import mybir
from contextlib import ExitStack, contextmanager

P = 128
T = 512
NT = T // P
D = 2048
KD = D // P
HEADS = 8
ROPE_D = 64
QL, KVL = 512, 256
KQ, KKV = QL // P, KVL // P
SGU_TILES = 8
TOPK = 16
KEYS = 128
EPS = 1e-6
GROUP = 4
NGROUPS = KEYS // GROUP
TB = 32
NTB = T // TB
QUADS = T // 4
SCALE = float(128 + ROPE_D) ** -0.5
PI = math.pi
PI_BELOW = 3.1415925
def two_pi_parts():
    parts, left = [], 2 * PI
    for _ in range(3):
        scale = 2.0 ** (8 - math.frexp(left)[1])
        parts.append(math.floor(left * scale) / scale)
        left -= parts[-1]
    return parts + [left]


ROUND = 12582912.0

PEER_SLOTS = [1] * GROUP + [1, 4] * (GROUP * (NGROUPS - 1)) + [4] * GROUP
STREAM = [("v", [1, 1, 1, 4] * 2), ("u", [1] * 8), ("c", [1] * 7), ("uq", [4] * 3), ("ukv", [8] * 2),
          ("out", [1] * 16), ("pq", [1] * 16), ("peer", PEER_SLOTS), ("proj", [8] * 2), ("gate", [1] * 16)]
S0 = {}
CUM = {-2: 0, -1: 0}
_n = 0
for _name, _marks in STREAM:
    S0[_name] = _n
    for _m in _marks:
        CUM[_n] = CUM[_n - 1] + _m
        _n += 1
NSLOTS = _n

GAINS = {}
_c = 0
for _name, _k in (("mix", KD), ("ffn", KD), ("ple", KD), ("final", KD), ("attn", 8), ("sgu", 8), ("cq", KQ), ("ckv", KKV)):
    GAINS[_name] = _c
    _c += _k
NGAINS = _c


class Steps:

    def __init__(self, eng, sem):
        self.eng, self.sem, self.base, self.k = eng, sem, 0, 0

    def did(self, ins):
        ins.then_inc(self.sem, 1)
        self.k += 1

    def settle(self):
        self.eng.wait_ge(self.sem, self.base + self.k)

    @contextmanager
    def loop(self, count, per):
        start = self.base + self.k
        with self.eng.Fori(0, count) as i:
            self.base, self.k = start + i * per, 0
            yield i
            assert self.k == per, (self.k, per)
        self.base, self.k = start + count * per, 0


def trunk_layer(nc, a, stream, out, gates_dram):
    F, R, U32, I32 = mybir.dt.float32, mybir.dt.float32r, mybir.dt.uint32, mybir.dt.int32
    ACT = mybir.ActivationFunctionType
    ALU = mybir.AluOpType
    AX = mybir.AxisListType.X

    base = (nc.sbuf_base + 31) // 32 * 32
    KB = 1024

    def at(name, shape, dt, offset):
        return nc.alloc_sbuf_tensor_at(name, [P] + shape, dt, offset=base + offset)

    H0, A0, RING0, W0, M0, C0 = 0, 32 * KB, 96 * KB, 144 * KB, 176 * KB, 192 * KB
    hT = at("hT", [KD, T], F, H0)
    vtok = at("vtok", [NT, 1024], F, H0)
    cT = at("cT", [7, T], F, H0 + 16 * KB)
    perm = at("perm", [P], F, H0 + 30 * KB)
    ln_stats = at("ln_stats", [8, 6], F, H0 + 30 * KB + 512)
    ln_mv = at("ln_mv", [8, 2], F, H0 + 30 * KB + 704)
    ln_rstd = at("ln_rstd", [8], F, H0 + 30 * KB + 768)
    freq = at("freq", [2], F, H0 + 30 * KB + 800)
    aH = at("aH", [KD, T], R, A0)
    aL = at("aL", [KD, T], R, A0 + 32 * KB)
    qT = at("qT", [12, T], F, A0)
    kT = at("kT", [HEADS, T], F, A0 + 24 * KB)
    vA = at("vA", [NT, 1024], F, A0 + 40 * KB)
    ckvH = at("ckvH", [KKV, T], R, A0 + 56 * KB)
    ckvL = at("ckvL", [KKV, T], R, A0 + 60 * KB)
    raw = [at(f"raw{i}", [2048], F, RING0 + 8 * KB * i) for i in range(2)]
    wH = [at(f"wH{i}", [2048], R, RING0 + (16 + 8 * i) * KB) for i in range(2)]
    wL = [at(f"wL{i}", [2048], R, RING0 + (32 + 8 * i) * KB) for i in range(2)]
    mixT = at("mixT", [KD, T], F, W0)
    cqH = at("cqH", [KQ, T], R, W0)
    cqL = at("cqL", [KQ, T], R, W0 + 8 * KB)
    pqT = [at(f"pqT{i}", [2, T], F, W0 + 4 * KB * i) for i in range(2)]
    keys = at("keys", [HEADS, 2, KEYS], F, W0 + 8 * KB)
    gstage = [at(f"gstage{i}", [KEYS, TB], F, W0 + 16 * KB * i) for i in range(2)]
    actH = [at(f"actH{i}", [GROUP, T], R, W0 + 16 * KB * i) for i in range(2)]
    actL = [at(f"actL{i}", [GROUP, T], R, W0 + 16 * KB * i + 8 * KB) for i in range(2)]
    projT = at("projT", [KD, T], F, W0)
    sgu_rows = at("sgu_rows", [3, 8, P], F, M0)
    wsT = at("wsT", [8, P], F, M0 + 12 * KB)
    cosT = at("cosT", [T], F, M0)
    sinT = at("sinT", [T], F, M0 + 2 * KB)
    krT = at("krT", [T], F, M0 + 4 * KB)
    prob = [at(f"prob{i}", [T], F, M0 + (6 + 2 * i) * KB) for i in range(2)]
    probT = [at(f"probT{i}", [T], F, M0 + (10 + 2 * i) * KB) for i in range(2)]
    rstdB = at("rstdB", [T], F, M0 + 14 * KB)
    rest = at("rest", [8, KEYS], F, M0)
    match = at("match", [NT, TOPK, TOPK], F, M0)
    cand = at("cand", [NT, 256], F, M0 + 4 * KB)
    cand_rest = at("cand_rest", [NT, 256], F, M0 + 8 * KB)
    top = at("top", [2, NT, TOPK], F, M0 + 12 * KB)
    top_at = at("top_at", [2, NT, TOPK], U32, M0 + 12 * KB + 512)
    top_atf = at("top_atf", [2, NT, TOPK], F, M0 + 13 * KB)
    best = at("best", [NT, TOPK], F, M0 + 13 * KB + 512)
    best_at = at("best_at", [NT, TOPK], U32, M0 + 13 * KB + 768)
    best_k = at("best_k", [2, NT, TOPK], U32, M0 + 14 * KB)
    best_kf = at("best_kf", [2, NT, TOPK], F, M0 + 14 * KB + 512)
    gate_e = at("gate_e", [NT, TOPK], F, M0 + 15 * KB)
    gate_sum = at("gate_sum", [NT], F, M0 + 15 * KB + 256)
    gate_inv = at("gate_inv", [NT], F, M0 + 15 * KB + 288)
    hk = at("hk", [3, T], F, M0)
    oh1 = at("oh1", [2, 4, P], F, M0 + 6 * KB)
    oh2 = at("oh2", [2, 4, P], F, M0 + 10 * KB)
    gtile = [at(f"gtile{i}", [NTB, GROUP, TB], F, M0 + 8 * KB * i) for i in range(2)]
    pRaw = at("pRaw", [2, T], F, M0)
    pH = at("pH", [2, T], R, M0 + 8 * KB)
    pL = at("pL", [2, T], R, M0 + 12 * KB)
    tmp = [at(f"tmp{i}", [T], F, C0 + 2 * KB * i) for i in range(2)]
    sq = [at(f"sq{i}", [T], F, C0 + (4 + 2 * i) * KB) for i in range(2)]
    route = at("route", [3, NT, P], F, C0)
    ssum = at("ssum", [T], F, C0 + 8 * KB)
    rstd = at("rstd", [T], F, C0 + 10 * KB)
    ident = at("ident", [P], F, C0 + 12 * KB)
    iota = at("iota", [P], F, C0 + 12 * KB + 512)
    identR = at("identR", [P], R, C0 + 13 * KB)
    causalR = at("causalR", [P], R, C0 + 13 * KB + 512)
    ones = at("ones", [P], F, C0 + 14 * KB)
    gains = at("gains", [NGAINS], F, C0 + 14 * KB + 512)
    smax = at("smax", [32], F, C0 + 14 * KB + 864)
    nbias = at("nbias", [32], F, C0 + 14 * KB + 992)
    rsum = at("rsum", [32], F, C0 + 14 * KB + 1120)
    rinv = at("rinv", [32], F, C0 + 14 * KB + 1248)
    held = at("held", [1], F, C0 + 14 * KB + 1376)

    ctx = ExitStack()
    with ctx:
        ps = ctx.enter_context(nc.psum_tensor("ps", [P, 8, 512], F))

        def sem(name):
            return ctx.enter_context(nc.semaphore(name))

        x_loaded = [sem(f"x_loaded{i}") for i in range(4)]
        consts_loaded = sem("consts_loaded")
        rows_loaded, perm_loaded = sem("rows_loaded"), sem("perm_loaded")
        raw_loaded = [sem(f"raw_loaded{i}") for i in range(2)]
        hi_ready, lo_ready, tile_done = sem("hi_ready"), sem("lo_ready"), sem("tile_done")
        dve_step, act_step, pool_step = sem("dve_step"), sem("act_step"), sem("pool_step")
        consts_ready = sem("consts_ready")
        causal_built = sem("causal_built")
        sq_ready, sq_added, sum_done, mean_ready, root_ready, rstd_ready = (
            sem("sq_ready"), sem("sq_added"), sem("sum_done"), sem("mean_ready"), sem("root_ready"), sem("rstd_ready"))
        act_scaled, act_hi, act_lo = sem("act_scaled"), sem("act_hi"), sem("act_lo")
        v_gelu, ln_var, ln_std, v_ready, u_gelu = sem("v_gelu"), sem("ln_var"), sem("ln_std"), sem("v_ready"), sem("u_gelu")
        c_copied = sem("c_copied")
        mix_done, sgu_ready = sem("mix_done"), sem("sgu_ready")
        angle_ready, trig_ready = sem("angle_ready"), sem("trig_ready")
        pos_loaded = sem("pos_loaded")
        uq_copied, swap_done, rope_ready = sem("uq_copied"), sem("swap_done"), sem("rope_ready")
        kv_copied = sem("kv_copied")
        score_done, nbias_ready, exp_done, p_ready = sem("score_done"), sem("nbias_ready"), sem("exp_done"), sem("p_ready")
        pt_done, pt_copied, pv_done, o_copied = sem("pt_done"), sem("pt_copied"), sem("pv_done"), sem("o_copied")
        x_again = sem("x_again")
        h_mixed = sem("h_mixed")
        keys_loaded = sem("keys_loaded")
        pq_copied, ps_done, tops_done, gate_sub, gate_exp, routed = (
            sem("pq_copied"), sem("ps_done"), sem("tops_done"), sem("gate_sub"), sem("gate_exp"), sem("routed"))
        hkT_done, hk_ready = sem("hkT_done"), sem("hk_ready")
        onehot_ready, gquad_done, gquad_copied = sem("onehot_ready"), sem("gquad_done"), sem("gquad_copied")
        gates_stored = [sem(f"gates_stored{i}") for i in range(2)]
        gates_loaded = [sem(f"gates_loaded{i}") for i in range(2)]
        gelu_done, act_gated, act_whi, act_wlo, h_acc = (
            sem("gelu_done"), sem("act_gated"), sem("act_whi"), sem("act_wlo"), sem("h_acc"))
        p_loaded, p_hi, p_lo, proj_copied = sem("p_loaded"), sem("p_hi"), sem("p_lo"), sem("proj_copied")
        sig_done, h_gated = sem("sig_done"), sem("h_gated")
        out_ready, out_stored = sem("out_ready"), sem("out_stored")

        block = ctx.enter_context(nc.Block())

        def gain(name, k):
            return gains[:, GAINS[name] + k:GAINS[name] + k + 1]

        N_SQ = {}
        _at = 0
        for name, k in (("mix", 16), ("cq", 4), ("ckv", 2), ("sgu", 8), ("attn", 8), ("ffn", 16), ("ple", 16), ("final", 16)):
            N_SQ[name] = _at
            _at += k
        NORMS = {n: i for i, n in enumerate(N_SQ)}
        N_SC = {}
        _at = 0
        for name, k in (("mix", 16), ("cq", 4), ("ckv", 2), ("out", 16), ("ffn", 16), ("ple", 16)):
            N_SC[name] = _at
            _at += k

        @block.sync
        def _(sp):
            def load(n, src, parity):
                sp.wait_ge(lo_ready, n - 1)
                sp.dma_start(raw[parity][:, :], src).then_inc(raw_loaded[parity], 16)

            for i in range(4):
                sp.dma_start(hT[:, 4 * i:4 * i + 4, :], a["x"][:, 4 * i:4 * i + 4, :]).then_inc(x_loaded[i], 16)
            for n in range(2):
                sp.dma_start(raw[n][:, :], stream["v"][n, :, :]).then_inc(raw_loaded[n], 16)
            for n in range(2, 8):
                load(n, stream["v"][n, :, :], n % 2)
            with sp.Fori(0, 4) as i:
                for j in range(2):
                    load(S0["u"] + 2 * i + j, stream["u"][2 * i + j, :, :], j)
            for name in ("c", "uq", "ukv"):
                for j in range(len(dict(STREAM)[name])):
                    load(S0[name] + j, stream[name][j, :, :], (S0[name] + j) % 2)
            for name in ("out", "pq"):
                with sp.Fori(0, 8) as i:
                    for j in range(2):
                        load(S0[name] + 2 * i + j, stream[name][2 * i + j, :, :], j)
            n0 = S0["peer"]
            for j in range(2):
                load(n0 + j, stream["pu"][j, :, :], j)

            with sp.Fori(0, NTB // 2) as i:
                for b in range(2):
                    sp.wait_ge(gquad_copied, 8 * (2 * i + b + 1))
                    sp.dma_start(gates_dram[2 * i + b, :, :, :], gstage[b][:, :, :]).then_inc(gates_stored[b], 16)
            for b in range(2):
                sp.wait_ge(gates_stored[b], 16 * (NTB // 2))

            def load_gates(g, b):
                sp.dma_start(gtile[b][:, :, :, :],
                             gates_dram[:, :, bass.ts(g, GROUP), :].rearrange("b p i t -> p b i t")).then_inc(gates_loaded[b], 16)

            load_gates(0, 0)
            load_gates(1, 1)
            for j in range(2, GROUP):
                load(n0 + j, stream["pu"][j, :, :], j % 2)

            def load_group(g, b):
                for j in range(GROUP):
                    load(n0 + GROUP + 8 * (g - 1) + 2 * j, stream["pu"][GROUP * g + j, :, :], 0)
                    if j == 0 and not (isinstance(g, int) and g == 1):
                        sp.wait_ge(act_gated, GROUP * (g - 1))
                        load_gates(g, b)
                    load(n0 + GROUP + 8 * (g - 1) + 2 * j + 1, stream["pv"][GROUP * (g - 1) + j, :, :], 1)

            load_group(1, 1)
            with sp.Fori(0, (NGROUPS - 2) // 2) as i:
                for b in range(2):
                    load_group(2 * i + 2 + b, b)
            sp.wait_ge(act_gated, GROUP * (NGROUPS - 1))
            sp.dma_start(pRaw[:, :, :], a["p"]).then_inc(p_loaded, 16)
            for j in range(GROUP):
                load(n0 + GROUP + 8 * (NGROUPS - 1) + j, stream["pv"][GROUP * (NGROUPS - 1) + j, :, :], j % 2)
            for j in range(2):
                load(S0["proj"] + j, stream["proj"][j, :, :], j)
            with sp.Fori(0, 8) as i:
                for j in range(2):
                    load(S0["gate"] + 2 * i + j, stream["gate"][2 * i + j, :, :], j)
            for i in range(4):
                sp.wait_ge(out_ready, 4 * i + 4)
                sp.dma_start(out[:, 4 * i:4 * i + 4, :], hT[:, 4 * i:4 * i + 4, :]).then_inc(out_stored, 16)
            sp.wait_ge(out_stored, 64)

        @block.gpsimd
        def _(pool):
            for dst, src in ((gains[:, :], a["gains"]), (ident[:, :], a["consts"][:, 0:128]),
                             (iota[:, :], a["consts"][:, 128:256])):
                pool.dma_start(dst, src).then_inc(consts_loaded, 16)
            pool.dma_start(wsT[:, :, :], a["ws"]).then_inc(rows_loaded, 16)
            pool.dma_start(sgu_rows[:, :, :, :].rearrange("p a b c -> p (a b c)"),
                           a["rows"].partition_broadcast(P)).then_inc(rows_loaded, 16)
            nc.gpsimd.memset(ones[:, :], 1.0).then_inc(consts_ready, 1)
            nc.gpsimd.memset(ssum[:, 0:P], 0.0).then_inc(pool_step, 1)
            pool.wait_ge(pool_step, 1)
            nc.gpsimd.affine_select(out=ssum[:, 0:P], in_=ssum[:, 0:P], compare_op=ALU.is_ge, fill=-1e30,
                                    base=0, pattern=[[-1, P]], channel_multiplier=1).then_inc(causal_built, 1)
            pool.wait_ge(rows_loaded, 32)
            nc.gpsimd.affine_select(out=wsT[:, :, :], in_=wsT[:, :, :], compare_op=ALU.is_ge, fill=0.0,
                                    base=0, pattern=[[0, 8], [1, P]], channel_multiplier=-1).then_inc(consts_ready, 1)
            pool.wait_ge(act_lo, KD)
            pool.dma_start(perm[:, :], a["consts"][:, 256:384]).then_inc(perm_loaded, 16)
            pool.dma_start(freq[:, :], a["consts"][:, 384:386]).then_inc(perm_loaded, 16)
            pool.wait_ge(sgu_ready, 8)
            pool.dma_start(krT[:, :].bitcast(I32), a["pos"].partition_broadcast(P)).then_inc(pos_loaded, 16)
            pool.wait_ge(rope_ready, 5)
            for i in range(4):
                pool.dma_start(hT[:, 4 * i:4 * i + 4, :], a["x"][:, 4 * i:4 * i + 4, :]).then_inc(x_again, 16)
            pool.wait_ge(act_lo, N_SC["ffn"])
            pool.dma_start(keys[:, :, :, :], a["keys"]).then_inc(keys_loaded, 16)

        @block.scalar
        def _(act):
            A = nc.scalar.activation

            def hi(n, parity, used):
                act.wait_ge(raw_loaded[parity], (n - parity) * 8 + 16)
                if not (isinstance(used, int) and used <= 0):
                    act.wait_ge(tile_done, used)
                A(wH[parity][:, :], raw[parity][:, :], ACT.Copy).then_inc(hi_ready, 1)

            def square(name, k, src):
                n = N_SQ[name] + k
                if not (isinstance(n, int) and n < 2):
                    act.wait_ge(sq_added, n - 1)
                A(sq[k0(k) % 2][:, :], src, ACT.Square).then_inc(sq_ready, 1)

            def root(name):
                act.wait_ge(mean_ready, NORMS[name] + 1)
                dst = rstdB if name == "sgu" else rstd
                A(dst[:, :], dst[:, :], ACT.Sqrt).then_inc(root_ready, 1)

            def split_hi(name, order, dst):
                for j, k in enumerate(order):
                    act.wait_ge(act_scaled, N_SC[name] + j + 1)
                    A(dst[:, k, :], tmp[j % 2][:, :], ACT.Copy).then_inc(act_hi, 1)

            def k0(k):
                return k if isinstance(k, int) else 0

            act.wait_ge(consts_loaded, 48)
            A(identR[:, :], ident[:, :], ACT.Copy)
            act.wait_ge(causal_built, 1)
            A(causalR[:, :], ssum[:, 0:P], ACT.Copy).then_inc(consts_ready, 1)

            for k in range(KD):
                if k % 4 == 0:
                    act.wait_ge(x_loaded[k // 4], 16)
                square("mix", k, hT[:, k, :])
            hi(0, 0, 0)
            root("mix")
            split_hi("mix", range(KD), aH)

            for cb in range(2):
                for n in range(S0["v"] + 4 * cb, S0["v"] + 4 * cb + 4):
                    hi(n + 1, (n + 1) % 2, CUM[n - 1])
                for tt in range(NT):
                    act.wait_ge(tile_done, 7 * cb + 4 + tt)
                    A(vtok[:, tt, bass.ts(cb, 512)], ps[:, tt, :], ACT.Gelu_apprx_tanh).then_inc(v_gelu, 1)
            with act.Fori(0, 4) as i:
                for j in range(2):
                    n = S0["u"] + 2 * i + j
                    hi(n + 1, (j + 1) % 2, CUM[S0["u"] + j - 1] + 2 * i)
                    if j == 0:
                        act.wait_ge(ln_var, i + 1)
                        A(ln_rstd[:, :], ln_rstd[:, :], ACT.Sqrt).then_inc(ln_std, 1)
                    act.wait_ge(tile_done, CUM[S0["u"] + j] + 2 * i)
                    A(mixT[:, 8 + 2 * i + j, :], ps[:, 4 + j, :], ACT.Gelu_apprx_tanh).then_inc(u_gelu, 1)
            for j in range(7):
                n = S0["c"] + j
                hi(n + 1, (n + 1) % 2, CUM[n - 1])
                if j < 4:
                    act.wait_ge(c_copied, j + 1)
                    square("cq", j, cT[:, j, :])
                elif j < 6:
                    act.wait_ge(c_copied, j + 1)
                    square("ckv", j - 4, cT[:, j, :])
                if j == 4:
                    root("cq")
                    split_hi("cq", range(KQ), cqH)
            root("ckv")
            split_hi("ckv", range(KKV), ckvH)
            for g in range(SGU_TILES):
                act.wait_ge(sgu_ready, g + 1)
                square("sgu", g, mixT[:, 8 + g, :])
            root("sgu")
            act.wait_ge(angle_ready, 1)
            A(cosT[:, :], cosT[:, :], ACT.Sin).then_inc(trig_ready, 1)
            act.wait_ge(angle_ready, 2)
            A(sinT[:, :], sinT[:, :], ACT.Sin).then_inc(trig_ready, 1)
            for s in range(3):
                n = S0["uq"] + s
                hi(n + 1, (n + 1) % 2, CUM[n - 1])
                for m in range(4):
                    t = 4 * s + m
                    act.wait_ge(tile_done, CUM[n - 1] + m + 1)
                    A(qT[:, t, :], ps[:, 4 + t % 4, :], ACT.Copy).then_inc(uq_copied, 1)
            for s in range(2):
                n = S0["ukv"] + s
                hi(n + 1, (n + 1) % 2, CUM[n - 1])
                for m in range(8):
                    act.wait_ge(tile_done, CUM[n - 1] + m + 1)
                    dst = kT[:, m, :] if s == 0 else vA[:, m % 4, 512 * (m // 4):512 * (m // 4) + 512]
                    A(dst, ps[:, 4 + m % 4, :], ACT.Copy).then_inc(kv_copied, 1)
            ITEMS = HEADS * NT
            for n in range(ITEMS + 3):
                if n < ITEMS:
                    w = P * (n % NT + 1)
                    act.wait_ge(nbias_ready, n + 1)
                    if n >= 2:
                        act.wait_ge(pt_done, n - 1)
                    A(prob[n % 2][:, 0:w], ps[:, n % 3, 0:w], ACT.Exp, bias=nbias[:, n:n + 1], scale=SCALE,
                      accum_out=rsum[:, n:n + 1]).then_inc(exp_done, 1)
                m = n - 2
                if 0 <= m < ITEMS:
                    w = P * (m % NT + 1)
                    act.wait_ge(pt_done, m + 1)
                    if m >= 2:
                        act.wait_ge(pv_done, m - 1)
                    A(probT[m % 2][:, 0:w], ps[:, 3 + m % 2, 0:w], ACT.Copy).then_inc(pt_copied, 1)
                if n >= 5 and (n - 5) % NT == 3:
                    h = (n - 5) // NT
                    act.wait_ge(o_copied, h + 1)
                    square("attn", h, mixT[:, h, :])
            for h in range((ITEMS + 2 - 5 - 3) // NT + 1, HEADS):
                act.wait_ge(o_copied, h + 1)
                square("attn", h, mixT[:, h, :])
            root("attn")
            split_hi("out", OUT_ORDER, aH)
            with act.Fori(0, 8) as i:
                for j in range(2):
                    hi(S0["out"] + 2 * i + j + 1, (j + 1) % 2, CUM[S0["out"] + j - 1] + 2 * i)
                    act.wait_ge(h_mixed, 2 * i + j + 1)
                    act.wait_ge(sq_added, N_SQ["ffn"] - 1 + 2 * i + j)
                    A(sq[j][:, :], hT[:, 2 * i + j, :], ACT.Square).then_inc(sq_ready, 1)
            root("ffn")
            split_hi("ffn", range(KD), aH)
            def query_tiles(h, b, i, j0):
                for s in range(2):
                    j = j0 + s
                    hi(S0["pq"] + 2 * h + s + 1, (s + 1) % 2, CUM[S0["pq"] + j - 1] + 4 * i)
                    act.wait_ge(tile_done, CUM[S0["pq"] + j] + 4 * i)
                    A(pqT[b][:, s, :], ps[:, s, :], ACT.Copy).then_inc(pq_copied, 1)

            def gate_exps(h):
                act.wait_ge(gate_sub, h + 1)
                A(gate_e[:, :, :], gate_e[:, :, :], ACT.Exp).then_inc(gate_exp, 1)

            query_tiles(0, 0, 0, 0)
            with act.Fori(0, 3) as i:
                for b in range(2):
                    query_tiles(2 * i + b + 1, 1 - b, i, 2 + 2 * b)
                    gate_exps(2 * i + b)
            query_tiles(7, 1, 3, 2)
            gate_exps(6)
            gate_exps(7)
            for r in range(3):
                act.wait_ge(hkT_done, r + 1)
                A(hk[:, r, :], ps[:, r, :], ACT.Copy).then_inc(hk_ready, 1)

            def stage(u, q, b):
                act.wait_ge(gquad_done, u + 1)
                A(gstage[b][:, :, 4 * q:4 * q + 4].rearrange("p i t -> p t i"),
                  ps[:, 4 + q % 4, :].rearrange("p (t i) -> p t i", t=4), ACT.Copy).then_inc(gquad_copied, 1)

            for b in range(2):
                for q in range(8):
                    stage(8 * b + q, q, b)
            with act.Fori(1, NTB // 2) as i:
                for b in range(2):
                    act.wait_ge(gates_stored[b], 16 * i)
                    for q in range(8):
                        stage(16 * i + 8 * b + q, q, b)

            n0 = S0["peer"]

            def gelu(uc, j, tiles, first=False):
                act.wait_ge(tile_done, tiles)
                if not first:
                    act.wait_ge(act_wlo, uc - 1)
                A(tmp[j % 2][:, :], ps[:, j % 2, :], ACT.Gelu_apprx_tanh).then_inc(gelu_done, 1)

            def weight_hi(uc, j, b):
                act.wait_ge(act_gated, uc + 1)
                A(actH[b][:, j, :], tmp[j % 2][:, :], ACT.Copy).then_inc(act_whi, 1)

            for j in range(GROUP):
                hi(n0 + j + 1, (j + 1) % 2, CUM[n0 + j - 1])
                gelu(j, j, CUM[n0 + j], first=j < 2)
                weight_hi(j, j, 0)

            def group(g, b, i=0):
                first = n0 + GROUP + 8 * (g - 1)
                for j in range(GROUP):
                    m = GROUP + 2 * j + 8 * b
                    hi(first + 2 * j + 1, 1, CUM[n0 + m - 1] + 40 * i)
                    gelu(GROUP * g + j, j, CUM[n0 + m] + 40 * i)
                    hi(first + 2 * j + 2, 0, CUM[n0 + m] + 40 * i)
                    weight_hi(GROUP * g + j, j, (b + 1) % 2)

            with act.Fori(0, (NGROUPS - 2) // 2) as i:
                for b in range(2):
                    group(2 * i + 1 + b, b, i)
            group(NGROUPS - 1, 0, (NGROUPS - 2) // 2)
            last = n0 + GROUP + 8 * (NGROUPS - 1)
            for j in range(GROUP):
                hi(last + j + 1, (j + 1) % 2, CUM[last + j - 1])
                if j == 0:
                    act.wait_ge(p_loaded, 16)
                    A(pH[:, :, :], pRaw[:, :, :], ACT.Copy).then_inc(p_hi, 1)
                for m in range(4):
                    act.wait_ge(h_acc, 16 * (NGROUPS - 1) + 4 * j + m + 1)
                    square("ple", 4 * j + m, hT[:, 4 * j + m, :])
            for s in range(2):
                n = S0["proj"] + s
                if s == 1:
                    root("ple")
                    split_hi("ple", range(KD), aH)
                hi(n + 1, (n + 1) % 2, CUM[n - 1])
                for m in range(8):
                    act.wait_ge(tile_done, CUM[n - 1] + m + 1)
                    A(projT[:, 8 * s + m, :], ps[:, 2 + m % 4, :], ACT.Copy).then_inc(proj_copied, 1)

            def gate_tile(i, j, last=False):
                if not last:
                    hi(S0["gate"] + 2 * i + j + 1, (j + 1) % 2, CUM[S0["gate"] + j - 1] + 2 * i)
                act.wait_ge(tile_done, CUM[S0["gate"] + j] + 2 * i)
                if not (isinstance(i, int) and i == 0):
                    act.wait_ge(h_gated, 2 * i + j - 1)
                A(tmp[j][:, :], ps[:, j, :], ACT.Sigmoid).then_inc(sig_done, 1)
                act.wait_ge(h_gated, 2 * i + j + 1)
                act.wait_ge(sq_added, N_SQ["final"] - 1 + 2 * i + j)
                A(sq[j][:, :], hT[:, 2 * i + j, :], ACT.Square).then_inc(sq_ready, 1)

            for j in range(2):
                gate_tile(0, j)
            with act.Fori(1, 7) as i:
                for j in range(2):
                    gate_tile(i, j)
            for j in range(2):
                gate_tile(7, j, last=j == 1)
            root("final")

        @block.vector
        def _(dve):
            V = nc.vector
            st = Steps(dve, dve_step)

            def hold():
                V.tensor_copy(held[:, :], ones[:, 0:1])

            def lo(n, parity):
                dve.wait_ge(hi_ready, n + 1)
                V.tensor_tensor(wL[parity][:, :], raw[parity][:, :], wH[parity][:, :].bitcast(F), ALU.subtract).then_inc(lo_ready, 1)

            def add_square(name, k, first=False, par=None):
                n = N_SQ[name] + k
                dve.wait_ge(sq_ready, n + 1)
                s = sq[k % 2 if par is None else par]
                if first:
                    if not (isinstance(n, int) and n == 0):
                        dve.wait_ge(sum_done, NORMS[name])
                    V.tensor_copy(ssum[:, :], s[:, :]).then_inc(sq_added, 1)
                else:
                    dve.wait_ge(sq_added, n)
                    V.tensor_tensor(ssum[:, :], ssum[:, :], s[:, :], ALU.add).then_inc(sq_added, 1)

            def inverse_root(name, width, bank):
                dst = rstdB if name == "sgu" else rstd
                dve.wait_ge(sum_done, NORMS[name] + 1)
                V.tensor_scalar(dst[:, :], ps[:, bank, :], 1.0 / width, EPS, ALU.mult, ALU.add).then_inc(mean_ready, 1)
                dve.wait_ge(root_ready, NORMS[name] + 1)
                V.reciprocal(dst[:, :], dst[:, :]).then_inc(rstd_ready, 1)
                dve.wait_ge(rstd_ready, NORMS[name] + 1)

            def scale_split(name, tiles, hi_dst, lo_dst):
                def low(j):
                    dve.wait_ge(act_hi, N_SC[name] + j + 1)
                    k = tiles[j][0]
                    V.tensor_tensor(lo_dst[:, k, :], tmp[j % 2][:, :], hi_dst[:, k, :].bitcast(F), ALU.subtract).then_inc(act_lo, 1)

                for j, (k, src, g, r) in enumerate(tiles):
                    if j >= 2:
                        dve.wait_ge(act_lo, N_SC[name] + j - 1)
                    V.scalar_tensor_tensor(tmp[j % 2][:, :], src, g, r[:, :], ALU.mult, ALU.mult).then_inc(act_scaled, 1)
                    if j >= 1:
                        low(j - 1)
                low(len(tiles) - 1)

            dve.wait_ge(consts_ready, 3)
            for k in range(KD):
                add_square("mix", k, first=k == 0)
            lo(0, 0)
            inverse_root("mix", D, 7)
            scale_split("mix", [(k, hT[:, k, :], gain("mix", k), rstd) for k in range(KD)], aH, aL)

            with dve.Fori(0, 2) as cb:
                for j in range(4):
                    lo(S0["v"] + 4 * cb + j + 1, (j + 1) % 2)
            dve.wait_ge(v_gelu, 8)
            with st.loop(4, 8 + 8 + 1 + 8 + 1) as i:
                lo(S0["u"] + 2 * i + 1, 1)
                for g in range(8):
                    st.did(V.bn_stats(ln_stats[:, g, :], vtok[:, i, g * P:(g + 1) * P]))
                st.settle()
                hold()
                for g in range(8):
                    st.did(V.bn_aggr(ln_mv[:, g, :], ln_stats[:, g, :]))
                st.settle()
                V.tensor_scalar_add(ln_rstd[:, :], ln_mv[:, :, 1], EPS).then_inc(ln_var, 1)
                dve.wait_ge(ln_std, i + 1)
                st.did(V.reciprocal(ln_rstd[:, :], ln_rstd[:, :]))
                st.settle()
                for g in range(8):
                    v = vtok[:, i, g * P:(g + 1) * P]
                    st.did(V.tensor_scalar(v, v, ln_mv[:, g, 0:1], ln_rstd[:, g:g + 1], ALU.subtract, ALU.mult))
                st.settle()
                lo(S0["u"] + 2 * i + 2, 0)
                v = vtok[:, i, :]
                st.did(V.tensor_tensor(v, v, sgu_rows[:, 1, :, :].rearrange("p a b -> p (a b)"), ALU.mult))
                st.settle()
                V.tensor_tensor(v, v, sgu_rows[:, 2, :, :].rearrange("p a b -> p (a b)"), ALU.add).then_inc(v_ready, 1)
            for j in range(7):
                n = S0["c"] + j
                lo(n + 1, (n + 1) % 2)
                dve.wait_ge(tile_done, CUM[n])
                V.tensor_copy(cT[:, j, :], ps[:, 6 + j % 2, :]).then_inc(c_copied, 1)
                if j < 4:
                    add_square("cq", j, first=j == 0)
                elif j < 6:
                    add_square("ckv", j - 4, first=j == 4)
                if j == 4:
                    inverse_root("cq", QL, 0)
                    dve.wait_ge(c_copied, 4)
                    scale_split("cq", [(k, cT[:, k, :], gain("cq", k), rstd) for k in range(KQ)], cqH, cqL)
            inverse_root("ckv", KVL, 0)
            scale_split("ckv", [(k, cT[:, KQ + k, :], gain("ckv", k), rstd) for k in range(KKV)], ckvH, ckvL)
            for g in range(SGU_TILES):
                dve.wait_ge(mix_done, g + 1)
                if g < 2:
                    dve.wait_ge(act_lo, N_SC["out"])
                else:
                    dve.wait_ge(sgu_ready, g - 1)
                st.did(V.tensor_tensor(tmp[g % 2][:, :].rearrange("p (c t) -> p c t", c=NT),
                                       ps[:, 2 + g % 2, :].rearrange("p (c t) -> p c t", c=NT),
                                       sgu_rows[:, 0, g, :].unsqueeze(1).to_broadcast([P, NT, P]), ALU.add))
                st.settle()
                if g == 0:
                    dve.wait_ge(u_gelu, 8)
                V.tensor_tensor(mixT[:, 8 + g, :], mixT[:, 8 + g, :], tmp[g % 2][:, :], ALU.mult).then_inc(sgu_ready, 1)
                if g >= 1:
                    add_square("sgu", g - 1, first=g == 1)
            add_square("sgu", 7)
            inverse_root("sgu", 1024, 0)
            dve.wait_ge(pos_loaded, 16)
            dve.wait_ge(perm_loaded, 32)
            dve.wait_ge(sgu_ready, 8)
            st.did(V.tensor_copy(tmp[0][:, :], krT[:, :].bitcast(I32)))
            st.settle()
            st.did(V.tensor_scalar(tmp[0][:, :], tmp[0][:, :], freq[:, 0:1], None, ALU.mult))
            st.settle()
            for dst, quarter in ((cosT, 0.25), (sinT, 0.0)):
                st.did(V.tensor_scalar(tmp[1][:, :], tmp[0][:, :], 1.0 / (2 * PI), quarter, ALU.mult, ALU.add))
                st.settle()
                st.did(V.tensor_scalar(tmp[1][:, :], tmp[1][:, :], ROUND, None, ALU.add))
                st.settle()
                st.did(V.tensor_scalar(tmp[1][:, :], tmp[1][:, :], ROUND, None, ALU.subtract))
                st.settle()
                src = tmp[0]
                for part in two_pi_parts():
                    st.did(V.scalar_tensor_tensor(dst[:, :], tmp[1][:, :], -part, src[:, :], ALU.mult, ALU.add))
                    st.settle()
                    src = dst
                st.did(V.tensor_scalar(dst[:, :], dst[:, :], quarter * 2 * PI, PI_BELOW, ALU.add, ALU.min))
                st.settle()
                V.tensor_scalar(dst[:, :], dst[:, :], -PI_BELOW, None, ALU.max).then_inc(angle_ready, 1)

            def rope(j, src, dst):
                st.did(V.tensor_tensor(tmp[0][:, :], src, cosT[:, :], ALU.mult))
                dve.wait_ge(swap_done, j + 1)
                st.did(V.tensor_tensor(tmp[1][:, :], ps[:, j % 2, :], sinT[:, :], ALU.mult))
                st.settle()
                V.tensor_tensor(dst, tmp[0][:, :], tmp[1][:, :], ALU.add).then_inc(rope_ready, 1)

            dve.wait_ge(trig_ready, 2)
            for s in range(3):
                lo(S0["uq"] + s + 1, (S0["uq"] + s + 1) % 2)
                if s == 0:
                    rope(0, cT[:, 6, :], krT[:, :])
            lo(S0["ukv"] + 1, (S0["ukv"] + 1) % 2)
            for j in range(4):
                dve.wait_ge(uq_copied, 9 + j)
                dve.wait_ge(rope_ready, 1 + j)
                rope(1 + j, qT[:, 8 + j, :], qT[:, 8 + j, :])
            lo(S0["out"], 0)
            ITEMS = HEADS * NT
            for n in range(ITEMS + 1):
                if n < ITEMS:
                    w = P * (n % NT + 1)
                    dve.wait_ge(score_done, n + 1)
                    st.did(V.reduce_max(smax[:, n:n + 1], ps[:, n % 3, 0:w], AX))
                    st.settle()
                    V.tensor_scalar(nbias[:, n:n + 1], smax[:, n:n + 1], -SCALE, None, ALU.mult).then_inc(nbias_ready, 1)
                if n >= 1:
                    m = n - 1
                    w = P * (m % NT + 1)
                    dve.wait_ge(exp_done, m + 1)
                    st.did(V.reciprocal(rinv[:, m:m + 1], rsum[:, m:m + 1]))
                    st.settle()
                    V.tensor_scalar(prob[m % 2][:, 0:w], prob[m % 2][:, 0:w], rinv[:, m:m + 1], None, ALU.mult).then_inc(p_ready, 1)
                if n >= NT + 4 and n % NT == 0 or n == ITEMS:
                    for h in ([n // NT - 2] if n < ITEMS else [HEADS - 2, HEADS - 1]):
                        dve.wait_ge(pv_done, NT * (h + 1))
                        V.tensor_copy(mixT[:, h, :], ps[:, 5 + h % 2, :]).then_inc(o_copied, 1)
                        if h >= 1:
                            add_square("attn", h - 1, first=h == 1)
            add_square("attn", HEADS - 1)
            parts = [(k, mixT[:, k, :], gain("sgu", k - 8), rstdB) for k in OUT_ORDER[:8]]
            parts += [(k, mixT[:, k, :], gain("attn", k), rstd) for k in OUT_ORDER[8:]]
            inverse_root("attn", 1024, 7)
            scale_split("out", parts, aH, aL)
            dve.wait_ge(x_again, 64)

            def residual(i, j):
                lo(S0["out"] + 2 * i + j + 1, (j + 1) % 2)
                dve.wait_ge(tile_done, CUM[S0["out"] + j] + 2 * i)
                V.tensor_tensor(hT[:, 2 * i + j, :], hT[:, 2 * i + j, :], ps[:, j, :], ALU.add).then_inc(h_mixed, 1)

            residual(0, 0)
            add_square("ffn", 0, first=True)
            residual(0, 1)
            add_square("ffn", 1)
            with dve.Fori(1, 8) as i:
                for j in range(2):
                    residual(i, j)
                    add_square("ffn", 2 * i + j, par=j)
            inverse_root("ffn", D, 7)
            scale_split("ffn", [(k, hT[:, k, :], gain("ffn", k), rstd) for k in range(KD)], aH, aL)

            def best_keys(h, b):
                def unit(s, t):
                    return ps[:, 2 + 2 * b + s, t * P:(t + 1) * P]

                units = [(s, t) for s in range(2) for t in range(NT)]
                dve.wait_ge(ps_done, 2 * h + 2)
                hold()
                for s, t in units:
                    st.did(V.max(top[:, s, t, 0:8], unit(s, t)))
                st.settle()
                hold()
                for s, t in units:
                    st.did(V.match_replace(rest[:, s * NT + t, :], top[:, s, t, 0:8], unit(s, t), -3e38))
                st.settle()
                hold()
                for s, t in units:
                    st.did(V.max(top[:, s, t, 8:16], rest[:, s * NT + t, :]))
                for s, t in units:
                    st.did(V.max_index(top_at[:, s, t, 0:8], top[:, s, t, 0:8], unit(s, t)))
                st.settle()
                hold()
                for s, t in units[:-1]:
                    st.did(V.max_index(top_at[:, s, t, 8:16], top[:, s, t, 8:16], rest[:, s * NT + t, :]))
                s, t = units[-1]
                V.max_index(top_at[:, s, t, 8:16], top[:, s, t, 8:16], rest[:, s * NT + t, :]).then_inc(tops_done, 1)

            def best_pairs(h):
                for t in range(NT):
                    st.did(V.tensor_tensor(cand[:, t, :].rearrange("p (a b) -> p a b", a=TOPK),
                                           top[:, 0, t, :].unsqueeze(2).to_broadcast([P, TOPK, TOPK]),
                                           top[:, 1, t, :].unsqueeze(1).to_broadcast([P, TOPK, TOPK]), ALU.add))
                dve.wait_ge(tops_done, h + 1)
                st.did(V.tensor_copy(top_atf[:, :, :, :], top_at[:, :, :, :]))
                st.settle()
                hold()
                for t in range(NT):
                    st.did(V.max(best[:, t, 0:8], cand[:, t, :]))
                st.settle()
                hold()
                for t in range(NT):
                    st.did(V.match_replace(cand_rest[:, t, :], best[:, t, 0:8], cand[:, t, :], -3e38))
                st.settle()
                hold()
                for t in range(NT):
                    st.did(V.max(best[:, t, 8:16], cand_rest[:, t, :]))
                for t in range(NT):
                    st.did(V.max_index(best_at[:, t, 0:8], best[:, t, 0:8], cand[:, t, :]))
                st.settle()
                hold()
                for t in range(NT):
                    st.did(V.max_index(best_at[:, t, 8:16], best[:, t, 8:16], cand_rest[:, t, :]))
                V.tensor_tensor(gate_e[:, :, :], best[:, :, :], best[:, :, 0:1].to_broadcast([P, NT, TOPK]),
                                ALU.subtract).then_inc(gate_sub, 1)
                st.settle()
                st.did(V.tensor_single_scalar(best_k[:, 0, :, :], best_at[:, :, :], 4, ALU.logical_shift_right))
                st.did(V.tensor_single_scalar(best_k[:, 1, :, :], best_at[:, :, :], 15, ALU.bitwise_and))
                st.settle()
                st.did(V.tensor_copy(best_kf[:, :, :, :], best_k[:, :, :, :]))
                st.settle()
                for s in range(2):
                    m3 = match[:, :, :, :].rearrange("p t a b -> p (t a) b")
                    st.did(V.tensor_tensor(m3, iota[:, 0:TOPK].unsqueeze(1).to_broadcast([P, NT * TOPK, TOPK]),
                                           best_kf[:, s, :, :].rearrange("p t k -> p (t k)").unsqueeze(2)
                                           .to_broadcast([P, NT * TOPK, TOPK]), ALU.is_equal))
                    st.settle()
                    st.did(V.tensor_tensor(match[:, :, :, :], match[:, :, :, :],
                                           top_atf[:, s, :, :].unsqueeze(2).to_broadcast([P, NT, TOPK, TOPK]), ALU.mult))
                    st.settle()
                    st.did(V.tensor_reduce(route[:, 1 + s, :, bass.ts(h, TOPK)], match[:, :, :, :], AX, ALU.add))
                    st.settle()
                dve.wait_ge(gate_exp, h + 1)
                st.did(V.reduce_sum(gate_sum[:, :], gate_e[:, :, :], AX))
                st.settle()
                st.did(V.reciprocal(gate_inv[:, :], gate_sum[:, :]))
                st.settle()
                V.tensor_tensor(route[:, 0, :, bass.ts(h, TOPK)], gate_e[:, :, :],
                                gate_inv[:, :].unsqueeze(2).to_broadcast([P, NT, TOPK]), ALU.mult).then_inc(routed, 1)
                dve.wait_ge(routed, h + 1)

            KEY_STEPS, PAIR_STEPS = 39, 36
            lo(S0["pq"] + 1, 1)
            lo(S0["pq"] + 2, 0)
            with st.loop(3, 2 * (KEY_STEPS + PAIR_STEPS)) as i:
                for b in range(2):
                    h = 2 * i + b
                    lo(S0["pq"] + 2 * h + 3, 1)
                    best_keys(h, b)
                    lo(S0["pq"] + 2 * h + 4, 0)
                    best_pairs(h)
            lo(S0["pq"] + 15, 1)
            best_keys(6, 0)
            lo(S0["pq"] + 16, 0)
            best_pairs(6)
            best_keys(7, 1)
            best_pairs(7)

            dve.wait_ge(hk_ready, 3)

            def gate_rows(u, b):
                V.tensor_tensor(oh1[:, b, :, :], iota[:, :].unsqueeze(1).to_broadcast([P, 4, P]),
                                hk[:, 1, bass.ts(u, 4)].unsqueeze(2).to_broadcast([P, 4, P]), ALU.is_equal)
                for t in range(4):
                    ins = V.tensor_scalar(oh2[:, b, t, :], iota[:, :], hk[:, 2, bass.ds(4 * u + t, 1)],
                                          hk[:, 0, bass.ds(4 * u + t, 1)], ALU.is_equal, ALU.mult)
                ins.then_inc(onehot_ready, 1)

            for b in range(2):
                gate_rows(b, b)
            with dve.Fori(1, QUADS // 2) as i:
                for b in range(2):
                    dve.wait_ge(gquad_done, 2 * i + b - 1)
                    gate_rows(2 * i + b, b)

            n0 = S0["peer"]

            def apply_gates(uc, j, b):
                dve.wait_ge(gelu_done, uc + 1)
                g = gtile[b][:, :, j, :]
                t3 = tmp[j % 2][:, :].rearrange("p (b t) -> p b t", b=NTB)
                V.tensor_tensor(t3, t3, g, ALU.mult).then_inc(act_gated, 1)

            def weight_lo(uc, j, b):
                dve.wait_ge(act_whi, uc + 1)
                V.tensor_tensor(actL[b][:, j, :], tmp[j % 2][:, :], actH[b][:, j, :].bitcast(F), ALU.subtract).then_inc(act_wlo, 1)

            def accumulate(q, tiles, done):
                for m in range(4):
                    dve.wait_ge(tile_done, tiles + m + 1)
                    if not (isinstance(done, int) and done <= 0):
                        if m == 0 and q == 0:
                            dve.wait_ge(h_acc, done)
                    h = hT[:, 4 * q + m, :]
                    V.tensor_tensor(h, h, ps[:, 2 + m, :], ALU.add).then_inc(h_acc, 1)

            for j in range(GROUP):
                lo(n0 + j + 1, (j + 1) % 2)
                if j == 0:
                    dve.wait_ge(gates_loaded[0], 16)
                apply_gates(j, j, 0)
                weight_lo(j, j, 0)

            def group(g, b, i=0):
                first = n0 + GROUP + 8 * (g - 1)
                gb = (b + 1) % 2
                for j in range(GROUP):
                    m = GROUP + 2 * j + 8 * b
                    lo(first + 2 * j + 1, 1)
                    if j == 0:
                        dve.wait_ge(gates_loaded[gb], 8 * (g - gb) + 16)
                    apply_gates(GROUP * g + j, j, gb)
                    lo(first + 2 * j + 2, 0)
                    weight_lo(GROUP * g + j, j, gb)
                    done = 16 * (g - 1)
                    accumulate(j, CUM[n0 + m] + 40 * i, done)

            group(1, 0)
            with dve.Fori(0, (NGROUPS - 2) // 2) as i:
                for b in range(2):
                    g = 2 * i + 2 + b
                    first = n0 + GROUP + 8 * (g - 1)
                    for j in range(GROUP):
                        m = GROUP + 2 * j + 8 * (b + 1)
                        lo(first + 2 * j + 1, 1)
                        if j == 0:
                            dve.wait_ge(gates_loaded[b], 8 * (g - b) + 16)
                        apply_gates(GROUP * g + j, j, b)
                        lo(first + 2 * j + 2, 0)
                        weight_lo(GROUP * g + j, j, b)
                        accumulate(j, CUM[n0 + m] + 40 * i, 16 * (g - 1))
            last = n0 + GROUP + 8 * (NGROUPS - 1)
            for j in range(GROUP):
                lo(last + j + 1, (j + 1) % 2)
                if j == 0:
                    dve.wait_ge(p_hi, 1)
                    V.tensor_tensor(pL[:, :, :], pRaw[:, :, :], pH[:, :, :].bitcast(F), ALU.subtract).then_inc(p_lo, 1)
                accumulate(j, CUM[last + j - 1], 16 * (NGROUPS - 1))
                for m in range(4):
                    add_square("ple", 4 * j + m, first=j + m == 0)
            lo(S0["proj"] + 1, 1)
            inverse_root("ple", D, 7)
            scale_split("ple", [(k, hT[:, k, :], gain("ple", k), rstd) for k in range(KD)], aH, aL)
            lo(S0["gate"], 0)
            dve.wait_ge(proj_copied, 16)

            def gated(i, j, last=False, first=False):
                if not last:
                    lo(S0["gate"] + 2 * i + j + 1, (j + 1) % 2)
                m = 2 * i + j
                dve.wait_ge(sig_done, m + 1)
                st.did(V.tensor_tensor(tmp[j][:, :], tmp[j][:, :], projT[:, m, :], ALU.mult))
                st.settle()
                V.tensor_tensor(hT[:, m, :], hT[:, m, :], tmp[j][:, :], ALU.add).then_inc(h_gated, 1)
                add_square("final", m, first=first, par=j)

            for j in range(2):
                gated(0, j, first=j == 0)
            with st.loop(6, 2) as i:
                for j in range(2):
                    gated(i + 1, j)
            for j in range(2):
                gated(7, j, last=j == 1)
            inverse_root("final", D, 7)
            for k in range(KD):
                V.scalar_tensor_tensor(hT[:, k, :], hT[:, k, :], gain("final", k), rstd[:, :], ALU.mult, ALU.mult).then_inc(out_ready, 1)

        @block.tensor
        def _(pe):
            mm = nc.tensor.matmul

            def three(out, wh, wl, xh, xl, start, stop):
                mm(out, wh, xh, start=start, stop=False)
                mm(out, wh, xl, start=False, stop=False)
                return mm(out, wl, xh, start=False, stop=stop)

            def norm_sum(name, bank):
                pe.wait_ge(sq_added, N_SQ[name] + {"cq": 4, "ckv": 2, "sgu": 8, "attn": 8}.get(name, 16))
                mm(ps[:, bank, :], ones[:, :], ssum[:, :], start=True, stop=True).then_inc(sum_done, 1)

            def tile(n, parity, bank, order=range(KD), waits=None):
                pe.wait_ge(lo_ready, n + 1)
                for j, k in enumerate(order):
                    if waits is not None:
                        pe.wait_ge(act_lo, waits + j + 1)
                    w = slice(k * P, (k + 1) * P)
                    ins = three(ps[:, bank, :], wH[parity][:, w], wL[parity][:, w], aH[:, k, :], aL[:, k, :],
                                j == 0, j == KD - 1)
                ins.then_inc(tile_done, 1)

            pe.wait_ge(consts_ready, 3)
            norm_sum("mix", 7)

            def v_block(cb, waits=None):
                for s in range(4):
                    pe.wait_ge(lo_ready, S0["v"] + 4 * cb + s + 1)
                    for tt in range(NT):
                        if s == 0 and waits is None:
                            pe.wait_ge(v_gelu, tt + 1)
                        for k4 in range(4):
                            k = 4 * s + k4
                            if waits is not None and tt == 0:
                                pe.wait_ge(act_lo, waits + k + 1)
                            w = slice(k4 * 512, (k4 + 1) * 512)
                            t = slice(tt * P, (tt + 1) * P)
                            ins = three(ps[:, tt, :], aH[:, k, t], aL[:, k, t], wH[s % 2][:, w], wL[s % 2][:, w], k == 0, k == KD - 1)
                        if s == 3 or tt == NT - 1:
                            ins.then_inc(tile_done, 1)

            v_block(0, waits=0)
            v_block(1)
            for j in range(2):
                tile(S0["u"] + j, j, 4 + j)
            with pe.Fori(1, 4) as i:
                for j in range(2):
                    pe.wait_ge(u_gelu, 2 * i + j - 1)
                    tile(S0["u"] + 2 * i + j, j, 4 + j)
            for j in range(7):
                n = S0["c"] + j
                if j >= 2:
                    pe.wait_ge(c_copied, j - 1)
                tile(n, n % 2, 6 + j % 2)
                if j == 4:
                    pe.wait_ge(v_gelu, 8)
                    norm_sum("cq", 0)
            pe.wait_ge(mean_ready, NORMS["cq"] + 1)
            norm_sum("ckv", 0)
            pe.wait_ge(v_ready, 4)
            for g in range(SGU_TILES):
                if g >= 2:
                    pe.wait_ge(sgu_ready, g - 1)
                for c in range(NT):
                    t = slice(c * P, (c + 1) * P)
                    ins = mm(ps[:, 2 + g % 2, t], vtok[:, c, g * P:(g + 1) * P], wsT[:, g, :], start=True, stop=True)
                ins.then_inc(mix_done, 1)
            pe.wait_ge(mean_ready, NORMS["ckv"] + 1)
            norm_sum("sgu", 0)
            pe.wait_ge(act_lo, N_SC["cq"] + KQ)
            pe.wait_ge(u_gelu, 8)
            for s in range(3):
                n = S0["uq"] + s
                pe.wait_ge(lo_ready, n + 1)
                for m in range(4):
                    t = 4 * s + m
                    if t >= 4:
                        pe.wait_ge(uq_copied, t - 3)
                    elif t in (2, 3):
                        pe.wait_ge(c_copied, 7)
                    for k in range(KQ):
                        w = slice(k * 512 + m * P, k * 512 + (m + 1) * P)
                        ins = three(ps[:, 4 + t % 4, :], wH[n % 2][:, w], wL[n % 2][:, w], cqH[:, k, :], cqL[:, k, :], k == 0, k == KQ - 1)
                    ins.then_inc(tile_done, 1)
                if s == 1:
                    pe.wait_ge(mean_ready, NORMS["sgu"] + 1)
                    pe.wait_ge(perm_loaded, 32)
                    mm(ps[:, 0, :], perm[:, :], cT[:, 6, :], start=True, stop=True).then_inc(swap_done, 1)
            for s in range(2):
                n = S0["ukv"] + s
                pe.wait_ge(lo_ready, n + 1)
                if s == 0:
                    pe.wait_ge(act_lo, N_SC["ckv"] + KKV)
                for m in range(8):
                    if m < 4 and s == 0:
                        pe.wait_ge(uq_copied, 9 + m)
                    else:
                        pe.wait_ge(kv_copied, 8 * s + m - 3)
                    for k in range(KKV):
                        if s == 0:
                            w = slice(k * 1024 + m * P, k * 1024 + (m + 1) * P)
                            ins = three(ps[:, 4 + m % 4, :], wH[n % 2][:, w], wL[n % 2][:, w], ckvH[:, k, :], ckvL[:, k, :], k == 0, k == 1)
                        else:
                            w = slice(k * 1024 + (m // 4) * 512, k * 1024 + (m // 4) * 512 + 512)
                            t = slice((m % 4) * P, (m % 4 + 1) * P)
                            ins = three(ps[:, 4 + m % 4, :], ckvH[:, k, t], ckvL[:, k, t], wH[n % 2][:, w], wL[n % 2][:, w], k == 0, k == 1)
                    ins.then_inc(tile_done, 1)
                    if s == 0 and m in (1, 3, 5, 7):
                        j = m // 2
                        pe.wait_ge(uq_copied, 9 + j)
                        if j >= 1:
                            pe.wait_ge(rope_ready, j)
                        mm(ps[:, (1 + j) % 2, :], perm[:, :], qT[:, 8 + j, :], start=True, stop=True).then_inc(swap_done, 1)
            pe.wait_ge(kv_copied, 16)
            pe.wait_ge(rope_ready, 5)
            ITEMS = HEADS * NT
            for n in range(ITEMS + 3):
                if n < ITEMS:
                    h, qt = divmod(n, NT)
                    w = P * (qt + 1)
                    t = slice(qt * P, w)
                    if n >= 3:
                        pe.wait_ge(exp_done, n - 2)
                    r = slice(64 * (h % 2), 64 * (h % 2) + 64)
                    o = ps[:, n % 3, 0:w]
                    mm(o, qT[:, h, t], kT[:, h, 0:w], start=True, stop=False)
                    mm(o, qT[r, 8 + h // 2, t], krT[r, 0:w], start=False, stop=False)
                    mm(ps[:, n % 3, t], identR[:, :], causalR[:, :], start=False, stop=True).then_inc(score_done, 1)
                m = n - 2
                if 0 <= m < ITEMS:
                    pe.wait_ge(p_ready, m + 1)
                    if m >= 2:
                        pe.wait_ge(pt_copied, m - 1)
                    elif m == 0:
                        pe.wait_ge(kv_copied, 16)
                    for j in range(m % NT + 1):
                        s = slice(j * P, (j + 1) * P)
                        ins = nc.tensor.transpose(ps[:, 3 + m % 2, s], prob[m % 2][:, s], ident[:, :])
                    ins.then_inc(pt_done, 1)
                m = n - 3
                if 0 <= m < ITEMS:
                    h, qt = divmod(m, NT)
                    pe.wait_ge(pt_copied, m + 1)
                    if qt == 0 and h >= 2:
                        pe.wait_ge(o_copied, h - 1)
                    for j in range(qt + 1):
                        s = slice(j * P, (j + 1) * P)
                        ins = mm(ps[:, 5 + h % 2, qt * P:(qt + 1) * P], vA[:, j, h * P:(h + 1) * P], probT[m % 2][:, s],
                                 start=j == 0, stop=j == qt)
                    ins.then_inc(pv_done, 1)
            norm_sum("attn", 7)
            tile(S0["out"], 0, 0, order=OUT_ORDER, waits=N_SC["out"])
            tile(S0["out"] + 1, 1, 1)
            with pe.Fori(1, 8) as i:
                for j in range(2):
                    pe.wait_ge(h_mixed, 2 * i + j - 1)
                    tile(S0["out"] + 2 * i + j, j, j)
            norm_sum("ffn", 7)

            def scores(h, b):
                for s in range(2):
                    pe.wait_ge(pq_copied, 2 * h + s + 1)
                    for t in range(NT):
                        ts = slice(t * P, (t + 1) * P)
                        ins = mm(ps[:, 2 + 2 * b + s, ts], pqT[b][:, s, ts], keys[:, h, s, :], start=True, stop=True)
                    ins.then_inc(ps_done, 1)

            def peer_queries(i, waits=None):
                for b in range(2):
                    for s in range(2):
                        j = 2 * b + s
                        if waits is None or j >= 2:
                            pe.wait_ge(pq_copied, 4 * i + j - 1)
                        tile(S0["pq"] + 4 * i + j, s, s, waits=waits if j == 0 else None)
                    if waits is None:
                        pe.wait_ge(tops_done, 2 * i + b - 1)
                    elif b == 0:
                        pe.wait_ge(keys_loaded, 16)
                    scores(2 * i + b, b)

            pe.wait_ge(h_mixed, 16)
            peer_queries(0, waits=N_SC["ffn"])
            with pe.Fori(1, 4) as i:
                peer_queries(i)
            pe.wait_ge(routed, HEADS)
            for r in range(3):
                for t in range(NT):
                    ins = nc.tensor.transpose(ps[:, r, t * P:(t + 1) * P], route[:, r, t, :], ident[:, :])
                ins.then_inc(hkT_done, 1)

            def quad(u, x):
                pe.wait_ge(onehot_ready, u + 1)
                for t in range(4):
                    ins = mm(ps[:, 4 + x, t * P:(t + 1) * P], oh1[:, x % 2, t, :], oh2[:, x % 2, t, :], start=True, stop=True)
                ins.then_inc(gquad_done, 1)

            for x in range(4):
                quad(x, x)
            with pe.Fori(1, QUADS // 4) as i:
                for x in range(4):
                    pe.wait_ge(gquad_copied, 4 * i + x - 3)
                    quad(4 * i + x, x)
            n0 = S0["peer"]

            def u_slot(n, parity, uc, j, first=False):
                if not first:
                    pe.wait_ge(gelu_done, uc - 1)
                tile(n, parity, j % 2)

            def v_slot(n, parity, g, q, b, first=False):
                pe.wait_ge(lo_ready, n + 1)
                if q == 0:
                    pe.wait_ge(act_wlo, GROUP * (g + 1))
                for m in range(4):
                    if not (first and q == 0):
                        pe.wait_ge(h_acc, 16 * g + 4 * q + m - 3)
                    for c in range(GROUP):
                        w = slice(c * 512 + m * P, c * 512 + (m + 1) * P)
                        ins = three(ps[:, 2 + m, :], wH[parity][:, w], wL[parity][:, w], actH[b][:, c, :], actL[b][:, c, :], c == 0, c == GROUP - 1)
                    ins.then_inc(tile_done, 1)

            pe.wait_ge(gquad_copied, QUADS)
            pe.wait_ge(hk_ready, 3)
            for j in range(GROUP):
                u_slot(n0 + j, j % 2, j, j, first=j < 2)

            def group(g, b, first=False):
                s = n0 + GROUP + 8 * (g - 1)
                for j in range(GROUP):
                    u_slot(s + 2 * j, 0, GROUP * g + j, j)
                    v_slot(s + 2 * j + 1, 1, g - 1, j, b, first)

            group(1, 0, first=True)
            with pe.Fori(0, (NGROUPS - 2) // 2) as i:
                for b in range(2):
                    group(2 * i + 2 + b, (b + 1) % 2)
            for j in range(GROUP):
                v_slot(n0 + GROUP + 8 * (NGROUPS - 1) + j, j % 2, NGROUPS - 1, j, 1)
            pe.wait_ge(p_lo, 1)
            for s in range(2):
                n = S0["proj"] + s
                pe.wait_ge(lo_ready, n + 1)
                for m in range(8):
                    if s == 0 and m < 4:
                        pe.wait_ge(h_acc, 16 * NGROUPS - 3 + m)
                    else:
                        pe.wait_ge(proj_copied, 8 * s + m - 3)
                    for k in range(2):
                        w = slice(k * 1024 + m * P, k * 1024 + (m + 1) * P)
                        ins = three(ps[:, 2 + m % 4, :], wH[s][:, w], wL[s][:, w], pH[:, k, :], pL[:, k, :], k == 0, k == 1)
                    ins.then_inc(tile_done, 1)
                if s == 0:
                    norm_sum("ple", 7)
            tile(S0["gate"], 0, 0, waits=N_SC["ple"])
            tile(S0["gate"] + 1, 1, 1)
            with pe.Fori(1, 8) as i:
                for j in range(2):
                    pe.wait_ge(sig_done, 2 * i + j - 1)
                    tile(S0["gate"] + 2 * i + j, j, j)
            norm_sum("final", 7)


OUT_ORDER = list(range(8, 16)) + list(range(8))


def kernel(**inputs):
    import numpy as np
    import concourse.bacc as bacc
    from concourse.bass_utils import run_bass_kernel_spmd

    v = {k: np.asarray(x) for k, x in inputs.items()}
    w_in = v["w_in"][0]
    off_kr, off_u, off_v = QL + KVL, QL + KVL + ROPE_D, QL + KVL + ROPE_D + 1024

    def tiles(w):
        k, m = w.shape
        return w.reshape(k // P, P, m // P, P).transpose(2, 1, 0, 3).reshape(m // P, P, k)

    def wide(w, cols):
        k, m = w.shape
        return w.reshape(k // P, P, m // cols, cols).transpose(2, 1, 0, 3).reshape(m // cols, P, k // P * cols)

    uq = v["w_uq"][0].reshape(QL, HEADS, 128 + ROPE_D)
    ukv = v["w_ukv"][0].reshape(KVL, HEADS, 256)
    kr = w_in[:, off_kr:off_u]
    cols = lambda g: g.reshape(-1, P).T
    arrays = {
        "x": v["x"][0].T.reshape(KD, P, T).transpose(1, 0, 2),
        "p": v["p"][0, 0].T.reshape(2, P, T).transpose(1, 0, 2),
        "pos": v["positions"].reshape(1, T),
        "gains": np.concatenate([cols(v[k].reshape(-1)) for k in ("g_mix", "g_ffn", "g_ple", "g_final", "g_out_attn", "g_out_sgu", "g_cq", "g_ckv")], axis=1),
        "rows": np.concatenate([v[k].reshape(1, 1024) for k in ("b_sgu", "g_ln_sgu", "b_ln_sgu")], axis=1),
        "ws": v["w_sgu"][0].transpose(2, 0, 1),
        "keys": np.stack([v["peer_k1"][0], v["peer_k2"][0]], axis=1).transpose(3, 0, 1, 2),
        "s_v": w_in[:, off_v:].reshape(4, 4, P, 2, 512).transpose(3, 0, 2, 1, 4).reshape(8, P, 2048),
        "s_u": tiles(w_in[:, off_u:off_v]),
        "s_c": tiles(np.concatenate([w_in[:, :off_kr], kr, kr], axis=1)),
        "s_uq": wide(np.concatenate([uq[:, :, :128].reshape(QL, -1), uq[:, :, 128:].reshape(QL, -1)], axis=1), 512),
        "s_ukv": wide(np.concatenate([ukv[:, :, :128].reshape(KVL, -1), ukv[:, :, 128:].reshape(KVL, -1)], axis=1), 1024),
        "s_out": tiles(v["w_out"][0]),
        "s_pq": tiles(v["w_peer_q"][0]),
        "s_pu": v["peer_u"][0].reshape(KEYS, KEYS, KD, P).transpose(1, 3, 2, 0).reshape(KEYS, P, 2048),
        "s_pv": v["peer_v"][0].reshape(KEYS, NGROUPS, GROUP, 4, 512).transpose(1, 3, 0, 2, 4).reshape(KEYS, P, 2048),
        "s_proj": wide(v["w_ple_proj"][0], 1024),
        "s_gate": tiles(v["w_ple_gate"][0]),
    }
    half = ROPE_D // 2
    consts = np.zeros((P, 386), np.float32)
    consts[:, 0:128] = np.eye(P, dtype=np.float32)
    consts[:, 128:256] = np.arange(P, dtype=np.float32)[None, :]
    for o in range(P):
        if o % ROPE_D < half:
            consts[o + half, 256 + o] = -1.0
        else:
            consts[o - half, 256 + o] = 1.0
    exponent = -np.arange(half, dtype=np.float32) / np.float32(half)
    consts[:, 384:386] = np.tile(np.power(np.float32(10000.0), exponent).astype(np.float32), 4)[:, None]
    arrays["consts"] = consts
    arrays = {k: np.ascontiguousarray(x) for k, x in arrays.items()}

    nc = bacc.Bacc("TRN2", target_bir_lowering=False, num_devices=1)
    aps = {k: nc.dram_tensor(k, x.shape, mybir.dt.from_np(x.dtype), kind="ExternalInput").ap() for k, x in arrays.items()}
    stream = {k[2:]: x for k, x in aps.items() if k.startswith("s_")}
    gates = nc.dram_tensor("gates", (NTB, KEYS, KEYS, TB), mybir.dt.float32, kind="Internal").ap()
    out = nc.dram_tensor("out", (P, KD, T), mybir.dt.float32, kind="ExternalOutput").ap()
    trunk_layer(nc, aps, stream, out, gates)
    r = run_bass_kernel_spmd(nc, [arrays], core_ids=[0])
    return r.results[0]["out"].transpose(1, 0, 2).reshape(D, T).T.reshape(1, T, D)
```

```python
import math

import concourse.bass as bass
from concourse import mybir
from contextlib import ExitStack, contextmanager

P = 128
T = 512
NT = T // P
D = 2048
KD = D // P
HEADS = 8
ROPE_D = 64
QL, KVL = 512, 256
KQ, KKV = QL // P, KVL // P
SGU_TILES = 8
TOPK = 16
KEYS = 128
EPS = 1e-6
GROUP = 4
NGROUPS = KEYS // GROUP
TB = 32
NTB = T // TB
QUADS = T // 4
PRE_GROUPS = 6
NPRE = PRE_GROUPS * GROUP
SCALE = float(128 + ROPE_D) ** -0.5
PI = math.pi
PI_BELOW = 3.1415925
def two_pi_parts():
    parts, left = [], 2 * PI
    for _ in range(3):
        scale = 2.0 ** (8 - math.frexp(left)[1])
        parts.append(math.floor(left * scale) / scale)
        left -= parts[-1]
    return parts + [left]


ROUND = 12582912.0

PEER_SLOTS = [1] * NPRE + [4] * (NPRE - GROUP) + [1, 4] * (KEYS - NPRE) + [4] * GROUP
STREAM = [("v", [1, 1, 1, 4] * 2), ("u", [1] * 8), ("c", [1] * 7), ("uq", [4] * 3), ("ukv", [8] * 2),
          ("out", [1] * 16), ("pq", [1] * 16), ("peer", PEER_SLOTS), ("proj", [8] * 2), ("gate", [1] * 16)]
S0 = {}
CUM = {-2: 0, -1: 0}
_n = 0
for _name, _marks in STREAM:
    S0[_name] = _n
    for _m in _marks:
        CUM[_n] = CUM[_n - 1] + _m
        _n += 1
NSLOTS = _n

GAINS = {}
_c = 0
for _name, _k in (("mix", KD), ("ffn", KD), ("ple", KD), ("final", KD), ("attn", 8), ("sgu", 8), ("cq", KQ), ("ckv", KKV)):
    GAINS[_name] = _c
    _c += _k
NGAINS = _c


class Steps:

    def __init__(self, eng, sem):
        self.eng, self.sem, self.base, self.k = eng, sem, 0, 0

    def did(self, ins):
        ins.then_inc(self.sem, 1)
        self.k += 1

    def settle(self):
        self.eng.wait_ge(self.sem, self.base + self.k)

    @contextmanager
    def loop(self, count, per):
        start = self.base + self.k
        with self.eng.Fori(0, count) as i:
            self.base, self.k = start + i * per, 0
            yield i
            assert self.k == per, (self.k, per)
        self.base, self.k = start + count * per, 0


def trunk_layer(nc, a, stream, out, gates_dram, pre_dram):
    F, R, U32, I32 = mybir.dt.float32, mybir.dt.float32r, mybir.dt.uint32, mybir.dt.int32
    ACT = mybir.ActivationFunctionType
    ALU = mybir.AluOpType
    AX = mybir.AxisListType.X

    base = (nc.sbuf_base + 31) // 32 * 32
    KB = 1024

    def at(name, shape, dt, offset):
        return nc.alloc_sbuf_tensor_at(name, [P] + shape, dt, offset=base + offset)

    H0, A0, RING0, W0, M0, C0 = 0, 32 * KB, 96 * KB, 144 * KB, 176 * KB, 192 * KB
    hT = at("hT", [KD, T], F, H0)
    vtok = at("vtok", [NT, 1024], F, H0)
    cT = at("cT", [7, T], F, H0 + 16 * KB)
    perm = at("perm", [P], F, H0 + 30 * KB)
    ln_stats = at("ln_stats", [8, 6], F, H0 + 30 * KB + 512)
    ln_mv = at("ln_mv", [8, 2], F, H0 + 30 * KB + 704)
    ln_rstd = at("ln_rstd", [8], F, H0 + 30 * KB + 768)
    freq = at("freq", [2], F, H0 + 30 * KB + 800)
    aH = at("aH", [KD, T], R, A0)
    aL = at("aL", [KD, T], R, A0 + 32 * KB)
    qT = at("qT", [12, T], F, A0)
    kT = at("kT", [HEADS, T], F, A0 + 24 * KB)
    vA = at("vA", [NT, 1024], F, A0 + 40 * KB)
    ckvH = at("ckvH", [KKV, T], R, A0 + 56 * KB)
    ckvL = at("ckvL", [KKV, T], R, A0 + 60 * KB)
    raw = [at(f"raw{i}", [2048], F, RING0 + 8 * KB * i) for i in range(2)]
    wH = [at(f"wH{i}", [2048], R, RING0 + (16 + 8 * i) * KB) for i in range(2)]
    wL = [at(f"wL{i}", [2048], R, RING0 + (32 + 8 * i) * KB) for i in range(2)]
    mixT = at("mixT", [KD, T], F, W0)
    cqH = at("cqH", [KQ, T], R, W0)
    cqL = at("cqL", [KQ, T], R, W0 + 8 * KB)
    pqT = [at(f"pqT{i}", [2, T], F, W0 + 4 * KB * i) for i in range(2)]
    keys = at("keys", [HEADS, 2, KEYS], F, W0 + 8 * KB)
    gstage = [at(f"gstage{i}", [KEYS, TB], F, W0 + 16 * KB * i) for i in range(2)]
    actH = [at(f"actH{i}", [GROUP, T], R, W0 + 16 * KB * i) for i in range(2)]
    actL = [at(f"actL{i}", [GROUP, T], R, W0 + 16 * KB * i + 8 * KB) for i in range(2)]
    projT = at("projT", [KD, T], F, W0)
    sgu_rows = at("sgu_rows", [3, 8, P], F, M0)
    wsT = at("wsT", [8, P], F, M0 + 12 * KB)
    cosT = at("cosT", [T], F, M0)
    sinT = at("sinT", [T], F, M0 + 2 * KB)
    krT = at("krT", [T], F, M0 + 4 * KB)
    prob = [at(f"prob{i}", [T], F, M0 + (6 + 2 * i) * KB) for i in range(2)]
    probT = [at(f"probT{i}", [T], F, M0 + (10 + 2 * i) * KB) for i in range(2)]
    rstdB = at("rstdB", [T], F, M0 + 14 * KB)
    rstdL = at("rstdL", [T], F, M0 + 4 * KB)
    rest = at("rest", [8, KEYS], F, M0)
    match = at("match", [NT, TOPK, TOPK], F, M0)
    cand = at("cand", [NT, 256], F, M0 + 4 * KB)
    cand_rest = at("cand_rest", [NT, 256], F, M0 + 8 * KB)
    top = at("top", [2, NT, TOPK], F, M0 + 12 * KB)
    top_at = at("top_at", [2, NT, TOPK], U32, M0 + 12 * KB + 512)
    top_atf = at("top_atf", [2, NT, TOPK], F, M0 + 13 * KB)
    best = at("best", [NT, TOPK], F, M0 + 13 * KB + 512)
    best_at = at("best_at", [NT, TOPK], U32, M0 + 13 * KB + 768)
    best_k = at("best_k", [2, NT, TOPK], U32, M0 + 14 * KB)
    best_kf = at("best_kf", [2, NT, TOPK], F, M0 + 14 * KB + 512)
    gate_e = at("gate_e", [NT, TOPK], F, M0 + 15 * KB)
    gate_sum = at("gate_sum", [NT], F, M0 + 15 * KB + 256)
    gate_inv = at("gate_inv", [NT], F, M0 + 15 * KB + 288)
    hk = at("hk", [3, T], F, M0)
    oh1 = at("oh1", [2, 4, P], F, M0 + 6 * KB)
    oh2 = at("oh2", [2, 4, P], F, M0 + 10 * KB)
    gtile = [at(f"gtile{i}", [NTB, GROUP, TB], F, M0 + 8 * KB * i) for i in range(2)]
    pRaw = at("pRaw", [2, T], F, M0)
    pH = at("pH", [2, T], R, M0 + 8 * KB)
    pL = at("pL", [2, T], R, M0 + 12 * KB)
    tmp = [at(f"tmp{i}", [T], F, C0 + 2 * KB * i) for i in range(2)]
    sq = [at(f"sq{i}", [T], F, C0 + (4 + 2 * i) * KB) for i in range(2)]
    route = at("route", [3, NT, P], F, C0)
    ssum = at("ssum", [T], F, C0 + 8 * KB)
    ut = [at(f"ut{i}", [T], F, C0 + (6 + 2 * i) * KB) for i in range(2)]
    rstd = at("rstd", [T], F, C0 + 10 * KB)
    ident = at("ident", [P], F, C0 + 12 * KB)
    iota = at("iota", [P], F, C0 + 12 * KB + 512)
    identR = at("identR", [P], R, C0 + 13 * KB)
    causalR = at("causalR", [P], R, C0 + 13 * KB + 512)
    ones = at("ones", [P], F, C0 + 14 * KB)
    gains = at("gains", [NGAINS], F, C0 + 14 * KB + 512)
    smax = at("smax", [32], F, C0 + 14 * KB + 864)
    nbias = at("nbias", [32], F, C0 + 14 * KB + 992)
    rsum = at("rsum", [32], F, C0 + 14 * KB + 1120)
    rinv = at("rinv", [32], F, C0 + 14 * KB + 1248)
    held = at("held", [1], F, C0 + 14 * KB + 1376)
    rtok = at("rtok", [NT], F, C0 + 14 * KB + 1408)

    ctx = ExitStack()
    with ctx:
        ps = ctx.enter_context(nc.psum_tensor("ps", [P, 8, 512], F))

        def sem(name):
            return ctx.enter_context(nc.semaphore(name))

        x_loaded = [sem(f"x_loaded{i}") for i in range(8)]
        consts_loaded = sem("consts_loaded")
        rows_loaded, perm_loaded = sem("rows_loaded"), sem("perm_loaded")
        raw_loaded = [sem(f"raw_loaded{i}") for i in range(2)]
        hi_ready, lo_ready, tile_done = sem("hi_ready"), sem("lo_ready"), sem("tile_done")
        dve_step, act_step, pool_step = sem("dve_step"), sem("act_step"), sem("pool_step")
        consts_ready = sem("consts_ready")
        causal_built = sem("causal_built")
        sq_ready, sq_added, sum_done, mean_ready, root_ready, rstd_ready = (
            sem("sq_ready"), sem("sq_added"), sem("sum_done"), sem("mean_ready"), sem("root_ready"), sem("rstd_ready"))
        act_scaled, act_hi, act_lo = sem("act_scaled"), sem("act_hi"), sem("act_lo")
        v_gelu, ln_var, ln_std, v_ready, u_gelu = sem("v_gelu"), sem("ln_var"), sem("ln_std"), sem("v_ready"), sem("u_gelu")
        c_copied = sem("c_copied")
        mix_done, sgu_ready = sem("mix_done"), sem("sgu_ready")
        angle_ready, trig_ready = sem("angle_ready"), sem("trig_ready")
        pos_loaded = sem("pos_loaded")
        uq_copied, swap_done, rope_ready = sem("uq_copied"), sem("swap_done"), sem("rope_ready")
        kv_copied = sem("kv_copied")
        score_done, nbias_ready, exp_done, p_ready = sem("score_done"), sem("nbias_ready"), sem("exp_done"), sem("p_ready")
        pt_done, pt_copied, pv_done, o_copied = sem("pt_done"), sem("pt_copied"), sem("pv_done"), sem("o_copied")
        x_again = sem("x_again")
        h_mixed, a_read = sem("h_mixed"), sem("a_read")
        tok_done, tok_ready, u_scaled, sgu_scaled = sem("tok_done"), sem("tok_ready"), sem("u_scaled"), sem("sgu_scaled")
        chunk_scaled = sem("chunk_scaled")
        pre_stored = [sem(f"pre_stored{i}") for i in range(2)]
        pre_loaded = [sem(f"pre_loaded{i}") for i in range(2)]
        g_scaled = sem("g_scaled")
        keys_loaded = sem("keys_loaded")
        pq_copied, ps_done, tops_done, gate_sub, gate_exp, routed = (
            sem("pq_copied"), sem("ps_done"), sem("tops_done"), sem("gate_sub"), sem("gate_exp"), sem("routed"))
        hkT_done, hk_ready = sem("hkT_done"), sem("hk_ready")
        onehot_ready, gquad_done, gquad_copied = sem("onehot_ready"), sem("gquad_done"), sem("gquad_copied")
        gates_stored = [sem(f"gates_stored{i}") for i in range(2)]
        gates_loaded = [sem(f"gates_loaded{i}") for i in range(2)]
        gelu_done, act_gated, act_whi, act_wlo, h_acc = (
            sem("gelu_done"), sem("act_gated"), sem("act_whi"), sem("act_wlo"), sem("h_acc"))
        p_loaded, p_hi, p_lo, proj_copied = sem("p_loaded"), sem("p_hi"), sem("p_lo"), sem("proj_copied")
        sig_done, h_gated = sem("sig_done"), sem("h_gated")
        out_ready, out_stored = sem("out_ready"), sem("out_stored")

        block = ctx.enter_context(nc.Block())

        def rstd_of(name):
            return {"cq": rstdL, "ckv": rstdL, "sgu": rstdB}.get(name, rstd)

        def gain(name, k):
            return gains[:, GAINS[name] + k:GAINS[name] + k + 1]

        N_SQ = {}
        _at = 0
        for name, k in (("mix", 16), ("cq", 4), ("ckv", 2), ("sgu", 8), ("attn", 8), ("ffn", 16), ("ple", 16), ("final", 16)):
            N_SQ[name] = _at
            _at += k
        NORMS = {n: i for i, n in enumerate(N_SQ)}
        N_SC = {}
        N_TMP = {"cq": 0, "ckv": 4, "attn": 6}
        _at = 0
        for name, k in (("mix", 16), ("cq", 4), ("ckv", 2), ("sgu", 8), ("attn", 8), ("ffn", 16), ("ple", 16)):
            N_SC[name] = _at
            _at += k

        @block.sync
        def _(sp):
            def load(n, src, parity):
                sp.wait_ge(lo_ready, n - 1)
                sp.dma_start(raw[parity][:, :], src).then_inc(raw_loaded[parity], 16)

            for i in range(8):
                sp.dma_start(hT[:, 2 * i:2 * i + 2, :], a["x"][:, 2 * i:2 * i + 2, :]).then_inc(x_loaded[i], 16)
                if i < 2:
                    sp.dma_start(raw[i][:, :], stream["v"][i, :, :]).then_inc(raw_loaded[i], 16)
            for n in range(2, 8):
                load(n, stream["v"][n, :, :], n % 2)
            with sp.Fori(0, 4) as i:
                for j in range(2):
                    load(S0["u"] + 2 * i + j, stream["u"][2 * i + j, :, :], j)
            for name in ("c", "uq", "ukv"):
                for j in range(len(dict(STREAM)[name])):
                    load(S0[name] + j, stream[name][j, :, :], (S0[name] + j) % 2)
            for name in ("out", "pq"):
                with sp.Fori(0, 8) as i:
                    for j in range(2):
                        load(S0[name] + 2 * i + j, stream[name][2 * i + j, :, :], j)
            n0 = S0["peer"]
            for j in range(2):
                load(n0 + j, stream["pu"][j, :, :], j)

            def store_chunk(c, b):
                sp.wait_ge(gelu_done, c + 1)
                sp.dma_start(pre_dram[c, :, :], ut[b][:, :]).then_inc(pre_stored[b], 16)

            def store_gates(t, b):
                sp.wait_ge(gquad_copied, 8 * t + 8)
                sp.dma_start(gates_dram[t, :, :, :], gstage[b][:, :, :]).then_inc(gates_stored[b], 16)

            def load_gates(g, b):
                sp.dma_start(gtile[b][:, :, :, :],
                             gates_dram[:, :, bass.ts(g, GROUP), :].rearrange("b p i t -> p b i t")).then_inc(gates_loaded[b], 16)

            def load_chunk(c, b):
                sp.wait_ge(pre_stored[b], (c - b) * 8 + 16)
                if c >= 2:
                    sp.wait_ge(act_wlo, c - 1)
                sp.dma_start(tmp[b][:, :], pre_dram[c, :, :]).then_inc(pre_loaded[b], 16)

            for u in range(6):
                load(n0 + u + 2, stream["pu"][u + 2, :, :], u % 2)
                if u >= 1:
                    store_chunk(u - 1, (u - 1) % 2)
                if u == 5:
                    store_gates(0, 0)
            with sp.Fori(0, NTB // 2 - 1) as i:
                for b in range(2):
                    load(n0 + 2 * i + b + 8, stream["pu"][2 * i + b + 8, :, :], b)
                    store_chunk(2 * i + b + 5, 1 - b)
                    store_gates(2 * i + b + 1, 1 - b)
            for u in range(20, NPRE):
                k = u + 2
                load(n0 + k, stream["pu"][k, :, :] if k < NPRE else stream["pv"][k - NPRE, :, :], u % 2)
                store_chunk(u - 1, (u - 1) % 2)
                if u == 20:
                    store_gates(NTB - 1, 1)
                if u == 21:
                    for b in range(2):
                        sp.wait_ge(gates_stored[b], 16 * (NTB // 2))
                    load_gates(0, 0)
                    load_chunk(0, 0)
                    load_chunk(1, 1)
                    load_gates(1, 1)
                if u == 22:
                    load_chunk(2, 0)
                    load_chunk(3, 1)
            store_chunk(NPRE - 1, 1)
            for g in range(1, PRE_GROUPS):
                for j in range(GROUP):
                    k = GROUP * (g - 1) + j + 2
                    if k < NPRE - GROUP:
                        load(n0 + NPRE + k, stream["pv"][k, :, :], j % 2)
                    if j == 0 and g >= 2:
                        sp.wait_ge(act_gated, GROUP * (g - 1))
                        load_gates(g, g % 2)
                    load_chunk(GROUP * g + j, j % 2)

            s0 = n0 + 2 * NPRE - GROUP

            def load_group(g, b):
                for j in range(GROUP):
                    n = s0 + 8 * (g - PRE_GROUPS) + 2 * j
                    load(n, stream["pu"][GROUP * g + j, :, :], 0)
                    if j == 0:
                        sp.wait_ge(act_gated, GROUP * (g - 1))
                        load_gates(g, b)
                    load(n + 1, stream["pv"][GROUP * (g - 1) + j, :, :], 1)

            with sp.Fori(0, (NGROUPS - PRE_GROUPS) // 2) as i:
                for b in range(2):
                    load_group(2 * i + PRE_GROUPS + b, b)
            sp.wait_ge(act_gated, GROUP * (NGROUPS - 1))
            sp.dma_start(pRaw[:, :, :], a["p"]).then_inc(p_loaded, 16)
            for j in range(GROUP):
                load(n0 + 2 * KEYS - GROUP + j, stream["pv"][GROUP * (NGROUPS - 1) + j, :, :], j % 2)
            for j in range(2):
                load(S0["proj"] + j, stream["proj"][j, :, :], j)
            with sp.Fori(0, 8) as i:
                for j in range(2):
                    load(S0["gate"] + 2 * i + j, stream["gate"][2 * i + j, :, :], j)
            for i in range(4):
                sp.wait_ge(out_ready, 4 * i + 4)
                sp.dma_start(out[:, 4 * i:4 * i + 4, :], hT[:, 4 * i:4 * i + 4, :]).then_inc(out_stored, 16)
            sp.wait_ge(out_stored, 64)

        @block.gpsimd
        def _(pool):
            for dst, src in ((gains[:, :], a["gains"]), (ident[:, :], a["consts"][:, 0:128]),
                             (iota[:, :], a["consts"][:, 128:256])):
                pool.dma_start(dst, src).then_inc(consts_loaded, 16)
            pool.dma_start(wsT[:, :, :], a["ws"]).then_inc(rows_loaded, 16)
            pool.dma_start(sgu_rows[:, :, :, :].rearrange("p a b c -> p (a b c)"),
                           a["rows"].partition_broadcast(P)).then_inc(rows_loaded, 16)
            nc.gpsimd.memset(ones[:, :], 1.0).then_inc(consts_ready, 1)
            nc.gpsimd.memset(ssum[:, 0:P], 0.0).then_inc(pool_step, 1)
            pool.wait_ge(pool_step, 1)
            nc.gpsimd.affine_select(out=ssum[:, 0:P], in_=ssum[:, 0:P], compare_op=ALU.is_ge, fill=-1e30,
                                    base=0, pattern=[[-1, P]], channel_multiplier=1).then_inc(causal_built, 1)
            pool.wait_ge(rows_loaded, 32)
            nc.gpsimd.affine_select(out=wsT[:, :, :], in_=wsT[:, :, :], compare_op=ALU.is_ge, fill=0.0,
                                    base=0, pattern=[[0, 8], [1, P]], channel_multiplier=-1).then_inc(consts_ready, 1)
            pool.wait_ge(act_lo, KD)
            pool.wait_ge(sq_ready, KD)
            pool.dma_start(perm[:, :], a["consts"][:, 256:384]).then_inc(perm_loaded, 16)
            pool.dma_start(freq[:, :], a["consts"][:, 384:386]).then_inc(perm_loaded, 16)
            pool.wait_ge(sgu_ready, 8)
            pool.dma_start(krT[:, :].bitcast(I32), a["pos"].partition_broadcast(P)).then_inc(pos_loaded, 16)
            pool.wait_ge(rope_ready, 5)
            for i in range(4):
                pool.dma_start(hT[:, 4 * i:4 * i + 4, :], a["x"][:, 4 * i:4 * i + 4, :]).then_inc(x_again, 16)
            pool.wait_ge(act_lo, N_SC["ffn"])
            pool.dma_start(keys[:, :, :, :], a["keys"]).then_inc(keys_loaded, 16)

        @block.scalar
        def _(act):
            A = nc.scalar.activation

            def hi(n, parity, used):
                act.wait_ge(raw_loaded[parity], (n - parity) * 8 + 16)
                if not (isinstance(used, int) and used <= 0):
                    act.wait_ge(tile_done, used)
                A(wH[parity][:, :], raw[parity][:, :], ACT.Copy).then_inc(hi_ready, 1)

            def square(name, k, src):
                n = N_SQ[name] + k
                if not (isinstance(n, int) and n < 2):
                    act.wait_ge(sq_added, n - 1)
                A(sq[k0(k) % 2][:, :], src, ACT.Square).then_inc(sq_ready, 1)

            def root(name):
                act.wait_ge(mean_ready, NORMS[name] + 1)
                dst = rstd_of(name)
                A(dst[:, :], dst[:, :], ACT.Sqrt).then_inc(root_ready, 1)

            def split_hi(name, order, dst):
                for j, k in enumerate(order):
                    act.wait_ge(act_scaled, N_TMP[name] + j + 1)
                    A(dst[:, k, :], tmp[j % 2][:, :], ACT.Copy).then_inc(act_hi, 1)

            def gain_hi(name, k):
                A(aH[:, k, :], hT[:, k, :], ACT.Copy, scale=gain(name, k)).then_inc(act_hi, 1)

            def k0(k):
                return k if isinstance(k, int) else 0

            act.wait_ge(consts_loaded, 48)
            A(identR[:, :], ident[:, :], ACT.Copy)
            act.wait_ge(causal_built, 1)
            A(causalR[:, :], ssum[:, 0:P], ACT.Copy).then_inc(consts_ready, 1)

            for k in range(KD):
                if k % 2 == 0:
                    act.wait_ge(x_loaded[k // 2], 16)
                gain_hi("mix", k)
                square("mix", k, hT[:, k, :])
                if k in (1, 3):
                    hi(k // 2, k // 2, 0)
            hi(2, 0, CUM[0])
            root("mix")
            for cb in range(2):
                for n in range(max(2, S0["v"] + 4 * cb), S0["v"] + 4 * cb + 4):
                    hi(n + 1, (n + 1) % 2, CUM[n - 1])
                if cb == 0:
                    act.wait_ge(tok_ready, 1)
                for tt in range(NT):
                    act.wait_ge(tile_done, 7 * cb + 4 + tt)
                    A(vtok[:, tt, cb * 512:cb * 512 + 512], ps[:, tt, :], ACT.Gelu_apprx_tanh,
                      scale=rtok[:, tt:tt + 1]).then_inc(v_gelu, 1)
            with act.Fori(0, 4) as i:
                for j in range(2):
                    n = S0["u"] + 2 * i + j
                    hi(n + 1, (j + 1) % 2, CUM[S0["u"] + j - 1] + 2 * i)
                    if j == 0:
                        act.wait_ge(ln_var, i + 1)
                        A(ln_rstd[:, :], ln_rstd[:, :], ACT.Sqrt).then_inc(ln_std, 1)
                    act.wait_ge(u_scaled, 2 * i + j + 1)
                    u = mixT[:, 8 + 2 * i + j, :]
                    A(u, u, ACT.Gelu_apprx_tanh).then_inc(u_gelu, 1)
            for j in range(7):
                n = S0["c"] + j
                hi(n + 1, (n + 1) % 2, CUM[n - 1])
                if j < 4:
                    act.wait_ge(c_copied, j + 1)
                    square("cq", j, cT[:, j, :])
                elif j < 6:
                    act.wait_ge(c_copied, j + 1)
                    square("ckv", j - 4, cT[:, j, :])
                if j == 4:
                    root("cq")
                    split_hi("cq", range(KQ), cqH)
            root("ckv")
            split_hi("ckv", range(KKV), ckvH)
            for g in range(SGU_TILES):
                act.wait_ge(sgu_ready, g + 1)
                square("sgu", g, mixT[:, 8 + g, :])
            root("sgu")
            act.wait_ge(angle_ready, 1)
            A(cosT[:, :], cosT[:, :], ACT.Sin).then_inc(trig_ready, 1)
            act.wait_ge(angle_ready, 2)
            A(sinT[:, :], sinT[:, :], ACT.Sin).then_inc(trig_ready, 1)
            for s in range(3):
                n = S0["uq"] + s
                hi(n + 1, (n + 1) % 2, CUM[n - 1])
                for m in range(4):
                    t = 4 * s + m
                    act.wait_ge(tile_done, CUM[n - 1] + m + 1)
                    A(qT[:, t, :], ps[:, 4 + t % 4, :], ACT.Copy).then_inc(uq_copied, 1)
            for s in range(2):
                n = S0["ukv"] + s
                hi(n + 1, (n + 1) % 2, CUM[n - 1])
                for m in range(8):
                    act.wait_ge(tile_done, CUM[n - 1] + m + 1)
                    dst = kT[:, m, :] if s == 0 else vA[:, m % 4, 512 * (m // 4):512 * (m // 4) + 512]
                    A(dst, ps[:, 4 + m % 4, :], ACT.Copy).then_inc(kv_copied, 1)
            ITEMS = HEADS * NT
            for n in range(ITEMS + 3):
                if n < ITEMS:
                    w = P * (n % NT + 1)
                    act.wait_ge(nbias_ready, n + 1)
                    if n >= 2:
                        act.wait_ge(pt_done, n - 1)
                    A(prob[n % 2][:, 0:w], ps[:, n % 3, 0:w], ACT.Exp, bias=nbias[:, n:n + 1], scale=SCALE,
                      accum_out=rsum[:, n:n + 1]).then_inc(exp_done, 1)
                m = n - 2
                if 0 <= m < ITEMS:
                    w = P * (m % NT + 1)
                    act.wait_ge(pt_done, m + 1)
                    if m >= 2:
                        act.wait_ge(pv_done, m - 1)
                    A(probT[m % 2][:, 0:w], ps[:, 3 + m % 2, 0:w], ACT.Copy).then_inc(pt_copied, 1)
                if n >= 5 and (n - 5) % NT == 3:
                    h = (n - 5) // NT
                    act.wait_ge(o_copied, h + 1)
                    square("attn", h, mixT[:, h, :])
            for h in range((ITEMS + 2 - 5 - 3) // NT + 1, HEADS):
                act.wait_ge(o_copied, h + 1)
                square("attn", h, mixT[:, h, :])
            act.wait_ge(pv_done, ITEMS)
            act.wait_ge(sgu_scaled, 8)
            for g in range(SGU_TILES):
                A(aH[:, 8 + g, :], mixT[:, 8 + g, :], ACT.Copy).then_inc(act_hi, 1)
                if g == 3:
                    root("attn")
            split_hi("attn", range(8), aH)

            def mixed_square(i, j):
                act.wait_ge(h_mixed, 2 * i + j + 1)
                act.wait_ge(sq_added, N_SQ["ffn"] - 1 + 2 * i + j)
                A(sq[j][:, :], hT[:, 2 * i + j, :], ACT.Square).then_inc(sq_ready, 1)

            with act.Fori(0, 7) as i:
                for j in range(2):
                    hi(S0["out"] + 2 * i + j + 1, (j + 1) % 2, CUM[S0["out"] + j - 1] + 2 * i)
                    mixed_square(i, j)
            hi(S0["out"] + 15, 1, CUM[S0["out"] + 13])
            mixed_square(7, 0)
            hi(S0["out"] + 16, 0, CUM[S0["out"] + 14])
            for k in range(KD - 1):
                act.wait_ge(a_read, k + 1)
                gain_hi("ffn", k)
            mixed_square(7, 1)
            gain_hi("ffn", KD - 1)
            def query_tiles(h, b, i, j0):
                for s in range(2):
                    j = j0 + s
                    hi(S0["pq"] + 2 * h + s + 1, (s + 1) % 2, CUM[S0["pq"] + j - 1] + 4 * i)
                    if isinstance(h, int) and h == s == 0:
                        root("ffn")
                    act.wait_ge(tile_done, CUM[S0["pq"] + j] + 4 * i)
                    A(pqT[b][:, s, :], ps[:, s, :], ACT.Copy).then_inc(pq_copied, 1)

            def gate_exps(h):
                act.wait_ge(gate_sub, h + 1)
                for t in range(NT):
                    ins = A(gate_e[:, t, :], gate_e[:, t, :], ACT.Exp, scale=rtok[:, t:t + 1])
                ins.then_inc(gate_exp, 1)

            query_tiles(0, 0, 0, 0)
            act.wait_ge(tok_ready, 2)
            with act.Fori(0, 3) as i:
                for b in range(2):
                    query_tiles(2 * i + b + 1, 1 - b, i, 2 + 2 * b)
                    gate_exps(2 * i + b)
            query_tiles(7, 1, 3, 2)
            gate_exps(6)

            n0 = S0["peer"]

            def gelu(uc, b):
                act.wait_ge(chunk_scaled, uc + 1)
                A(ut[b][:, :], ut[b][:, :], ACT.Gelu_apprx_tanh).then_inc(gelu_done, 1)

            def pre_hi(u):
                hi(n0 + u + 1, (u + 1) % 2, CUM[n0 + u - 1])

            pre_hi(0)
            gelu(0, 0)
            pre_hi(1)
            gate_exps(7)
            gelu(1, 1)
            pre_hi(2)
            gelu(2, 0)
            pre_hi(3)
            for r in range(3):
                act.wait_ge(hkT_done, r + 1)
                A(hk[:, r, :], ps[:, 2 + r, :], ACT.Copy).then_inc(hk_ready, 1)

            def gate_block(t, b, i):
                hi(n0 + 5 + t, 1 - b, CUM[n0 + 3 + b] + 2 * i)
                gelu(3 + t, 1 - b)
                if not (isinstance(i, int) and i == 0):
                    act.wait_ge(gates_stored[b], 16 * i)
                for q in range(8):
                    act.wait_ge(gquad_done, 8 * t + q + 1)
                    A(gstage[b][:, :, 4 * q:4 * q + 4].rearrange("p i t -> p t i"),
                      ps[:, 4 + q % 4, :].rearrange("p (t i) -> p t i", t=4), ACT.Copy).then_inc(gquad_copied, 1)

            for b in range(2):
                gate_block(b, b, 0)
            with act.Fori(1, NTB // 2) as i:
                for b in range(2):
                    gate_block(2 * i + b, b, i)

            def weight_hi(uc, j, b, src):
                act.wait_ge(act_gated, uc + 1)
                A(actH[b][:, j, :], src[:, :], ACT.Copy).then_inc(act_whi, 1)

            for u in range(20, NPRE):
                pre_hi(u)
                gelu(u - 1, (u - 1) % 2)
                if u == 22:
                    weight_hi(0, 0, 0, tmp[0])
                    weight_hi(1, 1, 0, tmp[1])
                if u == 23:
                    weight_hi(2, 2, 0, tmp[0])
                    weight_hi(3, 3, 0, tmp[1])
            gelu(NPRE - 1, 1)
            for g in range(1, PRE_GROUPS):
                for j in range(GROUP):
                    n = n0 + NPRE + GROUP * (g - 1) + j
                    hi(n + 1, (j + 1) % 2, CUM[n - 1])
                    weight_hi(GROUP * g + j, j, g % 2, tmp[j % 2])

            s0 = n0 + 2 * NPRE - GROUP

            with act.Fori(0, (NGROUPS - PRE_GROUPS) // 2) as i:
                for b in range(2):
                    for j in range(GROUP):
                        m = s0 + 8 * b + 2 * j
                        g = 2 * i + PRE_GROUPS + b
                        hi(m + 1 + 16 * i, 1, CUM[m - 1] + 40 * i)
                        gelu(GROUP * g + j, j % 2)
                        hi(m + 2 + 16 * i, 0, CUM[m] + 40 * i)
                        weight_hi(GROUP * g + j, j, b, ut[j % 2])
            last = n0 + 2 * KEYS - GROUP
            for j in range(GROUP):
                hi(last + j + 1, (j + 1) % 2, CUM[last + j - 1])
                if j == 0:
                    act.wait_ge(p_loaded, 16)
                    A(pH[:, :, :], pRaw[:, :, :], ACT.Copy).then_inc(p_hi, 1)
                for m in range(4):
                    act.wait_ge(h_acc, 16 * (NGROUPS - 1) + 4 * j + m + 1)
                    square("ple", 4 * j + m, hT[:, 4 * j + m, :])
                    gain_hi("ple", 4 * j + m)
            for s in range(2):
                n = S0["proj"] + s
                if s == 1:
                    root("ple")
                hi(n + 1, (n + 1) % 2, CUM[n - 1])
                for m in range(8):
                    act.wait_ge(tile_done, CUM[n - 1] + m + 1)
                    A(projT[:, 8 * s + m, :], ps[:, 2 + m % 4, :], ACT.Copy).then_inc(proj_copied, 1)

            def gate_tile(i, j, last=False):
                if not last:
                    hi(S0["gate"] + 2 * i + j + 1, (j + 1) % 2, CUM[S0["gate"] + j - 1] + 2 * i)
                act.wait_ge(g_scaled, 2 * i + j + 1)
                A(tmp[j][:, :], tmp[j][:, :], ACT.Sigmoid).then_inc(sig_done, 1)
                act.wait_ge(h_gated, 2 * i + j + 1)
                act.wait_ge(sq_added, N_SQ["final"] - 1 + 2 * i + j)
                A(sq[j][:, :], hT[:, 2 * i + j, :], ACT.Square).then_inc(sq_ready, 1)

            for j in range(2):
                gate_tile(0, j)
            with act.Fori(1, 7) as i:
                for j in range(2):
                    gate_tile(i, j)
            for j in range(2):
                gate_tile(7, j, last=j == 1)
            root("final")

        @block.vector
        def _(dve):
            V = nc.vector
            st = Steps(dve, dve_step)

            def hold():
                V.tensor_copy(held[:, :], ones[:, 0:1])

            def lo(n, parity):
                dve.wait_ge(hi_ready, n + 1)
                V.tensor_tensor(wL[parity][:, :], raw[parity][:, :], wH[parity][:, :].bitcast(F), ALU.subtract).then_inc(lo_ready, 1)

            def add_square(name, k, first=False, par=None):
                n = N_SQ[name] + k
                dve.wait_ge(sq_ready, n + 1)
                s = sq[k % 2 if par is None else par]
                if first:
                    if not (isinstance(n, int) and n == 0):
                        dve.wait_ge(sum_done, NORMS[name])
                    V.tensor_copy(ssum[:, :], s[:, :]).then_inc(sq_added, 1)
                else:
                    dve.wait_ge(sq_added, n)
                    V.tensor_tensor(ssum[:, :], ssum[:, :], s[:, :], ALU.add).then_inc(sq_added, 1)

            def mean_of(name, width, bank):
                dst = rstd_of(name)
                dve.wait_ge(sum_done, NORMS[name] + 1)
                V.tensor_scalar(dst[:, :], ps[:, bank, :], 1.0 / width, EPS, ALU.mult, ALU.add).then_inc(mean_ready, 1)

            def inverse_root(name, width, bank):
                mean_of(name, width, bank)
                invert(name)

            def invert(name):
                dst = rstd_of(name)
                dve.wait_ge(root_ready, NORMS[name] + 1)
                V.reciprocal(dst[:, :], dst[:, :]).then_inc(rstd_ready, 1)
                dve.wait_ge(rstd_ready, NORMS[name] + 1)

            def scale_split(name, tiles, hi_dst, lo_dst):
                def low(j):
                    dve.wait_ge(act_hi, N_SC[name] + j + 1)
                    k = tiles[j][0]
                    V.tensor_tensor(lo_dst[:, k, :], tmp[j % 2][:, :], hi_dst[:, k, :].bitcast(F), ALU.subtract).then_inc(act_lo, 1)

                for j, (k, src, g, r) in enumerate(tiles):
                    if j >= 2:
                        dve.wait_ge(act_lo, N_SC[name] + j - 1)
                    V.scalar_tensor_tensor(tmp[j % 2][:, :], src, g, r[:, :], ALU.mult, ALU.mult).then_inc(act_scaled, 1)
                    if j >= 1:
                        low(j - 1)
                low(len(tiles) - 1)

            def gain_lo(name, k):
                dve.wait_ge(act_hi, N_SC[name] + k + 1)
                V.scalar_tensor_tensor(aL[:, k, :], hT[:, k, :], gain(name, k), aH[:, k, :].bitcast(F),
                                       ALU.mult, ALU.subtract).then_inc(act_lo, 1)

            def token_rms(n, bank):
                dve.wait_ge(tok_done, n)
                V.tensor_copy(rtok[:, :], ps[:, bank, 0:NT]).then_inc(tok_ready, 1)

            for k in range(KD):
                gain_lo("mix", k)
                add_square("mix", k, first=k == 0)
                if k == 1:
                    lo(0, 0)
                if k == 3:
                    lo(1, 1)
            lo(2, 0)
            inverse_root("mix", D, 7)

            for n in range(3, 9):
                lo(n, n % 2)
                if n == 3:
                    token_rms(1, 7)
            dve.wait_ge(v_gelu, 8)
            dve.wait_ge(rows_loaded, 32)
            with st.loop(4, 8 + 8 + 1 + 8 + 1) as i:
                def scale_u(j):
                    dve.wait_ge(tile_done, CUM[S0["u"] + j] + 2 * i)
                    V.tensor_tensor(mixT[:, 8 + 2 * i + j, :], ps[:, 4 + j, :], rstd[:, :], ALU.mult).then_inc(u_scaled, 1)

                lo(S0["u"] + 2 * i + 1, 1)
                for g in range(8):
                    st.did(V.bn_stats(ln_stats[:, g, :], vtok[:, i, g * P:(g + 1) * P]))
                st.settle()
                hold()
                for g in range(8):
                    st.did(V.bn_aggr(ln_mv[:, g, :], ln_stats[:, g, :]))
                st.settle()
                V.tensor_scalar_add(ln_rstd[:, :], ln_mv[:, :, 1], EPS).then_inc(ln_var, 1)
                dve.wait_ge(ln_std, i + 1)
                st.did(V.reciprocal(ln_rstd[:, :], ln_rstd[:, :]))
                st.settle()
                for g in range(8):
                    v = vtok[:, i, g * P:(g + 1) * P]
                    st.did(V.tensor_scalar(v, v, ln_mv[:, g, 0:1], ln_rstd[:, g:g + 1], ALU.subtract, ALU.mult))
                st.settle()
                scale_u(0)
                lo(S0["u"] + 2 * i + 2, 0)
                v = vtok[:, i, :]
                st.did(V.tensor_tensor(v, v, sgu_rows[:, 1, :, :].rearrange("p a b -> p (a b)"), ALU.mult))
                st.settle()
                V.tensor_tensor(v, v, sgu_rows[:, 2, :, :].rearrange("p a b -> p (a b)"), ALU.add).then_inc(v_ready, 1)
                scale_u(1)
            for j in range(7):
                n = S0["c"] + j
                lo(n + 1, (n + 1) % 2)
                dve.wait_ge(tile_done, CUM[n])
                V.tensor_tensor(cT[:, j, :], ps[:, 6 + j % 2, :], rstd[:, :], ALU.mult).then_inc(c_copied, 1)
                if j < 4:
                    add_square("cq", j, first=j == 0)
                elif j < 6:
                    add_square("ckv", j - 4, first=j == 4)
                if j == 4:
                    dve.wait_ge(v_ready, 4)
                    inverse_root("cq", QL, 0)
                    dve.wait_ge(c_copied, 4)
                    scale_split("cq", [(k, cT[:, k, :], gain("cq", k), rstdL) for k in range(KQ)], cqH, cqL)
            inverse_root("ckv", KVL, 0)
            scale_split("ckv", [(k, cT[:, KQ + k, :], gain("ckv", k), rstdL) for k in range(KKV)], ckvH, ckvL)
            for g in range(SGU_TILES):
                dve.wait_ge(mix_done, g + 1)
                if g < 2:
                    dve.wait_ge(act_lo, N_SC["sgu"])
                else:
                    dve.wait_ge(sgu_ready, g - 1)
                st.did(V.tensor_tensor(tmp[g % 2][:, :].rearrange("p (c t) -> p c t", c=NT),
                                       ps[:, 2 + g % 2, :].rearrange("p (c t) -> p c t", c=NT),
                                       sgu_rows[:, 0, g, :].unsqueeze(1).to_broadcast([P, NT, P]), ALU.add))
                st.settle()
                if g == 0:
                    dve.wait_ge(u_gelu, 8)
                V.tensor_tensor(mixT[:, 8 + g, :], mixT[:, 8 + g, :], tmp[g % 2][:, :], ALU.mult).then_inc(sgu_ready, 1)
                if g >= 1:
                    add_square("sgu", g - 1, first=g == 1)
            add_square("sgu", 7)
            inverse_root("sgu", 1024, 0)
            for g in range(SGU_TILES):
                V.scalar_tensor_tensor(mixT[:, 8 + g, :], mixT[:, 8 + g, :], gain("sgu", g), rstdB[:, :],
                                       ALU.mult, ALU.mult).then_inc(sgu_scaled, 1)
            dve.wait_ge(pos_loaded, 16)
            dve.wait_ge(perm_loaded, 32)
            dve.wait_ge(sgu_ready, 8)
            st.did(V.tensor_copy(tmp[0][:, :], krT[:, :].bitcast(I32)))
            st.settle()
            st.did(V.tensor_scalar(tmp[0][:, :], tmp[0][:, :], freq[:, 0:1], None, ALU.mult))
            st.settle()
            for dst, quarter in ((cosT, 0.25), (sinT, 0.0)):
                st.did(V.tensor_scalar(tmp[1][:, :], tmp[0][:, :], 1.0 / (2 * PI), quarter, ALU.mult, ALU.add))
                st.settle()
                st.did(V.tensor_scalar(tmp[1][:, :], tmp[1][:, :], ROUND, None, ALU.add))
                st.settle()
                st.did(V.tensor_scalar(tmp[1][:, :], tmp[1][:, :], ROUND, None, ALU.subtract))
                st.settle()
                src = tmp[0]
                for part in two_pi_parts():
                    st.did(V.scalar_tensor_tensor(dst[:, :], tmp[1][:, :], -part, src[:, :], ALU.mult, ALU.add))
                    st.settle()
                    src = dst
                st.did(V.tensor_scalar(dst[:, :], dst[:, :], quarter * 2 * PI, PI_BELOW, ALU.add, ALU.min))
                st.settle()
                V.tensor_scalar(dst[:, :], dst[:, :], -PI_BELOW, None, ALU.max).then_inc(angle_ready, 1)

            def rope(j, src, dst):
                st.did(V.tensor_tensor(tmp[0][:, :], src, cosT[:, :], ALU.mult))
                dve.wait_ge(swap_done, j + 1)
                st.did(V.tensor_tensor(tmp[1][:, :], ps[:, j % 2, :], sinT[:, :], ALU.mult))
                st.settle()
                V.tensor_tensor(dst, tmp[0][:, :], tmp[1][:, :], ALU.add).then_inc(rope_ready, 1)

            dve.wait_ge(trig_ready, 2)
            for s in range(3):
                lo(S0["uq"] + s + 1, (S0["uq"] + s + 1) % 2)
                if s == 0:
                    rope(0, cT[:, 6, :], krT[:, :])
            lo(S0["ukv"] + 1, (S0["ukv"] + 1) % 2)
            for j in range(4):
                dve.wait_ge(uq_copied, 9 + j)
                dve.wait_ge(rope_ready, 1 + j)
                rope(1 + j, qT[:, 8 + j, :], qT[:, 8 + j, :])
            lo(S0["out"], 0)
            ITEMS = HEADS * NT
            for n in range(ITEMS + 1):
                if n < ITEMS:
                    w = P * (n % NT + 1)
                    dve.wait_ge(score_done, n + 1)
                    st.did(V.reduce_max(smax[:, n:n + 1], ps[:, n % 3, 0:w], AX))
                    st.settle()
                    V.tensor_scalar(nbias[:, n:n + 1], smax[:, n:n + 1], -SCALE, None, ALU.mult).then_inc(nbias_ready, 1)
                if n >= 1:
                    m = n - 1
                    w = P * (m % NT + 1)
                    dve.wait_ge(exp_done, m + 1)
                    st.did(V.reciprocal(rinv[:, m:m + 1], rsum[:, m:m + 1]))
                    st.settle()
                    V.tensor_scalar(prob[m % 2][:, 0:w], prob[m % 2][:, 0:w], rinv[:, m:m + 1], None, ALU.mult).then_inc(p_ready, 1)
                if n >= NT + 4 and n % NT == 0 or n == ITEMS:
                    for h in ([n // NT - 2] if n < ITEMS else [HEADS - 2, HEADS - 1]):
                        dve.wait_ge(pv_done, NT * (h + 1))
                        V.tensor_copy(mixT[:, h, :], ps[:, 5 + h % 2, :]).then_inc(o_copied, 1)
                        if h >= 1:
                            add_square("attn", h - 1, first=h == 1)
            add_square("attn", HEADS - 1)

            def sgu_lo(g):
                dve.wait_ge(act_hi, N_SC["sgu"] + g + 1)
                V.tensor_tensor(aL[:, 8 + g, :], mixT[:, 8 + g, :], aH[:, 8 + g, :].bitcast(F), ALU.subtract).then_inc(act_lo, 1)

            mean_of("attn", 1024, 7)
            for g in range(4):
                sgu_lo(g)
            invert("attn")
            for g in range(4, 8):
                sgu_lo(g)
            scale_split("attn", [(k, mixT[:, k, :], gain("attn", k), rstd) for k in range(8)], aH, aL)
            dve.wait_ge(x_again, 64)

            def residual(i, j, last=False):
                if not last:
                    lo(S0["out"] + 2 * i + j + 1, (j + 1) % 2)
                dve.wait_ge(tile_done, CUM[S0["out"] + j] + 2 * i)
                V.tensor_tensor(hT[:, 2 * i + j, :], hT[:, 2 * i + j, :], ps[:, j, :], ALU.add).then_inc(h_mixed, 1)

            residual(0, 0)
            add_square("ffn", 0, first=True)
            residual(0, 1)
            add_square("ffn", 1)
            with dve.Fori(1, 7) as i:
                for j in range(2):
                    residual(i, j)
                    add_square("ffn", 2 * i + j, par=j)
            residual(7, 0)
            add_square("ffn", 14)
            lo(S0["out"] + 16, 0)
            for k in range(KD - 1):
                gain_lo("ffn", k)
            residual(7, 1, last=True)
            add_square("ffn", 15)
            gain_lo("ffn", KD - 1)

            def best_keys(h, b):
                def unit(s, t):
                    return ps[:, 2 + 2 * b + s, t * P:(t + 1) * P]

                units = [(s, t) for s in range(2) for t in range(NT)]
                dve.wait_ge(ps_done, 2 * h + 2)
                hold()
                for s, t in units:
                    st.did(V.max(top[:, s, t, 0:8], unit(s, t)))
                st.settle()
                hold()
                for s, t in units:
                    st.did(V.match_replace(rest[:, s * NT + t, :], top[:, s, t, 0:8], unit(s, t), -3e38))
                st.settle()
                hold()
                for s, t in units:
                    st.did(V.max(top[:, s, t, 8:16], rest[:, s * NT + t, :]))
                for s, t in units:
                    st.did(V.max_index(top_at[:, s, t, 0:8], top[:, s, t, 0:8], unit(s, t)))
                st.settle()
                hold()
                for s, t in units[:-1]:
                    st.did(V.max_index(top_at[:, s, t, 8:16], top[:, s, t, 8:16], rest[:, s * NT + t, :]))
                s, t = units[-1]
                V.max_index(top_at[:, s, t, 8:16], top[:, s, t, 8:16], rest[:, s * NT + t, :]).then_inc(tops_done, 1)

            def best_pairs(h):
                for t in range(NT):
                    st.did(V.tensor_tensor(cand[:, t, :].rearrange("p (a b) -> p a b", a=TOPK),
                                           top[:, 0, t, :].unsqueeze(2).to_broadcast([P, TOPK, TOPK]),
                                           top[:, 1, t, :].unsqueeze(1).to_broadcast([P, TOPK, TOPK]), ALU.add))
                dve.wait_ge(tops_done, h + 1)
                st.did(V.tensor_copy(top_atf[:, :, :, :], top_at[:, :, :, :]))
                st.settle()
                hold()
                for t in range(NT):
                    st.did(V.max(best[:, t, 0:8], cand[:, t, :]))
                st.settle()
                hold()
                for t in range(NT):
                    st.did(V.match_replace(cand_rest[:, t, :], best[:, t, 0:8], cand[:, t, :], -3e38))
                st.settle()
                hold()
                for t in range(NT):
                    st.did(V.max(best[:, t, 8:16], cand_rest[:, t, :]))
                for t in range(NT):
                    st.did(V.max_index(best_at[:, t, 0:8], best[:, t, 0:8], cand[:, t, :]))
                st.settle()
                hold()
                for t in range(NT):
                    st.did(V.max_index(best_at[:, t, 8:16], best[:, t, 8:16], cand_rest[:, t, :]))
                V.tensor_tensor(gate_e[:, :, :], best[:, :, :], best[:, :, 0:1].to_broadcast([P, NT, TOPK]),
                                ALU.subtract).then_inc(gate_sub, 1)
                st.settle()
                st.did(V.tensor_single_scalar(best_k[:, 0, :, :], best_at[:, :, :], 4, ALU.logical_shift_right))
                st.did(V.tensor_single_scalar(best_k[:, 1, :, :], best_at[:, :, :], 15, ALU.bitwise_and))
                st.settle()
                st.did(V.tensor_copy(best_kf[:, :, :, :], best_k[:, :, :, :]))
                st.settle()
                for s in range(2):
                    m3 = match[:, :, :, :].rearrange("p t a b -> p (t a) b")
                    st.did(V.tensor_tensor(m3, iota[:, 0:TOPK].unsqueeze(1).to_broadcast([P, NT * TOPK, TOPK]),
                                           best_kf[:, s, :, :].rearrange("p t k -> p (t k)").unsqueeze(2)
                                           .to_broadcast([P, NT * TOPK, TOPK]), ALU.is_equal))
                    st.settle()
                    st.did(V.tensor_tensor(match[:, :, :, :], match[:, :, :, :],
                                           top_atf[:, s, :, :].unsqueeze(2).to_broadcast([P, NT, TOPK, TOPK]), ALU.mult))
                    st.settle()
                    st.did(V.tensor_reduce(route[:, 1 + s, :, bass.ts(h, TOPK)], match[:, :, :, :], AX, ALU.add))
                    st.settle()
                dve.wait_ge(gate_exp, h + 1)
                st.did(V.reduce_sum(gate_sum[:, :], gate_e[:, :, :], AX))
                st.settle()
                st.did(V.reciprocal(gate_inv[:, :], gate_sum[:, :]))
                st.settle()
                V.tensor_tensor(route[:, 0, :, bass.ts(h, TOPK)], gate_e[:, :, :],
                                gate_inv[:, :].unsqueeze(2).to_broadcast([P, NT, TOPK]), ALU.mult).then_inc(routed, 1)
                dve.wait_ge(routed, h + 1)

            KEY_STEPS, PAIR_STEPS = 39, 36
            lo(S0["pq"] + 1, 1)
            inverse_root("ffn", D, 7)
            lo(S0["pq"] + 2, 0)
            token_rms(2, 7)
            with st.loop(3, 2 * (KEY_STEPS + PAIR_STEPS)) as i:
                for b in range(2):
                    h = 2 * i + b
                    lo(S0["pq"] + 2 * h + 3, 1)
                    best_keys(h, b)
                    lo(S0["pq"] + 2 * h + 4, 0)
                    best_pairs(h)
            lo(S0["pq"] + 15, 1)
            best_keys(6, 0)
            lo(S0["pq"] + 16, 0)
            best_pairs(6)

            n0 = S0["peer"]

            def scale_chunk(uc, b, tiles, pre=True):
                dve.wait_ge(tile_done, tiles)
                if pre:
                    if not (isinstance(uc, int) and uc < 2):
                        dve.wait_ge(pre_stored[b], (uc - b) * 8)
                else:
                    dve.wait_ge(act_wlo, uc - 1)
                V.tensor_tensor(ut[b][:, :], ps[:, b, :], rstd[:, :], ALU.mult).then_inc(chunk_scaled, 1)

            def pre_lo(u):
                lo(n0 + u + 1, (u + 1) % 2)

            pre_lo(0)
            best_keys(7, 1)
            scale_chunk(0, 0, CUM[n0])
            pre_lo(1)
            best_pairs(7)
            scale_chunk(1, 1, CUM[n0 + 1])
            pre_lo(2)
            scale_chunk(2, 0, CUM[n0 + 2])
            pre_lo(3)

            dve.wait_ge(hk_ready, 3)

            def one_hots(t, qs):
                for q in qs:
                    u = 8 * t + q
                    b = q % 2
                    if not (isinstance(u, int) and u < 2):
                        dve.wait_ge(gquad_done, u - 1)
                    V.tensor_tensor(oh1[:, b, :, :], iota[:, :].unsqueeze(1).to_broadcast([P, 4, P]),
                                    hk[:, 1, bass.ts(u, 4)].unsqueeze(2).to_broadcast([P, 4, P]), ALU.is_equal)
                    for k in range(4):
                        ins = V.tensor_scalar(oh2[:, b, k, :], iota[:, :], hk[:, 2, bass.ds(4 * u + k, 1)],
                                              hk[:, 0, bass.ds(4 * u + k, 1)], ALU.is_equal, ALU.mult)
                    ins.then_inc(onehot_ready, 1)

            def gate_block(t, b, i):
                one_hots(t, range(2))
                scale_chunk(3 + t, 1 - b, CUM[n0 + 3 + b] + 2 * i)
                one_hots(t, range(2, 4))
                lo(n0 + 5 + t, 1 - b)
                one_hots(t, range(4, 8))

            for b in range(2):
                gate_block(b, b, 0)
            with dve.Fori(1, NTB // 2) as i:
                for b in range(2):
                    gate_block(2 * i + b, b, i)

            def apply_gates(uc, j, b, src):
                t3 = src[:, :].rearrange("p (b t) -> p b t", b=NTB)
                V.tensor_tensor(t3, t3, gtile[b][:, :, j, :], ALU.mult).then_inc(act_gated, 1)

            def weight_lo(uc, j, b, src):
                dve.wait_ge(act_whi, uc + 1)
                V.tensor_tensor(actL[b][:, j, :], src[:, :], actH[b][:, j, :].bitcast(F), ALU.subtract).then_inc(act_wlo, 1)

            def accumulate(q, tiles, done):
                for m in range(4):
                    dve.wait_ge(tile_done, tiles + m + 1)
                    if m == 0 and q == 0 and not (isinstance(done, int) and done <= 0):
                        dve.wait_ge(h_acc, done)
                    h = hT[:, 4 * q + m, :]
                    V.tensor_tensor(h, h, ps[:, 2 + m, :], ALU.add).then_inc(h_acc, 1)

            def prepared(c, b):
                dve.wait_ge(pre_loaded[c % 2], 16 * (c // 2 + 1))
                if c % GROUP == 0:
                    g = c // GROUP
                    dve.wait_ge(gates_loaded[g % 2], 16 * (g // 2 + 1))
                apply_gates(c, c % GROUP, b, tmp[c % 2])

            for u in range(20, NPRE):
                scale_chunk(u - 1, (u - 1) % 2, CUM[n0 + u - 1])
                pre_lo(u)
                if u >= 22:
                    c = 2 * (u - 22)
                    prepared(c, 0)
                    prepared(c + 1, 0)
                    weight_lo(c, c, 0, tmp[0])
                    weight_lo(c + 1, c + 1, 0, tmp[1])
            scale_chunk(NPRE - 1, 1, CUM[n0 + NPRE - 1])
            for g in range(1, PRE_GROUPS):
                for j in range(GROUP):
                    n = n0 + NPRE + GROUP * (g - 1) + j
                    lo(n + 1, (j + 1) % 2)
                    prepared(GROUP * g + j, g % 2)
                    weight_lo(GROUP * g + j, j, g % 2, tmp[j % 2])
                    accumulate(j, CUM[n - 1], 16 * (g - 1))

            s0 = n0 + 2 * NPRE - GROUP
            with dve.Fori(0, (NGROUPS - PRE_GROUPS) // 2) as i:
                for b in range(2):
                    g = 2 * i + PRE_GROUPS + b
                    for j in range(GROUP):
                        m = s0 + 8 * b + 2 * j
                        c = GROUP * g + j
                        lo(m + 1 + 16 * i, 1)
                        scale_chunk(c, j % 2, CUM[m] + 40 * i, pre=False)
                        if j == 0:
                            dve.wait_ge(gates_loaded[b], 8 * (g - b) + 16)
                        dve.wait_ge(gelu_done, c + 1)
                        apply_gates(c, j, b, ut[j % 2])
                        lo(m + 2 + 16 * i, 0)
                        weight_lo(c, j, b, ut[j % 2])
                        accumulate(j, CUM[m] + 40 * i, 16 * (g - 1))
            last = n0 + 2 * KEYS - GROUP
            for j in range(GROUP):
                lo(last + j + 1, (j + 1) % 2)
                if j == 0:
                    dve.wait_ge(p_hi, 1)
                    V.tensor_tensor(pL[:, :, :], pRaw[:, :, :], pH[:, :, :].bitcast(F), ALU.subtract).then_inc(p_lo, 1)
                accumulate(j, CUM[last + j - 1], 16 * (NGROUPS - 1))
                for m in range(4):
                    add_square("ple", 4 * j + m, first=j + m == 0)
                    gain_lo("ple", 4 * j + m)
            lo(S0["proj"] + 1, 1)
            inverse_root("ple", D, 7)
            lo(S0["gate"], 0)
            dve.wait_ge(proj_copied, 16)

            def gated(i, j, last=False, first=False):
                if not last:
                    lo(S0["gate"] + 2 * i + j + 1, (j + 1) % 2)
                m = 2 * i + j
                dve.wait_ge(tile_done, CUM[S0["gate"] + j] + 2 * i)
                if not first and not (isinstance(i, int) and i == 0):
                    dve.wait_ge(h_gated, m - 1)
                V.tensor_tensor(tmp[j][:, :], ps[:, j, :], rstd[:, :], ALU.mult).then_inc(g_scaled, 1)
                dve.wait_ge(sig_done, m + 1)
                st.did(V.tensor_tensor(tmp[j][:, :], tmp[j][:, :], projT[:, m, :], ALU.mult))
                st.settle()
                V.tensor_tensor(hT[:, m, :], hT[:, m, :], tmp[j][:, :], ALU.add).then_inc(h_gated, 1)
                add_square("final", m, first=first, par=j)

            for j in range(2):
                gated(0, j, first=j == 0)
            with st.loop(6, 2) as i:
                for j in range(2):
                    gated(i + 1, j)
            for j in range(2):
                gated(7, j, last=j == 1)
            inverse_root("final", D, 7)
            for k in range(KD):
                V.scalar_tensor_tensor(hT[:, k, :], hT[:, k, :], gain("final", k), rstd[:, :], ALU.mult, ALU.mult).then_inc(out_ready, 1)

        @block.tensor
        def _(pe):
            mm = nc.tensor.matmul

            def three(out, wh, wl, xh, xl, start, stop):
                mm(out, wh, xh, start=start, stop=False)
                mm(out, wh, xl, start=False, stop=False)
                return mm(out, wl, xh, start=False, stop=stop)

            def norm_sum(name, bank):
                pe.wait_ge(sq_added, N_SQ[name] + {"cq": 4, "ckv": 2, "sgu": 8, "attn": 8}.get(name, 16))
                mm(ps[:, bank, :], ones[:, :], ssum[:, :], start=True, stop=True).then_inc(sum_done, 1)

            def token_rms(n, bank):
                pe.wait_ge(rstd_ready, n)
                for t in range(NT):
                    ins = mm(ps[:, bank, t:t + 1], rstd[:, t * P:(t + 1) * P], ident[:, 0:1], start=True, stop=True)
                ins.then_inc(tok_done, 1)

            def tile(n, parity, bank, order=range(KD), waits=None, after=None, every=1):
                pe.wait_ge(lo_ready, n + 1)
                for j, k in enumerate(order):
                    if waits is not None:
                        pe.wait_ge(act_lo, waits + j + 1)
                    w = slice(k * P, (k + 1) * P)
                    ins = three(ps[:, bank, :], wH[parity][:, w], wL[parity][:, w], aH[:, k, :], aL[:, k, :],
                                j == 0, j == KD - 1)
                    if after is not None and j % every == every - 1 and j < KD - 1:
                        after(ins, j // every)
                ins.then_inc(tile_done, 1)
                if after is not None and every > 1:
                    after(ins, KD // every - 1)


            def v_block(cb, waits=None):
                for s in range(4):
                    pe.wait_ge(lo_ready, S0["v"] + 4 * cb + s + 1)
                    for tt in range(NT):
                        if s == 0 and waits is None:
                            pe.wait_ge(v_gelu, tt + 1)
                        for k4 in range(4):
                            k = 4 * s + k4
                            if waits is not None and tt == 0:
                                pe.wait_ge(act_lo, waits + k + 1)
                            w = slice(k4 * 512, (k4 + 1) * 512)
                            t = slice(tt * P, (tt + 1) * P)
                            ins = three(ps[:, tt, :], aH[:, k, t], aL[:, k, t], wH[s % 2][:, w], wL[s % 2][:, w], k == 0, k == KD - 1)
                        if s == 3 or tt == NT - 1:
                            ins.then_inc(tile_done, 1)
                    if waits is not None and s == 1:
                        pe.wait_ge(consts_ready, 3)
                        norm_sum("mix", 7)
                    if waits is not None and s == 2:
                        token_rms(NORMS["mix"] + 1, 7)

            v_block(0, waits=0)
            v_block(1)
            for j in range(2):
                tile(S0["u"] + j, j, 4 + j)
            with pe.Fori(1, 4) as i:
                for j in range(2):
                    pe.wait_ge(u_scaled, 2 * i + j - 1)
                    tile(S0["u"] + 2 * i + j, j, 4 + j)
            for j in range(7):
                n = S0["c"] + j
                if j >= 2:
                    pe.wait_ge(c_copied, j - 1)
                tile(n, n % 2, 6 + j % 2)
                if j == 4:
                    pe.wait_ge(v_gelu, 8)
                    norm_sum("cq", 0)
            pe.wait_ge(mean_ready, NORMS["cq"] + 1)
            norm_sum("ckv", 0)
            pe.wait_ge(v_ready, 4)
            for g in range(SGU_TILES):
                if g >= 2:
                    pe.wait_ge(sgu_ready, g - 1)
                for c in range(NT):
                    t = slice(c * P, (c + 1) * P)
                    ins = mm(ps[:, 2 + g % 2, t], vtok[:, c, g * P:(g + 1) * P], wsT[:, g, :], start=True, stop=True)
                ins.then_inc(mix_done, 1)
            pe.wait_ge(mean_ready, NORMS["ckv"] + 1)
            norm_sum("sgu", 0)
            pe.wait_ge(act_lo, N_SC["cq"] + KQ)
            pe.wait_ge(u_scaled, 8)
            for s in range(3):
                n = S0["uq"] + s
                pe.wait_ge(lo_ready, n + 1)
                for m in range(4):
                    t = 4 * s + m
                    if t >= 4:
                        pe.wait_ge(uq_copied, t - 3)
                    elif t in (2, 3):
                        pe.wait_ge(c_copied, 7)
                    for k in range(KQ):
                        w = slice(k * 512 + m * P, k * 512 + (m + 1) * P)
                        ins = three(ps[:, 4 + t % 4, :], wH[n % 2][:, w], wL[n % 2][:, w], cqH[:, k, :], cqL[:, k, :], k == 0, k == KQ - 1)
                    ins.then_inc(tile_done, 1)
                if s == 1:
                    pe.wait_ge(mean_ready, NORMS["sgu"] + 1)
                    pe.wait_ge(perm_loaded, 32)
                    mm(ps[:, 0, :], perm[:, :], cT[:, 6, :], start=True, stop=True).then_inc(swap_done, 1)
            for s in range(2):
                n = S0["ukv"] + s
                pe.wait_ge(lo_ready, n + 1)
                if s == 0:
                    pe.wait_ge(act_lo, N_SC["ckv"] + KKV)
                for m in range(8):
                    if m < 4 and s == 0:
                        pe.wait_ge(uq_copied, 9 + m)
                    else:
                        pe.wait_ge(kv_copied, 8 * s + m - 3)
                    for k in range(KKV):
                        if s == 0:
                            w = slice(k * 1024 + m * P, k * 1024 + (m + 1) * P)
                            ins = three(ps[:, 4 + m % 4, :], wH[n % 2][:, w], wL[n % 2][:, w], ckvH[:, k, :], ckvL[:, k, :], k == 0, k == 1)
                        else:
                            w = slice(k * 1024 + (m // 4) * 512, k * 1024 + (m // 4) * 512 + 512)
                            t = slice((m % 4) * P, (m % 4 + 1) * P)
                            ins = three(ps[:, 4 + m % 4, :], ckvH[:, k, t], ckvL[:, k, t], wH[n % 2][:, w], wL[n % 2][:, w], k == 0, k == 1)
                    ins.then_inc(tile_done, 1)
                    if s == 0 and m in (1, 3, 5, 7):
                        j = m // 2
                        pe.wait_ge(uq_copied, 9 + j)
                        if j >= 1:
                            pe.wait_ge(rope_ready, j)
                        mm(ps[:, (1 + j) % 2, :], perm[:, :], qT[:, 8 + j, :], start=True, stop=True).then_inc(swap_done, 1)
            pe.wait_ge(kv_copied, 16)
            pe.wait_ge(rope_ready, 5)
            ITEMS = HEADS * NT
            for n in range(ITEMS + 3):
                if n < ITEMS:
                    h, qt = divmod(n, NT)
                    w = P * (qt + 1)
                    t = slice(qt * P, w)
                    if n >= 3:
                        pe.wait_ge(exp_done, n - 2)
                    r = slice(64 * (h % 2), 64 * (h % 2) + 64)
                    o = ps[:, n % 3, 0:w]
                    mm(o, qT[:, h, t], kT[:, h, 0:w], start=True, stop=False)
                    mm(o, qT[r, 8 + h // 2, t], krT[r, 0:w], start=False, stop=False)
                    mm(ps[:, n % 3, t], identR[:, :], causalR[:, :], start=False, stop=True).then_inc(score_done, 1)
                m = n - 2
                if 0 <= m < ITEMS:
                    pe.wait_ge(p_ready, m + 1)
                    if m >= 2:
                        pe.wait_ge(pt_copied, m - 1)
                    elif m == 0:
                        pe.wait_ge(kv_copied, 16)
                    for j in range(m % NT + 1):
                        s = slice(j * P, (j + 1) * P)
                        ins = nc.tensor.transpose(ps[:, 3 + m % 2, s], prob[m % 2][:, s], ident[:, :])
                    ins.then_inc(pt_done, 1)
                m = n - 3
                if 0 <= m < ITEMS:
                    h, qt = divmod(m, NT)
                    pe.wait_ge(pt_copied, m + 1)
                    if qt == 0 and h >= 2:
                        pe.wait_ge(o_copied, h - 1)
                    for j in range(qt + 1):
                        s = slice(j * P, (j + 1) * P)
                        ins = mm(ps[:, 5 + h % 2, qt * P:(qt + 1) * P], vA[:, j, h * P:(h + 1) * P], probT[m % 2][:, s],
                                 start=j == 0, stop=j == qt)
                    ins.then_inc(pv_done, 1)
            norm_sum("attn", 7)
            tile(S0["out"], 0, 0, order=OUT_ORDER, waits=N_SC["sgu"])
            tile(S0["out"] + 1, 1, 1)
            with pe.Fori(1, 7) as i:
                for j in range(2):
                    pe.wait_ge(h_mixed, 2 * i + j - 1)
                    tile(S0["out"] + 2 * i + j, j, j)
            pe.wait_ge(h_mixed, 13)
            tile(S0["out"] + 14, 0, 0)
            pe.wait_ge(h_mixed, 14)
            tile(S0["out"] + 15, 1, 1, after=lambda ins, j: ins.then_inc(a_read, 1))

            def scores(h, b):
                for s in range(2):
                    pe.wait_ge(pq_copied, 2 * h + s + 1)
                    for t in range(NT):
                        ts = slice(t * P, (t + 1) * P)
                        ins = mm(ps[:, 2 + 2 * b + s, ts], pqT[b][:, s, ts], keys[:, h, s, :], start=True, stop=True)
                    ins.then_inc(ps_done, 1)

            def peer_queries(i, waits=None):
                for b in range(2):
                    for s in range(2):
                        j = 2 * b + s
                        if waits is None or j >= 2:
                            pe.wait_ge(pq_copied, 4 * i + j - 1)
                        elif j == 0:
                            pe.wait_ge(h_mixed, 15)
                        else:
                            pe.wait_ge(h_mixed, 16)
                        tile(S0["pq"] + 4 * i + j, s, s, waits=waits if j == 0 else None)
                        if waits is not None and j == 0:
                            norm_sum("ffn", 7)
                        if waits is not None and j == 1:
                            token_rms(NORMS["ffn"] + 1, 7)
                    if waits is None:
                        pe.wait_ge(tops_done, 2 * i + b - 1)
                    elif b == 0:
                        pe.wait_ge(keys_loaded, 16)
                    scores(2 * i + b, b)

            peer_queries(0, waits=N_SC["ffn"])
            with pe.Fori(1, 4) as i:
                peer_queries(i)
            n0 = S0["peer"]

            def u_slot(n, parity, uc, j, first=False, **more):
                if not first:
                    pe.wait_ge(chunk_scaled, uc - 1)
                tile(n, parity, j % 2, **more)

            pe.wait_ge(pq_copied, 16)
            for j in range(3):
                u_slot(n0 + j, j % 2, j, j, first=j < 2)
            pe.wait_ge(routed, HEADS)
            for r in range(3):
                for t in range(NT):
                    ins = nc.tensor.transpose(ps[:, 2 + r, t * P:(t + 1) * P], route[:, r, t, :], ident[:, :])
                ins.then_inc(hkT_done, 1)
            u_slot(n0 + 3, 1, 3, 3)

            def gate_block(t, b, first=False):
                def quad(_, q):
                    u = 8 * t + q
                    if not (first and q < 4):
                        pe.wait_ge(gquad_copied, u - 3)
                    pe.wait_ge(onehot_ready, u + 1)
                    for k in range(4):
                        ins = mm(ps[:, 4 + q % 4, k * P:(k + 1) * P], oh1[:, q % 2, k, :], oh2[:, q % 2, k, :], start=True, stop=True)
                    ins.then_inc(gquad_done, 1)

                u_slot(n0 + 4 + t, b, 4 + t, b, after=quad, every=2)

            for b in range(2):
                gate_block(b, b, first=b == 0)
            with pe.Fori(1, NTB // 2) as i:
                for b in range(2):
                    gate_block(2 * i + b, b)
            for u in range(20, NPRE):
                u_slot(n0 + u, u % 2, u, u)

            def v_slot(n, parity, g, q, b, first=False):
                pe.wait_ge(lo_ready, n + 1)
                if q == 0:
                    pe.wait_ge(act_wlo, GROUP * (g + 1))
                for m in range(4):
                    if not (first and q == 0):
                        pe.wait_ge(h_acc, 16 * g + 4 * q + m - 3)
                    for c in range(GROUP):
                        w = slice(c * 512 + m * P, c * 512 + (m + 1) * P)
                        ins = three(ps[:, 2 + m, :], wH[parity][:, w], wL[parity][:, w], actH[b][:, c, :], actL[b][:, c, :], c == 0, c == GROUP - 1)
                    ins.then_inc(tile_done, 1)

            pe.wait_ge(gquad_copied, QUADS)
            for g in range(PRE_GROUPS - 1):
                for j in range(GROUP):
                    v_slot(n0 + NPRE + GROUP * g + j, j % 2, g, j, g % 2, first=g == 0)
            s0 = n0 + 2 * NPRE - GROUP
            with pe.Fori(0, (NGROUPS - PRE_GROUPS) // 2) as i:
                for b in range(2):
                    g = 2 * i + PRE_GROUPS + b
                    for j in range(GROUP):
                        n = s0 + 16 * i + 8 * b + 2 * j
                        u_slot(n, 0, GROUP * g + j, j)
                        v_slot(n + 1, 1, g - 1, j, 1 - b)
            for j in range(GROUP):
                v_slot(n0 + 2 * KEYS - GROUP + j, j % 2, NGROUPS - 1, j, 1)
            pe.wait_ge(p_lo, 1)
            for s in range(2):
                n = S0["proj"] + s
                pe.wait_ge(lo_ready, n + 1)
                for m in range(8):
                    if s == 0 and m < 4:
                        pe.wait_ge(h_acc, 16 * NGROUPS - 3 + m)
                    else:
                        pe.wait_ge(proj_copied, 8 * s + m - 3)
                    for k in range(2):
                        w = slice(k * 1024 + m * P, k * 1024 + (m + 1) * P)
                        ins = three(ps[:, 2 + m % 4, :], wH[s][:, w], wL[s][:, w], pH[:, k, :], pL[:, k, :], k == 0, k == 1)
                    ins.then_inc(tile_done, 1)
                if s == 0:
                    norm_sum("ple", 7)
            pe.wait_ge(act_lo, N_SC["ple"] + KD)
            tile(S0["gate"], 0, 0)
            tile(S0["gate"] + 1, 1, 1)
            with pe.Fori(1, 8) as i:
                for j in range(2):
                    pe.wait_ge(g_scaled, 2 * i + j - 1)
                    tile(S0["gate"] + 2 * i + j, j, j)
            norm_sum("final", 7)


OUT_ORDER = list(range(8, 16)) + list(range(8))


def kernel(**inputs):
    import numpy as np
    import concourse.bacc as bacc
    from concourse.bass_utils import run_bass_kernel_spmd

    v = {k: np.asarray(x) for k, x in inputs.items()}
    w_in = v["w_in"][0]
    off_kr, off_u, off_v = QL + KVL, QL + KVL + ROPE_D, QL + KVL + ROPE_D + 1024

    def tiles(w):
        k, m = w.shape
        return w.reshape(k // P, P, m // P, P).transpose(2, 1, 0, 3).reshape(m // P, P, k)

    def wide(w, cols):
        k, m = w.shape
        return w.reshape(k // P, P, m // cols, cols).transpose(2, 1, 0, 3).reshape(m // cols, P, k // P * cols)

    uq = v["w_uq"][0].reshape(QL, HEADS, 128 + ROPE_D)
    ukv = v["w_ukv"][0].reshape(KVL, HEADS, 256)
    kr = w_in[:, off_kr:off_u]
    cols = lambda g: g.reshape(-1, P).T
    arrays = {
        "x": v["x"][0].T.reshape(KD, P, T).transpose(1, 0, 2),
        "p": v["p"][0, 0].T.reshape(2, P, T).transpose(1, 0, 2),
        "pos": v["positions"].reshape(1, T),
        "gains": np.concatenate([cols(v[k].reshape(-1)) for k in ("g_mix", "g_ffn", "g_ple", "g_final", "g_out_attn", "g_out_sgu", "g_cq", "g_ckv")], axis=1),
        "rows": np.concatenate([v[k].reshape(1, 1024) for k in ("b_sgu", "g_ln_sgu", "b_ln_sgu")], axis=1),
        "ws": v["w_sgu"][0].transpose(2, 0, 1),
        "keys": np.stack([v["peer_k1"][0], v["peer_k2"][0]], axis=1).transpose(3, 0, 1, 2),
        "s_v": w_in[:, off_v:].reshape(4, 4, P, 2, 512).transpose(3, 0, 2, 1, 4).reshape(8, P, 2048),
        "s_u": tiles(w_in[:, off_u:off_v]),
        "s_c": tiles(np.concatenate([w_in[:, :off_kr], kr, kr], axis=1)),
        "s_uq": wide(np.concatenate([uq[:, :, :128].reshape(QL, -1), uq[:, :, 128:].reshape(QL, -1)], axis=1), 512),
        "s_ukv": wide(np.concatenate([ukv[:, :, :128].reshape(KVL, -1), ukv[:, :, 128:].reshape(KVL, -1)], axis=1), 1024),
        "s_out": tiles(v["w_out"][0]),
        "s_pq": tiles(v["w_peer_q"][0]),
        "s_pu": v["peer_u"][0].reshape(KEYS, KEYS, KD, P).transpose(1, 3, 2, 0).reshape(KEYS, P, 2048),
        "s_pv": v["peer_v"][0].reshape(KEYS, NGROUPS, GROUP, 4, 512).transpose(1, 3, 0, 2, 4).reshape(KEYS, P, 2048),
        "s_proj": wide(v["w_ple_proj"][0], 1024),
        "s_gate": tiles(v["w_ple_gate"][0]),
    }
    half = ROPE_D // 2
    consts = np.zeros((P, 386), np.float32)
    consts[:, 0:128] = np.eye(P, dtype=np.float32)
    consts[:, 128:256] = np.arange(P, dtype=np.float32)[None, :]
    for o in range(P):
        if o % ROPE_D < half:
            consts[o + half, 256 + o] = -1.0
        else:
            consts[o - half, 256 + o] = 1.0
    exponent = -np.arange(half, dtype=np.float32) / np.float32(half)
    consts[:, 384:386] = np.tile(np.power(np.float32(10000.0), exponent).astype(np.float32), 4)[:, None]
    arrays["consts"] = consts
    arrays = {k: np.ascontiguousarray(x) for k, x in arrays.items()}

    nc = bacc.Bacc("TRN2", target_bir_lowering=False, num_devices=1)
    aps = {k: nc.dram_tensor(k, x.shape, mybir.dt.from_np(x.dtype), kind="ExternalInput").ap() for k, x in arrays.items()}
    stream = {k[2:]: x for k, x in aps.items() if k.startswith("s_")}
    gates = nc.dram_tensor("gates", (NTB, KEYS, KEYS, TB), mybir.dt.float32, kind="Internal").ap()
    out = nc.dram_tensor("out", (P, KD, T), mybir.dt.float32, kind="ExternalOutput").ap()
    pre = nc.dram_tensor("pre", (NPRE, P, T), mybir.dt.float32, kind="Internal").ap()
    trunk_layer(nc, aps, stream, out, gates, pre)
    r = run_bass_kernel_spmd(nc, [arrays], core_ids=[0])
    return r.results[0]["out"].transpose(1, 0, 2).reshape(D, T).T.reshape(1, T, D)
```

```python
import math

import concourse.bass as bass
from concourse import mybir
from contextlib import ExitStack, contextmanager

P = 128
T = 512
NT = T // P
D = 2048
KD = D // P
HEADS = 8
ROPE_D = 64
QL, KVL = 512, 256
KQ, KKV = QL // P, KVL // P
SGU_TILES = 8
TOPK = 16
KEYS = 128
EPS = 1e-6
GROUP = 4
NGROUPS = KEYS // GROUP
TB = 32
NTB = T // TB
QUADS = T // 4
PRE_GROUPS = 14
NPRE = PRE_GROUPS * GROUP
BEATS = T // 16
Q_CHUNKS = 2 * HEADS
GATES_AT = Q_CHUNKS + 3
SCALE = float(128 + ROPE_D) ** -0.5
PI = math.pi
PI_BELOW = 3.1415925
def two_pi_parts():
    parts, left = [], 2 * PI
    for _ in range(3):
        scale = 2.0 ** (8 - math.frexp(left)[1])
        parts.append(math.floor(left * scale) / scale)
        left -= parts[-1]
    return parts + [left]


ROUND = 12582912.0

PEER_SLOTS = [1] * (NPRE - Q_CHUNKS) + [4] * (NPRE - GROUP) + [1, 4] * (KEYS - NPRE) + [4] * GROUP
STREAM = [("v", [1, 1, 1, 4] * 2), ("c", [1] * 7), ("u", [1] * 8), ("uq", [4] * 3), ("ukv", [8] * 2),
          ("out", [1] * 16), ("pq", [1] * 4 * HEADS), ("peer", PEER_SLOTS), ("proj", [8] * 2), ("gate", [1] * 14 + [2] * 2)]
S0 = {}
CUM = {-2: 0, -1: 0}
_n = 0
for _name, _marks in STREAM:
    S0[_name] = _n
    for _m in _marks:
        CUM[_n] = CUM[_n - 1] + _m
        _n += 1
NSLOTS = _n

GAINS = {}
_c = 0
for _name, _k in (("mix", KD), ("ffn", KD), ("ple", KD), ("final", KD), ("attn", 8), ("sgu", 8), ("cq", KQ), ("ckv", KKV)):
    GAINS[_name] = _c
    _c += _k
NGAINS = _c


class Steps:

    def __init__(self, eng, sem):
        self.eng, self.sem, self.base, self.k = eng, sem, 0, 0

    def did(self, ins):
        ins.then_inc(self.sem, 1)
        self.k += 1

    def settle(self):
        self.eng.wait_ge(self.sem, self.base + self.k)

    @contextmanager
    def loop(self, count, per):
        start = self.base + self.k
        with self.eng.Fori(0, count) as i:
            self.base, self.k = start + i * per, 0
            yield i
            assert self.k == per, (self.k, per)
        self.base, self.k = start + count * per, 0


def trunk_layer(nc, a, stream, out, gates_dram, pre_dram):
    F, R, U32, I32 = mybir.dt.float32, mybir.dt.float32r, mybir.dt.uint32, mybir.dt.int32
    ACT = mybir.ActivationFunctionType
    ALU = mybir.AluOpType
    AX = mybir.AxisListType.X

    base = (nc.sbuf_base + 31) // 32 * 32
    KB = 1024

    def at(name, shape, dt, offset):
        return nc.alloc_sbuf_tensor_at(name, [P] + shape, dt, offset=base + offset)

    H0, A0, RING0, W0, M0, C0 = 0, 32 * KB, 96 * KB, 144 * KB, 176 * KB, 192 * KB
    hT = at("hT", [KD, T], F, H0)
    vtok = at("vtok", [NT, 1024], F, H0)
    cT = at("cT", [7, T], F, H0 + 16 * KB)
    perm = at("perm", [P], F, H0 + 30 * KB)
    ln_stats = at("ln_stats", [8, 6], F, H0 + 30 * KB + 512)
    ln_mv = at("ln_mv", [8, 2], F, H0 + 30 * KB + 704)
    ln_rstd = at("ln_rstd", [8], F, H0 + 30 * KB + 768)
    freq = at("freq", [2], F, H0 + 30 * KB + 800)
    aH = at("aH", [KD, T], R, A0)
    aL = at("aL", [KD, T], R, A0 + 32 * KB)
    qT = at("qT", [12, T], F, A0)
    kT = at("kT", [HEADS, T], F, A0 + 24 * KB)
    vA = at("vA", [NT, 1024], F, A0 + 40 * KB)
    ckvH = at("ckvH", [KKV, T], R, A0 + 56 * KB)
    ckvL = at("ckvL", [KKV, T], R, A0 + 60 * KB)
    raw = [at(f"raw{i}", [2048], F, RING0 + 8 * KB * i) for i in range(2)]
    wH = [at(f"wH{i}", [2048], R, RING0 + (16 + 8 * i) * KB) for i in range(2)]
    wL = [at(f"wL{i}", [2048], R, RING0 + (32 + 8 * i) * KB) for i in range(2)]
    mixT = at("mixT", [KD, T], F, W0)
    cqH = at("cqH", [KQ, T], R, W0)
    cqL = at("cqL", [KQ, T], R, W0 + 8 * KB)
    rstdL = at("rstdL", [T], F, W0)
    pqT = [at(f"pqT{i}", [2, T], F, W0 + 4 * KB * i) for i in range(2)]
    keys = at("keys", [HEADS, 2, KEYS], F, W0 + 8 * KB)
    gstage = [at(f"gstage{i}", [KEYS, TB], F, W0 + 16 * KB * i) for i in range(2)]
    actH = [at(f"actH{i}", [GROUP, T], R, W0 + 16 * KB * i) for i in range(2)]
    actL = [at(f"actL{i}", [GROUP, T], R, W0 + 16 * KB * i + 8 * KB) for i in range(2)]
    projT = at("projT", [KD, T], F, W0)
    sgu_rows = at("sgu_rows", [3, 8, P], F, M0)
    wsT = at("wsT", [8, P], F, M0 + 12 * KB)
    cosT = at("cosT", [T], F, M0 + 4 * KB)
    sinT = at("sinT", [T], F, M0 + 6 * KB)
    krT = at("krT", [T], F, M0 + 8 * KB)
    rstdB = at("rstdB", [T], F, M0 + 10 * KB)
    diag = at("diag", [NT, P], F, M0)
    prob = [at(f"prob{i}", [T], F, M0 + 2 * i * KB) for i in range(2)]
    probT = [at(f"probT{i}", [T], F, M0 + (12 + 2 * i) * KB) for i in range(2)]
    rest = at("rest", [8, KEYS], F, M0)
    match = at("match", [NT, TOPK, TOPK], F, M0)
    cand = at("cand", [NT, 256], F, M0 + 4 * KB)
    cand_rest = at("cand_rest", [NT, 256], F, M0 + 8 * KB)
    top = at("top", [2, NT, TOPK], F, M0 + 12 * KB)
    top_at = at("top_at", [2, NT, TOPK], U32, M0 + 12 * KB + 512)
    top_atf = at("top_atf", [2, NT, TOPK], F, M0 + 13 * KB)
    best = at("best", [NT, TOPK], F, M0 + 13 * KB + 512)
    best_at = at("best_at", [NT, TOPK], U32, M0 + 13 * KB + 768)
    best_k = at("best_k", [2, NT, TOPK], U32, M0 + 14 * KB)
    best_kf = at("best_kf", [2, NT, TOPK], F, M0 + 14 * KB + 512)
    gate_e = at("gate_e", [NT, TOPK], F, M0 + 15 * KB)
    gate_sum = at("gate_sum", [NT], F, M0 + 15 * KB + 256)
    gate_inv = at("gate_inv", [NT], F, M0 + 15 * KB + 288)
    hk = at("hk", [3, T], F, M0)
    oh1 = at("oh1", [2, 4, P], F, M0 + 6 * KB)
    oh2 = at("oh2", [2, 4, P], F, M0 + 10 * KB)
    gtile = [at(f"gtile{i}", [NTB, GROUP, TB], F, M0 + 8 * KB * i) for i in range(2)]
    pRaw = at("pRaw", [2, T], F, M0)
    pH = at("pH", [2, T], R, M0 + 8 * KB)
    pL = at("pL", [2, T], R, M0 + 12 * KB)
    tmp = [at(f"tmp{i}", [T], F, C0 + 2 * KB * i) for i in range(2)]
    sq = [at(f"sq{i}", [T], F, C0 + (4 + 2 * i) * KB) for i in range(2)]
    route = at("route", [3, NT, P], F, C0)
    ssum = at("ssum", [T], F, C0 + 8 * KB)
    ut = [at(f"ut{i}", [T], F, C0 + (6 + 2 * i) * KB) for i in range(2)]
    rstd = at("rstd", [T], F, C0 + 10 * KB)
    ident = at("ident", [P], F, C0 + 12 * KB)
    iota = at("iota", [P], F, C0 + 12 * KB + 512)
    identR = at("identR", [P], R, C0 + 13 * KB)
    causalR = at("causalR", [P], R, C0 + 13 * KB + 512)
    ones = at("ones", [P], F, C0 + 14 * KB)
    gains = at("gains", [NGAINS], F, C0 + 14 * KB + 512)
    smax = at("smax", [32], F, C0 + 14 * KB + 864)
    nbias = at("nbias", [32], F, C0 + 14 * KB + 992)
    rsum = at("rsum", [32], F, C0 + 14 * KB + 1120)
    rinv = at("rinv", [32], F, C0 + 14 * KB + 1248)
    held = at("held", [1], F, C0 + 14 * KB + 1376)
    rtok = at("rtok", [NT], F, C0 + 14 * KB + 1408)

    ctx = ExitStack()
    with ctx:
        ps = ctx.enter_context(nc.psum_tensor("ps", [P, 8, 512], F))

        def sem(name):
            return ctx.enter_context(nc.semaphore(name))

        x_loaded = [sem(f"x_loaded{i}") for i in range(8)]
        first_loaded, first_hi, first_lo = sem("first_loaded"), sem("first_hi"), sem("first_lo")
        gains_loaded, consts_loaded = sem("gains_loaded"), sem("consts_loaded")
        rows_loaded, perm_loaded = sem("rows_loaded"), sem("perm_loaded")
        raw_loaded = [sem(f"raw_loaded{i}") for i in range(2)]
        hi_ready, lo_ready, tile_done = sem("hi_ready"), sem("lo_ready"), sem("tile_done")
        dve_step, pool_step = sem("dve_step"), sem("pool_step")
        consts_ready = sem("consts_ready")
        causal_built = sem("causal_built")
        sq_ready, sq_added, sum_done, mean_ready, root_ready, rstd_ready = (
            sem("sq_ready"), sem("sq_added"), sem("sum_done"), sem("mean_ready"), sem("root_ready"), sem("rstd_ready"))
        act_scaled, act_hi, act_lo = sem("act_scaled"), sem("act_hi"), sem("act_lo")
        v_gelu, ln_var, ln_std, v_ready, u_gelu = sem("v_gelu"), sem("ln_var"), sem("ln_std"), sem("v_ready"), sem("u_gelu")
        c_copied, c_scaled = sem("c_copied"), sem("c_scaled")
        mix_done, sgu_ready = sem("mix_done"), sem("sgu_ready")
        angle_ready, trig_ready = sem("angle_ready"), sem("trig_ready")
        pos_loaded = sem("pos_loaded")
        uq_copied, swap_done, rope_ready = sem("uq_copied"), sem("swap_done"), sem("rope_ready")
        kv_copied = sem("kv_copied")
        score_done, nbias_ready, exp_done, p_ready = sem("score_done"), sem("nbias_ready"), sem("exp_done"), sem("p_ready")
        pt_done, pt_copied, pv_done, o_copied = sem("pt_done"), sem("pt_copied"), sem("pv_done"), sem("o_copied")
        x_again = sem("x_again")
        h_mixed, a_read = sem("h_mixed"), sem("a_read")
        tok_done, tok_ready, u_scaled, sgu_scaled = sem("tok_done"), sem("tok_ready"), sem("u_scaled"), sem("sgu_scaled")
        chunk_scaled = sem("chunk_scaled")
        pre_stored = [sem(f"pre_stored{i}") for i in range(2)]
        pre_loaded = [sem(f"pre_loaded{i}") for i in range(2)]
        g_scaled = sem("g_scaled")
        keys_loaded = sem("keys_loaded")
        pq_copied, ps_done, tops_done, gate_sub, gate_exp, routed = (
            sem("pq_copied"), sem("ps_done"), sem("tops_done"), sem("gate_sub"), sem("gate_exp"), sem("routed"))
        hkT_done, hk_ready = sem("hkT_done"), sem("hk_ready")
        onehot_ready, gquad_done, gquad_copied = sem("onehot_ready"), sem("gquad_done"), sem("gquad_copied")
        gates_stored = [sem(f"gates_stored{i}") for i in range(2)]
        gates_loaded = [sem(f"gates_loaded{i}") for i in range(2)]
        gelu_done, act_gated, act_whi, act_wlo, h_acc = (
            sem("gelu_done"), sem("act_gated"), sem("act_whi"), sem("act_wlo"), sem("h_acc"))
        p_loaded, p_hi, p_lo, proj_copied = sem("p_loaded"), sem("p_hi"), sem("p_lo"), sem("proj_copied")
        sig_done, h_gated = sem("sig_done"), sem("h_gated")
        row_summed, row_mean, row_root, row_diag, row_spread = (
            sem("row_summed"), sem("row_mean"), sem("row_root"), sem("row_diag"), sem("row_spread"))
        out_ready, out_stored = sem("out_ready"), sem("out_stored")

        block = ctx.enter_context(nc.Block())

        def rstd_of(name):
            return {"cq": rstdL, "ckv": rstdL, "sgu": rstdB}.get(name, rstd)

        def gain(name, k):
            return gains[:, GAINS[name] + k:GAINS[name] + k + 1]

        N_SQ = {}
        _at = 0
        for name, k in (("mix", 16), ("cq", 4), ("ckv", 2), ("sgu", 8), ("attn", 8), ("ffn", 16), ("ple", 16), ("final", 16)):
            N_SQ[name] = _at
            _at += k
        NORMS = {"mix": 0, "cq": 1, "ckv": 2, "sgu": 3, "attn": 4, "ffn": 4, "ple": 5, "final": 6}
        N_SC = {}
        _at = 0
        for name, k in (("mix", 16), ("cq", 4), ("ckv", 2), ("sgu", 8), ("attn", 8), ("ffn", 16), ("ple", 16)):
            N_SC[name] = _at
            _at += k

        @block.sync
        def _(sp):
            def load(n, src, parity):
                sp.wait_ge(lo_ready, n - 1)
                sp.dma_start(raw[parity][:, :], src).then_inc(raw_loaded[parity], 16)

            sp.dma_start(raw[0][:, 0:1024], stream["v"][0, :, 0:1024]).then_inc(first_loaded, 16)
            sp.dma_start(gains[:, :], a["gains"]).then_inc(gains_loaded, 16)
            for i in range(8):
                sp.dma_start(hT[:, 2 * i:2 * i + 2, :], a["x"][:, 2 * i:2 * i + 2, :]).then_inc(x_loaded[i], 16)
                if i == 0:
                    sp.dma_start(raw[0][:, 1024:2048], stream["v"][0, :, 1024:2048]).then_inc(raw_loaded[0], 16)
                if i == 1:
                    sp.dma_start(raw[1][:, :], stream["v"][1, :, :]).then_inc(raw_loaded[1], 16)
            for name in ("v", "c", "u", "uq", "ukv"):
                for j in range(len(dict(STREAM)[name])):
                    if S0[name] + j >= 2:
                        load(S0[name] + j, stream[name][j, :, :], (S0[name] + j) % 2)
            with sp.Fori(0, 8) as i:
                for j in range(2):
                    load(S0["out"] + 2 * i + j, stream["out"][2 * i + j, :, :], j)
            def store_chunk(c, b):
                sp.wait_ge(gelu_done, c + 1)
                sp.dma_start(pre_dram[c, :, :], ut[b][:, :]).then_inc(pre_stored[b], 16)

            def load_head(h):
                n = S0["pq"] + 4 * h
                for s in range(2):
                    load(n + s, stream["pq"][2 * h + s, :, :], s)
                for s in range(2):
                    if not (isinstance(h, int) and h == 0):
                        store_chunk(2 * h - 2 + s, s)
                    load(n + 2 + s, stream["pu"][2 * h + s, :, :], s)

            load_head(0)
            with sp.Fori(1, HEADS) as h:
                load_head(h)
            n0 = S0["peer"] - Q_CHUNKS

            def store_gates(t, b):
                sp.wait_ge(gquad_copied, 8 * t + 8)
                sp.dma_start(gates_dram[t, :, :, :], gstage[b][:, :, :]).then_inc(gates_stored[b], 16)

            def load_gates(g, b):
                sp.dma_start(gtile[b][:, :, :, :],
                             gates_dram[:, :, bass.ts(g, GROUP), :].rearrange("b p i t -> p b i t")).then_inc(gates_loaded[b], 16)

            def load_chunk(c, b):
                if isinstance(c, int) and c < GROUP:
                    sp.wait_ge(pre_stored[b], (c - b) * 8 + 16)
                if not (isinstance(c, int) and c < 2):
                    sp.wait_ge(act_wlo, c - 1)
                sp.dma_start(tmp[b][:, :], pre_dram[c, :, :]).then_inc(pre_loaded[b], 16)

            for c in range(Q_CHUNKS, GATES_AT + 5):
                load(n0 + c, stream["pu"][c, :, :], c % 2)
                if c == GATES_AT + 3:
                    store_gates(0, 0)
                store_chunk(c - 2, c % 2)
            with sp.Fori(0, (BEATS - 4) // 4) as i:
                for b in range(4):
                    c = 4 * i + b + GATES_AT + 5
                    load(n0 + c, stream["pu"][c, :, :], b % 2)
                    if b % 2 == 0:
                        store_gates(2 * i + 1 + b // 2, 1 - b // 2)
                    store_chunk(c - 2, b % 2)
            for c in range(GATES_AT + 1 + BEATS, NPRE + 2):
                src = stream["pu"][c, :, :] if c < NPRE else stream["pv"][c - NPRE, :, :]
                load(n0 + c, src, c % 2)
                if c == GATES_AT + 1 + BEATS:
                    store_gates(NTB - 1, 1)
                store_chunk(c - 2, c % 2)
                if c == GATES_AT + 2 + BEATS:
                    for b in range(2):
                        sp.wait_ge(gates_stored[b], 16 * (NTB // 2))
                    load_gates(0, 0)
                    load_chunk(0, 0)
                    load_chunk(1, 1)
                    load_gates(1, 1)
                if c == NPRE:
                    load_chunk(2, 0)
                    load_chunk(3, 1)

            def load_prepared(g, b, first=False, last=False):
                for j in range(GROUP):
                    k = GROUP * (g - 1) + j + 2
                    if not (last and j >= 2):
                        load(n0 + NPRE + k, stream["pv"][k, :, :], j % 2)
                    if j == 0 and not first:
                        sp.wait_ge(act_gated, GROUP * (g - 1))
                        load_gates(g, b)
                    load_chunk(GROUP * g + j, j % 2)

            for b in range(2):
                sp.wait_ge(pre_stored[b], 16 * (NPRE // 2))
            load_prepared(1, 1, first=True)
            with sp.Fori(0, PRE_GROUPS // 2 - 2) as i:
                for b in range(2):
                    load_prepared(2 * i + 2 + b, b)
            load_prepared(PRE_GROUPS - 2, 0)
            load_prepared(PRE_GROUPS - 1, 1, last=True)

            s0 = n0 + 2 * NPRE - GROUP

            def load_group(g, b):
                for j in range(GROUP):
                    n = s0 + 8 * (g - PRE_GROUPS) + 2 * j
                    load(n, stream["pu"][GROUP * g + j, :, :], 0)
                    if j == 0:
                        sp.wait_ge(act_gated, GROUP * (g - 1))
                        load_gates(g, b)
                    load(n + 1, stream["pv"][GROUP * (g - 1) + j, :, :], 1)

            with sp.Fori(0, (NGROUPS - PRE_GROUPS) // 2) as i:
                for b in range(2):
                    load_group(2 * i + PRE_GROUPS + b, b)
            sp.wait_ge(act_gated, GROUP * (NGROUPS - 1))
            sp.dma_start(pRaw[:, :, :], a["p"]).then_inc(p_loaded, 16)
            for j in range(GROUP):
                load(S0["proj"] - GROUP + j, stream["pv"][GROUP * (NGROUPS - 1) + j, :, :], j % 2)
            for j in range(2):
                load(S0["proj"] + j, stream["proj"][j, :, :], j)
            with sp.Fori(0, 8) as i:
                for j in range(2):
                    load(S0["gate"] + 2 * i + j, stream["gate"][2 * i + j, :, :], j)
            for half in range(2):
                t = slice(256 * half, 256 * half + 256)
                for i in range(4):
                    sp.wait_ge(out_ready, 16 * half + 4 * i + 4)
                    sp.dma_start(out[:, 4 * i:4 * i + 4, t], hT[:, 4 * i:4 * i + 4, t]).then_inc(out_stored, 16)
            sp.wait_ge(out_stored, 16 * 8)

        @block.gpsimd
        def _(pool):
            for dst, src in ((ident[:, :], a["consts"][:, 0:128]), (iota[:, :], a["consts"][:, 128:256])):
                pool.dma_start(dst, src).then_inc(consts_loaded, 16)
            pool.dma_start(wsT[:, :, :], a["ws"]).then_inc(rows_loaded, 16)
            pool.dma_start(sgu_rows[:, :, :, :].rearrange("p a b c -> p (a b c)"),
                           a["rows"].partition_broadcast(P)).then_inc(rows_loaded, 16)
            nc.gpsimd.memset(ones[:, :], 1.0).then_inc(consts_ready, 1)
            nc.gpsimd.memset(rstd[:, 0:P], 0.0).then_inc(pool_step, 1)
            pool.wait_ge(pool_step, 1)
            nc.gpsimd.affine_select(out=rstd[:, 0:P], in_=rstd[:, 0:P], compare_op=ALU.is_ge, fill=-1e30,
                                    base=0, pattern=[[-1, P]], channel_multiplier=1).then_inc(causal_built, 1)
            pool.wait_ge(rows_loaded, 32)
            nc.gpsimd.affine_select(out=wsT[:, :, :], in_=wsT[:, :, :], compare_op=ALU.is_ge, fill=0.0,
                                    base=0, pattern=[[0, 8], [1, P]], channel_multiplier=-1).then_inc(consts_ready, 1)
            pool.wait_ge(act_lo, KD)
            pool.wait_ge(sq_ready, KD)
            pool.dma_start(perm[:, :], a["consts"][:, 256:384]).then_inc(perm_loaded, 16)
            pool.dma_start(freq[:, :], a["consts"][:, 384:386]).then_inc(perm_loaded, 16)
            pool.wait_ge(v_ready, 4)
            pool.dma_start(krT[:, :].bitcast(I32), a["pos"].partition_broadcast(P)).then_inc(pos_loaded, 16)
            pool.wait_ge(rope_ready, 5)
            pool.wait_ge(sgu_ready, 8)
            pool.wait_ge(act_lo, N_SC["sgu"])
            for i in range(4):
                pool.dma_start(hT[:, 4 * i:4 * i + 4, :], a["x"][:, 4 * i:4 * i + 4, :]).then_inc(x_again, 16)
            pool.wait_ge(act_lo, N_SC["ffn"])
            pool.dma_start(keys[:, :, :, :], a["keys"]).then_inc(keys_loaded, 16)

        @block.scalar
        def _(act):
            A = nc.scalar.activation

            def hi(n, parity, used):
                act.wait_ge(raw_loaded[parity], (n - parity) * 8 + 16)
                if not (isinstance(used, int) and used <= 0):
                    act.wait_ge(tile_done, used)
                A(wH[parity][:, :], raw[parity][:, :], ACT.Copy).then_inc(hi_ready, 1)

            def square(name, k, src):
                n = N_SQ[name] + k
                if not (isinstance(n, int) and n < 2):
                    act.wait_ge(sq_added, n - 1)
                A(sq[k0(k) % 2][:, :], src, ACT.Square).then_inc(sq_ready, 1)

            def root(name):
                act.wait_ge(mean_ready, NORMS[name] + 1)
                dst = rstd_of(name)
                A(dst[:, :], dst[:, :], ACT.Sqrt).then_inc(root_ready, 1)

            def row_root_of(n, t):
                act.wait_ge(row_mean, n)
                A(rtok[:, t], rtok[:, t], ACT.Sqrt).then_inc(row_root, 1)

            def split_hi(name, order, dst):
                for j, k in enumerate(order):
                    act.wait_ge(act_scaled, j + 1)
                    A(dst[:, k, :], tmp[j % 2][:, :], ACT.Copy).then_inc(act_hi, 1)

            def gain_hi(name, k):
                A(aH[:, k, :], hT[:, k, :], ACT.Copy, scale=gain(name, k)).then_inc(act_hi, 1)

            def k0(k):
                return k if isinstance(k, int) else 0

            act.wait_ge(first_loaded, 16)
            A(wH[0][:, 0:1024], raw[0][:, 0:1024], ACT.Copy).then_inc(first_hi, 1)
            act.wait_ge(gains_loaded, 16)
            for k in range(KD):
                if k % 2 == 0:
                    act.wait_ge(x_loaded[k // 2], 16)
                gain_hi("mix", k)
                if k == 0:
                    act.wait_ge(raw_loaded[0], 16)
                    A(wH[0][:, 1024:2048], raw[0][:, 1024:2048], ACT.Copy).then_inc(hi_ready, 1)
                square("mix", k, hT[:, k, :])
                if k == 3:
                    hi(1, 1, 0)
                if k == 5:
                    act.wait_ge(consts_loaded, 32)
                    A(identR[:, :], ident[:, :], ACT.Copy)
                    act.wait_ge(causal_built, 1)
                    A(causalR[:, :], rstd[:, 0:P], ACT.Copy).then_inc(consts_ready, 1)
            hi(2, 0, CUM[0])
            root("mix")
            for cb in range(2):
                for n in range(max(2, S0["v"] + 4 * cb), S0["v"] + 4 * cb + 4):
                    hi(n + 1, (n + 1) % 2, CUM[n - 1])
                if cb == 0:
                    act.wait_ge(tok_ready, 1)
                for tt in range(NT):
                    act.wait_ge(tile_done, 7 * cb + 4 + tt)
                    A(vtok[:, tt, cb * 512:cb * 512 + 512], ps[:, tt, :], ACT.Gelu_apprx_tanh,
                      scale=rtok[:, tt:tt + 1]).then_inc(v_gelu, 1)
            for j in range(7):
                n = S0["c"] + j
                hi(n + 1, (n + 1) % 2, CUM[n - 1])
                if j % 2 == 0:
                    act.wait_ge(ln_var, j // 2 + 1)
                    A(ln_rstd[:, :], ln_rstd[:, :], ACT.Sqrt).then_inc(ln_std, 1)
                if j < 4:
                    act.wait_ge(c_copied, j + 1)
                    square("cq", j, cT[:, j, :])
            for m in range(8):
                n = S0["u"] + m
                hi(n + 1, (n + 1) % 2, CUM[n - 1])
                if m == 1:
                    root("cq")
                if m == 2:
                    act.wait_ge(c_copied, 6)
                    for k in range(KKV):
                        square("ckv", k, cT[:, KQ + k, :])
                if m == 4:
                    root("ckv")
                if m == 5:
                    act.wait_ge(angle_ready, 1)
                    A(cosT[:, :], cosT[:, :], ACT.Sin).then_inc(trig_ready, 1)
                if m == 6:
                    act.wait_ge(c_scaled, KQ + KKV)
                    for k in range(KQ):
                        A(cqH[:, k, :], cT[:, k, :], ACT.Copy).then_inc(act_hi, 1)
                if m == 7:
                    act.wait_ge(angle_ready, 2)
                    A(sinT[:, :], sinT[:, :], ACT.Sin).then_inc(trig_ready, 1)
                act.wait_ge(u_scaled, m + 1)
                u = mixT[:, 8 + m, :]
                A(u, u, ACT.Gelu_apprx_tanh).then_inc(u_gelu, 1)
            for s in range(3):
                n = S0["uq"] + s
                hi(n + 1, (n + 1) % 2, CUM[n - 1])
                if s == 0:
                    for k in range(KKV):
                        A(ckvH[:, k, :], cT[:, KQ + k, :], ACT.Copy).then_inc(act_hi, 1)
                for m in range(4):
                    t = 4 * s + m
                    if t < SGU_TILES:
                        act.wait_ge(sgu_ready, t + 1)
                        square("sgu", t, mixT[:, 8 + t, :])
                    act.wait_ge(tile_done, CUM[n - 1] + m + 1)
                    A(qT[:, t, :], ps[:, 4 + t % 4, :], ACT.Copy).then_inc(uq_copied, 1)
            for s in range(2):
                n = S0["ukv"] + s
                hi(n + 1, (n + 1) % 2, CUM[n - 1])
                for m in range(8):
                    act.wait_ge(tile_done, CUM[n - 1] + m + 1)
                    dst = kT[:, m, :] if s == 0 else vA[:, m % 4, 512 * (m // 4):512 * (m // 4) + 512]
                    A(dst, ps[:, 4 + m % 4, :], ACT.Copy).then_inc(kv_copied, 1)
                    if s == 0 and m == 1:
                        root("sgu")
            ITEMS = HEADS * NT
            for n in range(ITEMS + 3):
                if n == 6:
                    hi(S0["out"] + 1, 1, CUM[S0["out"] - 1])
                if n < ITEMS:
                    w = P * (n % NT + 1)
                    act.wait_ge(nbias_ready, n + 1)
                    if n >= 2:
                        act.wait_ge(pt_done, n - 1)
                    A(prob[n % 2][:, 0:w], ps[:, n % 3, 0:w], ACT.Exp, bias=nbias[:, n:n + 1], scale=SCALE,
                      accum_out=rsum[:, n:n + 1]).then_inc(exp_done, 1)
                m = n - 2
                if 0 <= m < ITEMS:
                    w = P * (m % NT + 1)
                    act.wait_ge(pt_done, m + 1)
                    if m >= 2:
                        act.wait_ge(pv_done, m - 1)
                    A(probT[m % 2][:, 0:w], ps[:, 3 + m % 2, 0:w], ACT.Copy).then_inc(pt_copied, 1)
                if n >= 5 and (n - 5) % NT == 3:
                    h = (n - 5) // NT
                    act.wait_ge(o_copied, h + 1)
                    square("attn", h, mixT[:, h, :])
            for h in range((ITEMS + 2 - 5 - 3) // NT + 1, HEADS - 1):
                act.wait_ge(o_copied, h + 1)
                square("attn", h, mixT[:, h, :])
            act.wait_ge(pv_done, ITEMS)
            act.wait_ge(sgu_scaled, 8)
            for g in range(SGU_TILES):
                A(aH[:, 8 + g, :], mixT[:, 8 + g, :], ACT.Copy).then_inc(act_hi, 1)
                if g == 0:
                    act.wait_ge(o_copied, HEADS)
                    square("attn", HEADS - 1, mixT[:, HEADS - 1, :])
                if g == 4:
                    row_root_of(1, slice(0, NT))
            split_hi("attn", range(8), aH)

            def mixed_square(i, j):
                act.wait_ge(h_mixed, 2 * i + j + 1)
                act.wait_ge(sq_added, N_SQ["ffn"] - 1 + 2 * i + j)
                A(sq[j][:, :], hT[:, 2 * i + j, :], ACT.Square).then_inc(sq_ready, 1)

            mixed_square(0, 0)
            hi(S0["out"] + 2, 0, CUM[S0["out"]])
            mixed_square(0, 1)
            with act.Fori(1, 7) as i:
                for j in range(2):
                    hi(S0["out"] + 2 * i + j + 1, (j + 1) % 2, CUM[S0["out"] + j - 1] + 2 * i)
                    mixed_square(i, j)
            hi(S0["out"] + 15, 1, CUM[S0["out"] + 13])
            mixed_square(7, 0)
            hi(S0["out"] + 16, 0, CUM[S0["out"] + 14])
            for k in range(KD - 1):
                act.wait_ge(a_read, k + 1)
                gain_hi("ffn", k)
            mixed_square(7, 1)
            gain_hi("ffn", KD - 1)
            def gelu(uc, b):
                act.wait_ge(chunk_scaled, uc + 1)
                A(ut[b][:, :], ut[b][:, :], ACT.Gelu_apprx_tanh).then_inc(gelu_done, 1)

            def head(h, b, i, m, lead=lambda: None, exps=lambda: None):
                n = S0["pq"] + 4 * h
                hi(n + 1, 1, CUM[m - 1] + 8 * i)
                lead()
                for s in range(2):
                    act.wait_ge(tile_done, CUM[m + s] + 8 * i)
                    A(pqT[b][:, s, :], ps[:, s, :], ACT.Copy).then_inc(pq_copied, 1)
                    if s == 0:
                        hi(n + 2, 0, CUM[m] + 8 * i)
                        exps()
                hi(n + 3, 1, CUM[m + 1] + 8 * i)
                hi(n + 4, 0, CUM[m + 2] + 8 * i)
                gelu(2 * h, 0)

            def gate_exps(h):
                act.wait_ge(gate_sub, h + 1)
                for t in range(NT):
                    ins = A(gate_e[:, t, :], gate_e[:, t, :], ACT.Exp, scale=rtok[:, t:t + 1])
                ins.then_inc(gate_exp, 1)

            head(0, 0, 0, S0["pq"], lead=lambda: root("ffn"))
            act.wait_ge(tok_ready, 2)
            with act.Fori(0, 3) as i:
                for b in range(2):
                    h = 2 * i + b + 1
                    head(h, 1 - b, i, S0["pq"] + 4 + 4 * b, lead=lambda: gelu(2 * h - 1, 1), exps=lambda: gate_exps(h - 1))
            head(7, 1, 3, S0["pq"] + 4, lead=lambda: gelu(13, 1), exps=lambda: gate_exps(6))

            n0 = S0["peer"] - Q_CHUNKS

            def pre_hi(c):
                hi(n0 + c + 1, (c + 1) % 2, CUM[n0 + c - 1])

            pre_hi(Q_CHUNKS)
            gelu(Q_CHUNKS - 1, 1)
            pre_hi(Q_CHUNKS + 1)
            gate_exps(HEADS - 1)
            gelu(Q_CHUNKS, 0)
            pre_hi(Q_CHUNKS + 2)
            gelu(Q_CHUNKS + 1, 1)
            for r in range(3):
                act.wait_ge(hkT_done, r + 1)
                A(hk[:, r, :], ps[:, r, :], ACT.Copy).then_inc(hk_ready, 1)

            def gate_beat(t, b, i):
                c = GATES_AT + b
                hi(n0 + GATES_AT + 1 + t, (c + 1) % 2, CUM[n0 + c - 1] + 4 * i)
                gelu(GATES_AT - 1 + t, (c - 1) % 2)
                if b % 2 == 0 and not (isinstance(i, int) and i == 0):
                    act.wait_ge(gates_stored[b // 2], 16 * i)
                for q in range(4):
                    act.wait_ge(gquad_done, 4 * t + q + 1)
                    k = 16 * (b % 2) + 4 * q
                    A(gstage[b // 2][:, :, k:k + 4].rearrange("p i t -> p t i"),
                      ps[:, 2 + q, :].rearrange("p (t i) -> p t i", t=4), ACT.Copy).then_inc(gquad_copied, 1)

            for b in range(4):
                gate_beat(b, b, 0)
            with act.Fori(1, BEATS // 4) as i:
                for b in range(4):
                    gate_beat(4 * i + b, b, i)

            def weight_hi(uc, j, b, src):
                act.wait_ge(act_gated, uc + 1)
                A(actH[b][:, j, :], src[:, :], ACT.Copy).then_inc(act_whi, 1)

            for c in range(GATES_AT + BEATS, NPRE):
                pre_hi(c)
                gelu(c - 1, (c - 1) % 2)
                if c >= NPRE - 2:
                    for k in range(2):
                        w = 2 * (c - NPRE + 2) + k
                        weight_hi(w, w, 0, tmp[k])
            gelu(NPRE - 1, 1)

            def prepared_hi(g, b, m, i):
                for j in range(GROUP):
                    hi(m + j + 1 + 8 * i, (j + 1) % 2, CUM[m + j - 1] + 32 * i)
                    weight_hi(GROUP * g + j, j, b, tmp[j % 2])

            prepared_hi(1, 1, n0 + NPRE, 0)
            with act.Fori(0, PRE_GROUPS // 2 - 1) as i:
                for b in range(2):
                    prepared_hi(2 * i + 2 + b, b, n0 + NPRE + GROUP * (1 + b), i)

            s0 = n0 + 2 * NPRE - GROUP

            with act.Fori(0, (NGROUPS - PRE_GROUPS) // 2) as i:
                for b in range(2):
                    for j in range(GROUP):
                        m = s0 + 8 * b + 2 * j
                        g = 2 * i + PRE_GROUPS + b
                        hi(m + 1 + 16 * i, 1, CUM[m - 1] + 40 * i)
                        gelu(GROUP * g + j, j % 2)
                        hi(m + 2 + 16 * i, 0, CUM[m] + 40 * i)
                        weight_hi(GROUP * g + j, j, b, ut[j % 2])
            last = S0["proj"] - GROUP
            for j in range(GROUP):
                hi(last + j + 1, (j + 1) % 2, CUM[last + j - 1])
                if j == 0:
                    act.wait_ge(p_loaded, 16)
                    A(pH[:, :, :], pRaw[:, :, :], ACT.Copy).then_inc(p_hi, 1)
                for m in range(4):
                    act.wait_ge(h_acc, 16 * (NGROUPS - 1) + 4 * j + m + 1)
                    square("ple", 4 * j + m, hT[:, 4 * j + m, :])
                    gain_hi("ple", 4 * j + m)
            for s in range(2):
                n = S0["proj"] + s
                if s == 1:
                    root("ple")
                hi(n + 1, (n + 1) % 2, CUM[n - 1])
                for m in range(8):
                    act.wait_ge(tile_done, CUM[n - 1] + m + 1)
                    A(projT[:, 8 * s + m, :], ps[:, 2 + m % 4, :], ACT.Copy).then_inc(proj_copied, 1)

            def gate_tile(i, j):
                hi(S0["gate"] + 2 * i + j + 1, (j + 1) % 2, CUM[S0["gate"] + j - 1] + 2 * i)
                if isinstance(i, int) and (i, j) == (6, 1):
                    hi(S0["gate"] + 15, 1, CUM[S0["gate"] + 13])
                act.wait_ge(g_scaled, 2 * i + j + 1)
                A(tmp[j][:, :], tmp[j][:, :], ACT.Sigmoid).then_inc(sig_done, 1)
                act.wait_ge(h_gated, 2 * i + j + 1)
                act.wait_ge(sq_added, N_SQ["final"] - 1 + 2 * i + j)
                A(sq[j][:, :], hT[:, 2 * i + j, :], ACT.Square).then_inc(sq_ready, 1)

            for j in range(2):
                gate_tile(0, j)
            with act.Fori(1, 6) as i:
                for j in range(2):
                    gate_tile(i, j)
            for j in range(2):
                gate_tile(6, j)
            for half in range(2):
                t = slice(256 * half, 256 * half + 256)
                for j in range(2):
                    n = 14 + 2 * half + j
                    act.wait_ge(g_scaled, n + 1)
                    A(tmp[j][:, t], tmp[j][:, t], ACT.Sigmoid).then_inc(sig_done, 1)
                    act.wait_ge(h_gated, n + 1)
                    act.wait_ge(sq_added, N_SQ["final"] - 1 + n)
                    A(sq[j][:, t], hT[:, 14 + j, t], ACT.Square).then_inc(sq_ready, 1)
                row_root_of(2 + half, slice(2 * half, 2 * half + 2))

        @block.vector
        def _(dve):
            V = nc.vector
            st = Steps(dve, dve_step)

            def hold():
                V.tensor_copy(held[:, :], ones[:, 0:1])

            def lo(n, parity):
                dve.wait_ge(hi_ready, n + 1)
                V.tensor_tensor(wL[parity][:, :], raw[parity][:, :], wH[parity][:, :].bitcast(F), ALU.subtract).then_inc(lo_ready, 1)

            def add_square(name, k, first=False, par=None):
                n = N_SQ[name] + k
                dve.wait_ge(sq_ready, n + 1)
                s = sq[k % 2 if par is None else par]
                if first:
                    if not (isinstance(n, int) and n == 0):
                        dve.wait_ge(sum_done, NORMS[name])
                    V.tensor_copy(ssum[:, :], s[:, :]).then_inc(sq_added, 1)
                else:
                    dve.wait_ge(sq_added, n)
                    V.tensor_tensor(ssum[:, :], ssum[:, :], s[:, :], ALU.add).then_inc(sq_added, 1)

            def mean_of(name, width, bank):
                dst = rstd_of(name)
                dve.wait_ge(sum_done, NORMS[name] + 1)
                V.tensor_scalar(dst[:, :], ps[:, bank, :], 1.0 / width, EPS, ALU.mult, ALU.add).then_inc(mean_ready, 1)

            def row_mean_of(n, width, bank, t):
                dve.wait_ge(row_summed, n)
                V.tensor_scalar(rtok[:, t], ps[:, bank, t], 1.0 / width, EPS, ALU.mult, ALU.add).then_inc(row_mean, 1)

            def row_inverse(n, t):
                dve.wait_ge(row_root, n)
                st.did(V.reciprocal(rtok[:, t], rtok[:, t]))
                st.settle()
                count = t.stop - t.start
                V.tensor_tensor(diag[:, t, :], ident[:, :].unsqueeze(1).to_broadcast([P, count, P]),
                                rtok[:, t].unsqueeze(2).to_broadcast([P, count, P]), ALU.mult).then_inc(row_diag, 1)

            def inverse_root(name, width, bank):
                mean_of(name, width, bank)
                dst = rstd_of(name)
                dve.wait_ge(root_ready, NORMS[name] + 1)
                V.reciprocal(dst[:, :], dst[:, :]).then_inc(rstd_ready, 1)
                dve.wait_ge(rstd_ready, NORMS[name] + 1)

            def scale_split(name, tiles, hi_dst, lo_dst):
                def low(j):
                    dve.wait_ge(act_hi, N_SC[name] + j + 1)
                    k = tiles[j][0]
                    V.tensor_tensor(lo_dst[:, k, :], tmp[j % 2][:, :], hi_dst[:, k, :].bitcast(F), ALU.subtract).then_inc(act_lo, 1)

                for j, (k, src, g, r) in enumerate(tiles):
                    if j >= 2:
                        dve.wait_ge(act_lo, N_SC[name] + j - 1)
                    V.scalar_tensor_tensor(tmp[j % 2][:, :], src, g, r[:, :], ALU.mult, ALU.mult).then_inc(act_scaled, 1)
                    if j >= 1:
                        low(j - 1)
                low(len(tiles) - 1)

            def gain_lo(name, k):
                dve.wait_ge(act_hi, N_SC[name] + k + 1)
                V.scalar_tensor_tensor(aL[:, k, :], hT[:, k, :], gain(name, k), aH[:, k, :].bitcast(F),
                                       ALU.mult, ALU.subtract).then_inc(act_lo, 1)

            def token_rms(n, bank):
                dve.wait_ge(tok_done, n)
                V.tensor_copy(rtok[:, :], ps[:, bank, 0:NT]).then_inc(tok_ready, 1)

            dve.wait_ge(first_hi, 1)
            V.tensor_tensor(wL[0][:, 0:1024], raw[0][:, 0:1024], wH[0][:, 0:1024].bitcast(F), ALU.subtract).then_inc(first_lo, 1)
            for k in range(KD):
                gain_lo("mix", k)
                if k == 0:
                    dve.wait_ge(hi_ready, 1)
                    V.tensor_tensor(wL[0][:, 1024:2048], raw[0][:, 1024:2048], wH[0][:, 1024:2048].bitcast(F),
                                    ALU.subtract).then_inc(lo_ready, 1)
                add_square("mix", k, first=k == 0)
                if k == 3:
                    lo(1, 1)
            lo(2, 0)
            inverse_root("mix", D, 7)

            for n in range(3, S0["c"] + 1):
                lo(n, n % 2)
                if n == 3:
                    token_rms(1, 7)
            dve.wait_ge(v_gelu, 8)
            dve.wait_ge(rows_loaded, 32)

            def layer_norm(t):
                dve.wait_ge(v_gelu, 5 + t)
                for g in range(8):
                    st.did(V.bn_stats(ln_stats[:, g, :], vtok[:, t, g * P:(g + 1) * P]))
                st.settle()
                for g in range(8):
                    st.did(V.bn_aggr(ln_mv[:, g, :], ln_stats[:, g, :]))
                st.settle()
                V.tensor_scalar_add(ln_rstd[:, :], ln_mv[:, :, 1], EPS).then_inc(ln_var, 1)
                dve.wait_ge(ln_std, t + 1)
                st.did(V.reciprocal(ln_rstd[:, :], ln_rstd[:, :]))
                st.settle()
                for g in range(8):
                    v = vtok[:, t, g * P:(g + 1) * P]
                    st.did(V.tensor_scalar(v, v, ln_mv[:, g, 0:1], ln_rstd[:, g:g + 1], ALU.subtract, ALU.mult))
                st.settle()
                v = vtok[:, t, :]
                st.did(V.tensor_tensor(v, v, sgu_rows[:, 1, :, :].rearrange("p a b -> p (a b)"), ALU.mult))
                st.settle()
                V.tensor_tensor(v, v, sgu_rows[:, 2, :, :].rearrange("p a b -> p (a b)"), ALU.add).then_inc(v_ready, 1)

            for j in range(7):
                n = S0["c"] + j
                lo(n + 1, (n + 1) % 2)
                if j % 2 == 0:
                    layer_norm(j // 2)
                dve.wait_ge(tile_done, CUM[n])
                V.tensor_tensor(cT[:, j, :], ps[:, 6 + j % 2, :], rstd[:, :], ALU.mult).then_inc(c_copied, 1)
                if j < 4:
                    add_square("cq", j, first=j == 0)

            def angle(dst, quarter):
                st.did(V.tensor_scalar(tmp[1][:, :], tmp[0][:, :], 1.0 / (2 * PI), quarter, ALU.mult, ALU.add))
                st.settle()
                st.did(V.tensor_scalar(tmp[1][:, :], tmp[1][:, :], ROUND, None, ALU.add))
                st.settle()
                st.did(V.tensor_scalar(tmp[1][:, :], tmp[1][:, :], ROUND, None, ALU.subtract))
                st.settle()
                src = tmp[0]
                for part in two_pi_parts():
                    st.did(V.scalar_tensor_tensor(dst[:, :], tmp[1][:, :], -part, src[:, :], ALU.mult, ALU.add))
                    st.settle()
                    src = dst
                st.did(V.tensor_scalar(dst[:, :], dst[:, :], quarter * 2 * PI, PI_BELOW, ALU.add, ALU.min))
                st.settle()
                V.tensor_scalar(dst[:, :], dst[:, :], -PI_BELOW, None, ALU.max).then_inc(angle_ready, 1)

            def scale_latent(name, k0, count):
                for k in range(count):
                    V.scalar_tensor_tensor(cT[:, k0 + k, :], cT[:, k0 + k, :], gain(name, k), rstdL[:, :],
                                           ALU.mult, ALU.mult).then_inc(c_scaled, 1)

            for m in range(8):
                n = S0["u"] + m
                lo(n + 1, (n + 1) % 2)
                if m == 1:
                    inverse_root("cq", QL, 0)
                    scale_latent("cq", 0, KQ)
                if m == 2:
                    for k in range(KKV):
                        add_square("ckv", k, first=k == 0)
                if m == 3:
                    dve.wait_ge(pos_loaded, 16)
                    dve.wait_ge(perm_loaded, 32)
                    st.did(V.tensor_copy(tmp[0][:, :], krT[:, :].bitcast(I32)))
                    st.settle()
                    st.did(V.tensor_scalar(tmp[0][:, :], tmp[0][:, :], freq[:, 0:1], None, ALU.mult))
                    st.settle()
                    angle(cosT, 0.25)
                if m == 4:
                    dve.wait_ge(c_scaled, KQ)
                    inverse_root("ckv", KVL, 1)
                    scale_latent("ckv", KQ, KKV)
                if m == 5:
                    angle(sinT, 0.0)
                if m == 6:
                    for k in range(KQ):
                        dve.wait_ge(act_hi, N_SC["cq"] + k + 1)
                        V.tensor_tensor(cqL[:, k, :], cT[:, k, :], cqH[:, k, :].bitcast(F), ALU.subtract).then_inc(act_lo, 1)
                dve.wait_ge(tile_done, CUM[n])
                V.tensor_tensor(mixT[:, 8 + m, :], ps[:, 4 + m % 2, :], rstd[:, :], ALU.mult).then_inc(u_scaled, 1)

            for s in range(3):
                lo(S0["uq"] + s + 1, (S0["uq"] + s + 1) % 2)
                if s == 0:
                    for k in range(KKV):
                        dve.wait_ge(act_hi, N_SC["ckv"] + k + 1)
                        V.tensor_tensor(ckvL[:, k, :], cT[:, KQ + k, :], ckvH[:, k, :].bitcast(F), ALU.subtract).then_inc(act_lo, 1)
                if s == 2:
                    continue
                for g in range(4 * s, 4 * s + 4):
                    dve.wait_ge(mix_done, g + 1)
                    if g < 2:
                        dve.wait_ge(angle_ready, 2)
                    else:
                        dve.wait_ge(sgu_ready, g - 1)
                    st.did(V.tensor_tensor(tmp[g % 2][:, :].rearrange("p (c t) -> p c t", c=NT),
                                           ps[:, g % 4, :].rearrange("p (c t) -> p c t", c=NT),
                                           sgu_rows[:, 0, g, :].unsqueeze(1).to_broadcast([P, NT, P]), ALU.add))
                    st.settle()
                    if g == 0:
                        dve.wait_ge(u_gelu, 8)
                    V.tensor_tensor(mixT[:, 8 + g, :], mixT[:, 8 + g, :], tmp[g % 2][:, :], ALU.mult).then_inc(sgu_ready, 1)
                    if g >= 1:
                        add_square("sgu", g - 1, first=g == 1)
            add_square("sgu", 7)

            def rope(j, src, dst):
                st.did(V.tensor_tensor(tmp[0][:, :], src, cosT[:, :], ALU.mult))
                dve.wait_ge(swap_done, j + 1)
                st.did(V.tensor_tensor(tmp[1][:, :], ps[:, 2 + j % 2, :], sinT[:, :], ALU.mult))
                st.settle()
                V.tensor_tensor(dst, tmp[0][:, :], tmp[1][:, :], ALU.add).then_inc(rope_ready, 1)

            dve.wait_ge(trig_ready, 2)
            dve.wait_ge(sgu_ready, 8)
            rope(0, cT[:, 6, :], krT[:, :])
            lo(S0["ukv"] + 1, (S0["ukv"] + 1) % 2)
            inverse_root("sgu", 1024, 0)
            for j in range(4):
                dve.wait_ge(uq_copied, 9 + j)
                dve.wait_ge(rope_ready, 1 + j)
                rope(1 + j, qT[:, 8 + j, :], qT[:, 8 + j, :])
            for g in range(SGU_TILES):
                V.scalar_tensor_tensor(mixT[:, 8 + g, :], mixT[:, 8 + g, :], gain("sgu", g), rstdB[:, :],
                                       ALU.mult, ALU.mult).then_inc(sgu_scaled, 1)
            lo(S0["out"], 0)
            ITEMS = HEADS * NT
            for n in range(ITEMS + 1):
                if n == 8:
                    lo(S0["out"] + 1, 1)
                if n < ITEMS:
                    w = P * (n % NT + 1)
                    dve.wait_ge(score_done, n + 1)
                    st.did(V.reduce_max(smax[:, n:n + 1], ps[:, n % 3, 0:w], AX))
                    st.settle()
                    V.tensor_scalar(nbias[:, n:n + 1], smax[:, n:n + 1], -SCALE, None, ALU.mult).then_inc(nbias_ready, 1)
                if n >= 1:
                    m = n - 1
                    w = P * (m % NT + 1)
                    dve.wait_ge(exp_done, m + 1)
                    st.did(V.reciprocal(rinv[:, m:m + 1], rsum[:, m:m + 1]))
                    st.settle()
                    V.tensor_scalar(prob[m % 2][:, 0:w], prob[m % 2][:, 0:w], rinv[:, m:m + 1], None, ALU.mult).then_inc(p_ready, 1)
                if n >= NT + 4 and n % NT == 0 or n == ITEMS:
                    for h in ([n // NT - 2] if n < ITEMS else [HEADS - 2, HEADS - 1]):
                        dve.wait_ge(pv_done, NT * (h + 1))
                        V.tensor_copy(mixT[:, h, :], ps[:, 5 + h % 2, :]).then_inc(o_copied, 1)
                        if h >= 1:
                            add_square("attn", h - 1, first=h == 1)

            def sgu_lo(g):
                dve.wait_ge(act_hi, N_SC["sgu"] + g + 1)
                V.tensor_tensor(aL[:, 8 + g, :], mixT[:, 8 + g, :], aH[:, 8 + g, :].bitcast(F), ALU.subtract).then_inc(act_lo, 1)

            sgu_lo(0)
            add_square("attn", HEADS - 1)
            for g in range(1, 3):
                sgu_lo(g)
            row_mean_of(1, 1024, 7, slice(0, NT))
            for g in range(3, 5):
                sgu_lo(g)
            row_inverse(1, slice(0, NT))
            for g in range(5, 8):
                sgu_lo(g)
            dve.wait_ge(row_spread, 1)
            scale_split("attn", [(k, mixT[:, k, :], gain("attn", k), ps[:, 7, :]) for k in range(8)], aH, aL)
            dve.wait_ge(x_again, 64)

            def residual(i, j, split=True):
                if split:
                    lo(S0["out"] + 2 * i + j + 1, (j + 1) % 2)
                dve.wait_ge(tile_done, CUM[S0["out"] + j] + 2 * i)
                V.tensor_tensor(hT[:, 2 * i + j, :], hT[:, 2 * i + j, :], ps[:, j, :], ALU.add).then_inc(h_mixed, 1)

            residual(0, 0, split=False)
            add_square("ffn", 0, first=True)
            residual(0, 1)
            add_square("ffn", 1)
            with dve.Fori(1, 7) as i:
                for j in range(2):
                    residual(i, j)
                    add_square("ffn", 2 * i + j, par=j)
            residual(7, 0)
            add_square("ffn", 14)
            lo(S0["out"] + 16, 0)
            for k in range(KD - 1):
                gain_lo("ffn", k)
            residual(7, 1, split=False)
            add_square("ffn", 15)
            gain_lo("ffn", KD - 1)

            KEY_STEPS, PAIR_STEPS = 39, 36

            units = [(s, t) for s in range(2) for t in range(NT)]

            def best_keys(h, b):
                def unit(s, t):
                    return ps[:, 2 + 2 * b + s, t * P:(t + 1) * P]

                dve.wait_ge(ps_done, 2 * h + 2)
                hold()
                for s, t in units:
                    st.did(V.max(top[:, s, t, 0:8], unit(s, t)))
                st.settle()
                hold()
                for s, t in units:
                    st.did(V.match_replace(rest[:, s * NT + t, :], top[:, s, t, 0:8], unit(s, t), -3e38))
                st.settle()
                hold()
                for s, t in units:
                    st.did(V.max(top[:, s, t, 8:16], rest[:, s * NT + t, :]))
                for s, t in units:
                    st.did(V.max_index(top_at[:, s, t, 0:8], top[:, s, t, 0:8], unit(s, t)))
                st.settle()

            def best_pairs(h):
                hold()
                for s, t in units[:-1]:
                    st.did(V.max_index(top_at[:, s, t, 8:16], top[:, s, t, 8:16], rest[:, s * NT + t, :]))
                s, t = units[-1]
                V.max_index(top_at[:, s, t, 8:16], top[:, s, t, 8:16], rest[:, s * NT + t, :]).then_inc(tops_done, 1)

                for t in range(NT):
                    st.did(V.tensor_tensor(cand[:, t, :].rearrange("p (a b) -> p a b", a=TOPK),
                                           top[:, 0, t, :].unsqueeze(2).to_broadcast([P, TOPK, TOPK]),
                                           top[:, 1, t, :].unsqueeze(1).to_broadcast([P, TOPK, TOPK]), ALU.add))
                dve.wait_ge(tops_done, h + 1)
                st.did(V.tensor_copy(top_atf[:, :, :, :], top_at[:, :, :, :]))
                st.settle()
                hold()
                for t in range(NT):
                    st.did(V.max(best[:, t, 0:8], cand[:, t, :]))
                st.settle()
                hold()
                for t in range(NT):
                    st.did(V.match_replace(cand_rest[:, t, :], best[:, t, 0:8], cand[:, t, :], -3e38))
                st.settle()
                hold()
                for t in range(NT):
                    st.did(V.max(best[:, t, 8:16], cand_rest[:, t, :]))
                st.settle()

            def index_of(h, s):
                m3 = match[:, :, :, :].rearrange("p t a b -> p (t a) b")
                st.did(V.tensor_tensor(m3, iota[:, 0:TOPK].unsqueeze(1).to_broadcast([P, NT * TOPK, TOPK]),
                                       best_kf[:, s, :, :].rearrange("p t k -> p (t k)").unsqueeze(2)
                                       .to_broadcast([P, NT * TOPK, TOPK]), ALU.is_equal))
                st.settle()
                st.did(V.tensor_tensor(match[:, :, :, :], match[:, :, :, :],
                                       top_atf[:, s, :, :].unsqueeze(2).to_broadcast([P, NT, TOPK, TOPK]), ALU.mult))
                st.settle()
                st.did(V.tensor_reduce(route[:, 1 + s, :, bass.ts(h, TOPK)], match[:, :, :, :], AX, ALU.add))
                st.settle()

            def pair_indices(h):
                hold()
                for t in range(NT):
                    st.did(V.max_index(best_at[:, t, 0:8], best[:, t, 0:8], cand[:, t, :]))
                st.settle()
                hold()
                for t in range(NT):
                    st.did(V.max_index(best_at[:, t, 8:16], best[:, t, 8:16], cand_rest[:, t, :]))
                V.tensor_tensor(gate_e[:, :, :], best[:, :, :], best[:, :, 0:1].to_broadcast([P, NT, TOPK]),
                                ALU.subtract).then_inc(gate_sub, 1)
                st.settle()
                st.did(V.tensor_single_scalar(best_k[:, 0, :, :], best_at[:, :, :], 4, ALU.logical_shift_right))
                st.did(V.tensor_single_scalar(best_k[:, 1, :, :], best_at[:, :, :], 15, ALU.bitwise_and))
                st.settle()
                st.did(V.tensor_copy(best_kf[:, :, :, :], best_k[:, :, :, :]))
                st.settle()
                index_of(h, 0)

            def route_head(h):
                index_of(h, 1)
                dve.wait_ge(gate_exp, h + 1)
                st.did(V.reduce_sum(gate_sum[:, :], gate_e[:, :, :], AX))
                st.settle()
                st.did(V.reciprocal(gate_inv[:, :], gate_sum[:, :]))
                st.settle()
                V.tensor_tensor(route[:, 0, :, bass.ts(h, TOPK)], gate_e[:, :, :],
                                gate_inv[:, :].unsqueeze(2).to_broadcast([P, NT, TOPK]), ALU.mult).then_inc(routed, 1)
                dve.wait_ge(routed, h + 1)

            n0 = S0["peer"] - Q_CHUNKS

            def scale_chunk(uc, b, tiles, pre=True):
                dve.wait_ge(tile_done, tiles)
                if pre:
                    if not (isinstance(uc, int) and uc < 2):
                        dve.wait_ge(pre_stored[b], (uc - b) * 8)
                else:
                    dve.wait_ge(act_wlo, uc - 1)
                V.tensor_tensor(ut[b][:, :], ps[:, 6 + b, :], rstd[:, :], ALU.mult).then_inc(chunk_scaled, 1)

            def pre_lo(c):
                lo(n0 + c + 1, (c + 1) % 2)

            def retrieve(h, b, i, m):
                n = S0["pq"] + 4 * h
                scale_chunk(2 * h - 1, 1, CUM[m - 1] + 8 * i)
                lo(n + 1, 1)
                pair_indices(h - 1)
                lo(n + 2, 0)
                route_head(h - 1)
                lo(n + 3, 1)
                best_keys(h, b)
                scale_chunk(2 * h, 0, CUM[m + 2] + 8 * i)
                lo(n + 4, 0)
                best_pairs(h)

            lo(S0["pq"] + 1, 1)
            inverse_root("ffn", D, 4)
            lo(S0["pq"] + 2, 0)
            token_rms(2, 5)
            lo(S0["pq"] + 3, 1)
            best_keys(0, 0)
            scale_chunk(0, 0, CUM[S0["pq"] + 2])
            lo(S0["pq"] + 4, 0)
            best_pairs(0)
            retrieve(1, 1, 0, S0["pq"] + 4)
            with st.loop(HEADS // 2 - 1, 2 * (KEY_STEPS + PAIR_STEPS)) as i:
                for b in range(2):
                    retrieve(2 * i + 2 + b, b, i, S0["pq"] + 8 + 4 * b)
            scale_chunk(Q_CHUNKS - 1, 1, CUM[S0["peer"] - 1])
            pre_lo(Q_CHUNKS)
            pair_indices(HEADS - 1)
            scale_chunk(Q_CHUNKS, 0, CUM[n0 + Q_CHUNKS])
            pre_lo(Q_CHUNKS + 1)
            route_head(HEADS - 1)
            scale_chunk(Q_CHUNKS + 1, 1, CUM[n0 + Q_CHUNKS + 1])
            pre_lo(Q_CHUNKS + 2)

            dve.wait_ge(hk_ready, 3)

            def one_hots(t, qs):
                for q in qs:
                    u = 4 * t + q
                    b = q % 2
                    if not (isinstance(u, int) and u < 2):
                        dve.wait_ge(gquad_done, u - 1)
                    V.tensor_tensor(oh1[:, b, :, :], iota[:, :].unsqueeze(1).to_broadcast([P, 4, P]),
                                    hk[:, 1, bass.ts(u, 4)].unsqueeze(2).to_broadcast([P, 4, P]), ALU.is_equal)
                    for k in range(4):
                        ins = V.tensor_scalar(oh2[:, b, k, :], iota[:, :], hk[:, 2, bass.ds(4 * u + k, 1)],
                                              hk[:, 0, bass.ds(4 * u + k, 1)], ALU.is_equal, ALU.mult)
                    ins.then_inc(onehot_ready, 1)

            def gate_beat(t, b, i):
                c = GATES_AT + b
                one_hots(t, range(1))
                scale_chunk(GATES_AT - 1 + t, (c - 1) % 2, CUM[n0 + c - 1] + 4 * i)
                one_hots(t, range(1, 2))
                lo(n0 + GATES_AT + 1 + t, (c + 1) % 2)
                one_hots(t, range(2, 4))

            for b in range(4):
                gate_beat(b, b, 0)
            with dve.Fori(1, BEATS // 4) as i:
                for b in range(4):
                    gate_beat(4 * i + b, b, i)

            def apply_gates(uc, j, b, src):
                t3 = src[:, :].rearrange("p (b t) -> p b t", b=NTB)
                V.tensor_tensor(t3, t3, gtile[b][:, :, j, :], ALU.mult).then_inc(act_gated, 1)

            def weight_lo(uc, j, b, src):
                dve.wait_ge(act_whi, uc + 1)
                V.tensor_tensor(actL[b][:, j, :], src[:, :], actH[b][:, j, :].bitcast(F), ALU.subtract).then_inc(act_wlo, 1)

            def accumulate(q, tiles, done):
                for m in range(4):
                    dve.wait_ge(tile_done, tiles + m + 1)
                    if m == 0 and q == 0 and not (isinstance(done, int) and done <= 0):
                        dve.wait_ge(h_acc, done)
                    h = hT[:, 4 * q + m, :]
                    V.tensor_tensor(h, h, ps[:, 2 + m, :], ALU.add).then_inc(h_acc, 1)

            def prepared(c, j, b, gates=None):
                dve.wait_ge(pre_loaded[j % 2], (c - j % 2) * 8 + 16)
                if gates is not None:
                    dve.wait_ge(gates_loaded[b], gates)
                apply_gates(c, j, b, tmp[j % 2])

            for c in range(GATES_AT + BEATS, NPRE):
                scale_chunk(c - 1, (c - 1) % 2, CUM[n0 + c - 1])
                pre_lo(c)
                if c >= NPRE - 2:
                    w = 2 * (c - NPRE + 2)
                    prepared(w, w, 0, gates=16 if w == 0 else None)
                    prepared(w + 1, w + 1, 0)
                    weight_lo(w, w, 0, tmp[0])
                    weight_lo(w + 1, w + 1, 0, tmp[1])
            scale_chunk(NPRE - 1, 1, CUM[n0 + NPRE - 1])

            def prepared_group(g, b, m, i):
                for j in range(GROUP):
                    lo(m + j + 1 + 8 * i, (j + 1) % 2)
                    prepared(GROUP * g + j, j, b, gates=8 * (g - b) + 16 if j == 0 else None)
                    weight_lo(GROUP * g + j, j, b, tmp[j % 2])
                    accumulate(j, CUM[m + j - 1] + 32 * i, 16 * (g - 1))

            prepared_group(1, 1, n0 + NPRE, 0)
            with dve.Fori(0, PRE_GROUPS // 2 - 1) as i:
                for b in range(2):
                    prepared_group(2 * i + 2 + b, b, n0 + NPRE + GROUP * (1 + b), i)

            s0 = n0 + 2 * NPRE - GROUP
            with dve.Fori(0, (NGROUPS - PRE_GROUPS) // 2) as i:
                for b in range(2):
                    g = 2 * i + PRE_GROUPS + b
                    for j in range(GROUP):
                        m = s0 + 8 * b + 2 * j
                        c = GROUP * g + j
                        lo(m + 1 + 16 * i, 1)
                        scale_chunk(c, j % 2, CUM[m] + 40 * i, pre=False)
                        if j == 0:
                            dve.wait_ge(gates_loaded[b], 8 * (g - b) + 16)
                        dve.wait_ge(gelu_done, c + 1)
                        apply_gates(c, j, b, ut[j % 2])
                        lo(m + 2 + 16 * i, 0)
                        weight_lo(c, j, b, ut[j % 2])
                        accumulate(j, CUM[m] + 40 * i, 16 * (g - 1))
            last = S0["proj"] - GROUP
            for j in range(GROUP):
                lo(last + j + 1, (j + 1) % 2)
                if j == 0:
                    dve.wait_ge(p_hi, 1)
                    V.tensor_tensor(pL[:, :, :], pRaw[:, :, :], pH[:, :, :].bitcast(F), ALU.subtract).then_inc(p_lo, 1)
                accumulate(j, CUM[last + j - 1], 16 * (NGROUPS - 1))
                for m in range(4):
                    add_square("ple", 4 * j + m, first=j + m == 0)
                    gain_lo("ple", 4 * j + m)
            lo(S0["proj"] + 1, 1)
            inverse_root("ple", D, 7)
            lo(S0["gate"], 0)
            dve.wait_ge(proj_copied, 16)

            def gated(i, j, first=False):
                lo(S0["gate"] + 2 * i + j + 1, (j + 1) % 2)
                if isinstance(i, int) and (i, j) == (6, 1):
                    lo(S0["gate"] + 15, 1)
                m = 2 * i + j
                dve.wait_ge(tile_done, CUM[S0["gate"] + j] + 2 * i)
                if not first and not (isinstance(i, int) and i == 0):
                    dve.wait_ge(h_gated, m - 1)
                V.tensor_tensor(tmp[j][:, :], ps[:, j, :], rstd[:, :], ALU.mult).then_inc(g_scaled, 1)
                dve.wait_ge(sig_done, m + 1)
                st.did(V.tensor_tensor(tmp[j][:, :], tmp[j][:, :], projT[:, m, :], ALU.mult))
                st.settle()
                V.tensor_tensor(hT[:, m, :], hT[:, m, :], tmp[j][:, :], ALU.add).then_inc(h_gated, 1)
                add_square("final", m, first=first, par=j)

            for j in range(2):
                gated(0, j, first=j == 0)
            with st.loop(5, 2) as i:
                for j in range(2):
                    gated(i + 1, j)
            for j in range(2):
                gated(6, j)

            def half_scaled(half, j):
                t = slice(256 * half, 256 * half + 256)
                dve.wait_ge(tile_done, CUM[S0["gate"] + 13] + 2 * half + j + 1)
                dve.wait_ge(h_gated, 12 + 2 * half + j + 1)
                V.tensor_tensor(tmp[j][:, t], ps[:, 2 * half + j, t], rstd[:, t], ALU.mult).then_inc(g_scaled, 1)

            def half_gated(half, j):
                t = slice(256 * half, 256 * half + 256)
                n = 14 + 2 * half + j
                dve.wait_ge(sig_done, n + 1)
                st.did(V.tensor_tensor(tmp[j][:, t], tmp[j][:, t], projT[:, 14 + j, t], ALU.mult))
                st.settle()
                V.tensor_tensor(hT[:, 14 + j, t], hT[:, 14 + j, t], tmp[j][:, t], ALU.add).then_inc(h_gated, 1)

            def half_square(half, j):
                t = slice(256 * half, 256 * half + 256)
                n = N_SQ["final"] + 14 + 2 * half + j
                dve.wait_ge(sq_ready, n + 1)
                dve.wait_ge(sq_added, n)
                V.tensor_tensor(ssum[:, t], ssum[:, t], sq[j][:, t], ALU.add).then_inc(sq_added, 1)

            def final(half, tiles):
                t = slice(256 * half, 256 * half + 256)
                dve.wait_ge(row_spread, 2 + half)
                dve.wait_ge(h_gated, 16 + 2 * half)
                for k in tiles:
                    V.scalar_tensor_tensor(hT[:, k, t], hT[:, k, t], gain("final", k), ps[:, 7 - half, t],
                                           ALU.mult, ALU.mult).then_inc(out_ready, 1)

            for j in range(2):
                half_scaled(0, j)
                half_gated(0, j)
                half_square(0, j)
            row_mean_of(2, D, 7, slice(0, 2))
            row_inverse(2, slice(0, 2))
            half_scaled(1, 0)
            half_gated(1, 0)
            half_square(1, 0)
            final(0, range(7))
            half_scaled(1, 1)
            final(0, range(7, 9))
            half_gated(1, 1)
            final(0, range(9, 11))
            half_square(1, 1)
            final(0, range(11, 13))
            row_mean_of(3, D, 6, slice(2, 4))
            row_inverse(3, slice(2, 4))
            final(0, range(13, 16))
            final(1, range(16))

        @block.tensor
        def _(pe):
            mm = nc.tensor.matmul

            def three(out, wh, wl, xh, xl, start, stop):
                mm(out, wh, xh, start=start, stop=False)
                mm(out, wh, xl, start=False, stop=False)
                return mm(out, wl, xh, start=False, stop=stop)

            def norm_sum(name, bank):
                pe.wait_ge(sq_added, N_SQ[name] + {"cq": 4, "ckv": 2, "sgu": 8, "attn": 8}.get(name, 16))
                mm(ps[:, bank, :], ones[:, :], ssum[:, :], start=True, stop=True).then_inc(sum_done, 1)

            def row_sums(name, count, bank, t):
                pe.wait_ge(sq_added, N_SQ[name] + count)
                for i in range(t.start, t.stop):
                    ins = mm(ps[:, bank, i:i + 1], ssum[:, i * P:(i + 1) * P], ones[:, 0:1], start=True, stop=True)
                ins.then_inc(row_summed, 1)

            def row_spread_out(n, bank, t):
                pe.wait_ge(row_diag, n)
                mm(ps[:, bank, t.start * P:t.stop * P], ones[:, :], diag[:, t, :].rearrange("p t k -> p (t k)"),
                   start=True, stop=True).then_inc(row_spread, 1)

            def token_rms(n, bank):
                pe.wait_ge(rstd_ready, n)
                for t in range(NT):
                    ins = mm(ps[:, bank, t:t + 1], rstd[:, t * P:(t + 1) * P], ident[:, 0:1], start=True, stop=True)
                ins.then_inc(tok_done, 1)

            def tile(n, parity, bank, order=range(KD), waits=None, after=None, every=1):
                pe.wait_ge(lo_ready, n + 1)
                for j, k in enumerate(order):
                    if waits is not None:
                        pe.wait_ge(act_lo, waits + j + 1)
                    w = slice(k * P, (k + 1) * P)
                    ins = three(ps[:, bank, :], wH[parity][:, w], wL[parity][:, w], aH[:, k, :], aL[:, k, :],
                                j == 0, j == KD - 1)
                    if after is not None and j % every == every - 1 and j < KD - 1:
                        after(ins, j // every)
                ins.then_inc(tile_done, 1)
                if after is not None and every > 1:
                    after(ins, KD // every - 1)


            def v_block(cb, waits=None):
                for s in range(4):
                    early = waits is not None and s == 0
                    if early:
                        pe.wait_ge(first_lo, 1)
                    else:
                        pe.wait_ge(lo_ready, S0["v"] + 4 * cb + s + 1)
                    for tt in range(NT):
                        if s == 0 and waits is None:
                            pe.wait_ge(v_gelu, tt + 1)
                        for k4 in range(4):
                            k = 4 * s + k4
                            if early and (tt, k4) == (0, 2):
                                pe.wait_ge(lo_ready, 1)
                            if waits is not None and tt == 0:
                                pe.wait_ge(act_lo, waits + k + 1)
                            w = slice(k4 * 512, (k4 + 1) * 512)
                            t = slice(tt * P, (tt + 1) * P)
                            ins = three(ps[:, tt, :], aH[:, k, t], aL[:, k, t], wH[s % 2][:, w], wL[s % 2][:, w], k == 0, k == KD - 1)
                        if s == 3 or tt == NT - 1:
                            ins.then_inc(tile_done, 1)
                    if waits is not None and s == 1:
                        pe.wait_ge(consts_ready, 3)
                        norm_sum("mix", 7)
                    if waits is not None and s == 2:
                        token_rms(NORMS["mix"] + 1, 7)

            v_block(0, waits=0)
            v_block(1)
            for j in range(7):
                n = S0["c"] + j
                if j == 1:
                    pe.wait_ge(tok_ready, 1)
                if j >= 2:
                    pe.wait_ge(c_copied, j - 1)
                tile(n, n % 2, 6 + j % 2)
            for m in range(8):
                if m >= 2:
                    pe.wait_ge(u_scaled, m - 1)
                tile(S0["u"] + m, (m + 1) % 2, 4 + m % 2)
                if m == 0:
                    pe.wait_ge(v_gelu, 8)
                    norm_sum("cq", 0)
                if m == 3:
                    norm_sum("ckv", 1)

            def spatial(g):
                if g >= 4:
                    pe.wait_ge(sgu_ready, g - 3)
                for c in range(NT):
                    t = slice(c * P, (c + 1) * P)
                    ins = mm(ps[:, g % 4, t], vtok[:, c, g * P:(g + 1) * P], wsT[:, g, :], start=True, stop=True)
                ins.then_inc(mix_done, 1)

            def swap(j, src):
                mm(ps[:, 2 + j % 2, :], perm[:, :], src, start=True, stop=True).then_inc(swap_done, 1)

            pe.wait_ge(v_ready, 4)
            pe.wait_ge(mean_ready, NORMS["ckv"] + 1)
            for g in range(4):
                spatial(g)
            pe.wait_ge(act_lo, N_SC["cq"] + KQ)
            pe.wait_ge(u_scaled, 8)
            for s in range(3):
                n = S0["uq"] + s
                pe.wait_ge(lo_ready, n + 1)
                for m in range(4):
                    t = 4 * s + m
                    if t >= 4:
                        pe.wait_ge(uq_copied, t - 3)
                    elif t in (2, 3):
                        pe.wait_ge(c_copied, 7)
                    for k in range(KQ):
                        w = slice(k * 512 + m * P, k * 512 + (m + 1) * P)
                        ins = three(ps[:, 4 + t % 4, :], wH[n % 2][:, w], wL[n % 2][:, w], cqH[:, k, :], cqL[:, k, :], k == 0, k == KQ - 1)
                    ins.then_inc(tile_done, 1)
                    if s == 0:
                        spatial(4 + m)
            pe.wait_ge(sgu_ready, 8)
            pe.wait_ge(perm_loaded, 32)
            swap(0, cT[:, 6, :])
            for s in range(2):
                n = S0["ukv"] + s
                pe.wait_ge(lo_ready, n + 1)
                if s == 0:
                    pe.wait_ge(act_lo, N_SC["ckv"] + KKV)
                for m in range(8):
                    if m < 4 and s == 0:
                        pe.wait_ge(uq_copied, 9 + m)
                    else:
                        pe.wait_ge(kv_copied, 8 * s + m - 3)
                    for k in range(KKV):
                        if s == 0:
                            w = slice(k * 1024 + m * P, k * 1024 + (m + 1) * P)
                            ins = three(ps[:, 4 + m % 4, :], wH[n % 2][:, w], wL[n % 2][:, w], ckvH[:, k, :], ckvL[:, k, :], k == 0, k == 1)
                        else:
                            w = slice(k * 1024 + (m // 4) * 512, k * 1024 + (m // 4) * 512 + 512)
                            t = slice((m % 4) * P, (m % 4 + 1) * P)
                            ins = three(ps[:, 4 + m % 4, :], ckvH[:, k, t], ckvL[:, k, t], wH[n % 2][:, w], wL[n % 2][:, w], k == 0, k == 1)
                    ins.then_inc(tile_done, 1)
                    if s == 0 and m == 0:
                        norm_sum("sgu", 0)
                    if s == 0 and m % 2 == 1:
                        j = m // 2
                        pe.wait_ge(uq_copied, 9 + j)
                        if j >= 1:
                            pe.wait_ge(rope_ready, j)
                        swap(1 + j, qT[:, 8 + j, :])
            pe.wait_ge(kv_copied, 16)
            pe.wait_ge(rope_ready, 5)
            pe.wait_ge(mean_ready, NORMS["sgu"] + 1)
            ITEMS = HEADS * NT
            for n in range(ITEMS + 3):
                if n < ITEMS:
                    h, qt = divmod(n, NT)
                    w = P * (qt + 1)
                    t = slice(qt * P, w)
                    if n >= 3:
                        pe.wait_ge(exp_done, n - 2)
                    r = slice(64 * (h % 2), 64 * (h % 2) + 64)
                    o = ps[:, n % 3, 0:w]
                    mm(o, qT[:, h, t], kT[:, h, 0:w], start=True, stop=False)
                    mm(o, qT[r, 8 + h // 2, t], krT[r, 0:w], start=False, stop=False)
                    mm(ps[:, n % 3, t], identR[:, :], causalR[:, :], start=False, stop=True).then_inc(score_done, 1)
                m = n - 2
                if 0 <= m < ITEMS:
                    pe.wait_ge(p_ready, m + 1)
                    if m >= 2:
                        pe.wait_ge(pt_copied, m - 1)
                    for j in range(m % NT + 1):
                        s = slice(j * P, (j + 1) * P)
                        ins = nc.tensor.transpose(ps[:, 3 + m % 2, s], prob[m % 2][:, s], ident[:, :])
                    ins.then_inc(pt_done, 1)
                m = n - 3
                if 0 <= m < ITEMS:
                    h, qt = divmod(m, NT)
                    pe.wait_ge(pt_copied, m + 1)
                    if qt == 0 and h >= 2:
                        pe.wait_ge(o_copied, h - 1)
                    for j in range(qt + 1):
                        s = slice(j * P, (j + 1) * P)
                        ins = mm(ps[:, 5 + h % 2, qt * P:(qt + 1) * P], vA[:, j, h * P:(h + 1) * P], probT[m % 2][:, s],
                                 start=j == 0, stop=j == qt)
                    ins.then_inc(pv_done, 1)
            pe.wait_ge(lo_ready, S0["out"] + 2)
            together = KD // 2 + 1
            order = [(i, j) for i in range(together) for j in range(2)] + \
                    [(i, j) for j in range(2) for i in range(together, KD)]
            for i, j in order:
                k = OUT_ORDER[i]
                w = slice(k * P, (k + 1) * P)
                if j == 0:
                    pe.wait_ge(act_lo, N_SC["sgu"] + i + 1)
                ins = three(ps[:, j, :], wH[j][:, w], wL[j][:, w], aH[:, k, :], aL[:, k, :], i == 0, i == KD - 1)
                if i == KD - 1:
                    ins.then_inc(tile_done, 1)
                if (i, j) == (0, 1):
                    row_sums("attn", 8, 7, slice(0, NT))
                if (i, j) == (2, 0):
                    row_spread_out(1, 7, slice(0, NT))
            with pe.Fori(1, 7) as i:
                for j in range(2):
                    pe.wait_ge(h_mixed, 2 * i + j - 1)
                    tile(S0["out"] + 2 * i + j, j, j)
            pe.wait_ge(h_mixed, 13)
            tile(S0["out"] + 14, 0, 0)
            pe.wait_ge(h_mixed, 14)
            tile(S0["out"] + 15, 1, 1, after=lambda ins, j: ins.then_inc(a_read, 1))

            def scores(h, b):
                for s in range(2):
                    pe.wait_ge(pq_copied, 2 * h + s + 1)
                    for t in range(NT):
                        ts = slice(t * P, (t + 1) * P)
                        ins = mm(ps[:, 2 + 2 * b + s, ts], pqT[b][:, s, ts], keys[:, h, s, :], start=True, stop=True)
                    ins.then_inc(ps_done, 1)

            def u_slot(n, parity, uc, j, first=False, **more):
                if not first:
                    pe.wait_ge(chunk_scaled, uc - 1)
                tile(n, parity, 6 + j % 2, **more)

            def head_slots(h, b, waits=None):
                n = S0["pq"] + 4 * h
                for s in range(2):
                    if not (isinstance(h, int) and h == 0):
                        pe.wait_ge(pq_copied, 2 * h + s - 1)
                    else:
                        pe.wait_ge(h_mixed, 15 + s)
                    tile(n + s, s, s, waits=waits if s == 0 else None)
                    if waits is not None:
                        norm_sum("ffn", 4) if s == 0 else token_rms(NORMS["ffn"] + 1, 5)
                if isinstance(h, int):
                    if h == 0:
                        pe.wait_ge(keys_loaded, 16)
                    if h == 1:
                        pe.wait_ge(tok_ready, 2)
                else:
                    pe.wait_ge(tops_done, h - 1)
                scores(h, b)
                for s in range(2):
                    u_slot(n + 2 + s, s, 2 * h + s, s, first=isinstance(h, int) and h == 0)

            head_slots(0, 0, waits=N_SC["ffn"])
            head_slots(1, 1)
            with pe.Fori(1, HEADS // 2) as i:
                for b in range(2):
                    head_slots(2 * i + b, b)
            n0 = S0["peer"] - Q_CHUNKS
            for c in range(Q_CHUNKS, GATES_AT - 1):
                u_slot(n0 + c, c % 2, c, c)
            pe.wait_ge(pq_copied, 16)
            pe.wait_ge(routed, HEADS)
            for r in range(3):
                for t in range(NT):
                    ins = nc.tensor.transpose(ps[:, r, t * P:(t + 1) * P], route[:, r, t, :], ident[:, :])
                ins.then_inc(hkT_done, 1)
            c = GATES_AT - 1
            u_slot(n0 + c, c % 2, c, c)

            def gate_beat(t, b, first=False):
                def quad(_, q):
                    u = 4 * t + q
                    if not first:
                        pe.wait_ge(gquad_copied, u - 3)
                    pe.wait_ge(onehot_ready, u + 1)
                    for k in range(4):
                        ins = mm(ps[:, 2 + q, k * P:(k + 1) * P], oh1[:, q % 2, k, :], oh2[:, q % 2, k, :], start=True, stop=True)
                    ins.then_inc(gquad_done, 1)

                c = GATES_AT + b
                u_slot(n0 + GATES_AT + t, c % 2, GATES_AT + t, c, after=quad, every=4)

            for b in range(4):
                gate_beat(b, b, first=b == 0)
            with pe.Fori(1, BEATS // 4) as i:
                for b in range(4):
                    gate_beat(4 * i + b, b)
            for c in range(GATES_AT + BEATS, NPRE):
                u_slot(n0 + c, c % 2, c, c)

            def v_slot(n, parity, g, q, b, first=False):
                pe.wait_ge(lo_ready, n + 1)
                if q == 0:
                    pe.wait_ge(act_wlo, GROUP * (g + 1))
                for m in range(4):
                    if not (first and q == 0):
                        pe.wait_ge(h_acc, 16 * g + 4 * q + m - 3)
                    for c in range(GROUP):
                        w = slice(c * 512 + m * P, c * 512 + (m + 1) * P)
                        ins = three(ps[:, 2 + m, :], wH[parity][:, w], wL[parity][:, w], actH[b][:, c, :], actL[b][:, c, :], c == 0, c == GROUP - 1)
                    ins.then_inc(tile_done, 1)

            pe.wait_ge(gquad_copied, QUADS)

            def v_group(g, b, first=False):
                for j in range(GROUP):
                    v_slot(n0 + NPRE + GROUP * g + j, j % 2, g, j, b, first=first)

            v_group(0, 0, first=True)
            with pe.Fori(0, PRE_GROUPS // 2 - 1) as i:
                for b in range(2):
                    v_group(2 * i + 1 + b, 1 - b)
            s0 = n0 + 2 * NPRE - GROUP
            with pe.Fori(0, (NGROUPS - PRE_GROUPS) // 2) as i:
                for b in range(2):
                    g = 2 * i + PRE_GROUPS + b
                    for j in range(GROUP):
                        n = s0 + 16 * i + 8 * b + 2 * j
                        u_slot(n, 0, GROUP * g + j, j)
                        v_slot(n + 1, 1, g - 1, j, 1 - b)
            for j in range(GROUP):
                v_slot(S0["proj"] - GROUP + j, j % 2, NGROUPS - 1, j, 1)
            pe.wait_ge(p_lo, 1)
            for s in range(2):
                n = S0["proj"] + s
                pe.wait_ge(lo_ready, n + 1)
                for m in range(8):
                    if s == 0 and m < 4:
                        pe.wait_ge(h_acc, 16 * NGROUPS - 3 + m)
                    else:
                        pe.wait_ge(proj_copied, 8 * s + m - 3)
                    for k in range(2):
                        w = slice(k * 1024 + m * P, k * 1024 + (m + 1) * P)
                        ins = three(ps[:, 2 + m % 4, :], wH[s][:, w], wL[s][:, w], pH[:, k, :], pL[:, k, :], k == 0, k == 1)
                    ins.then_inc(tile_done, 1)
                if s == 0:
                    norm_sum("ple", 7)
            pe.wait_ge(act_lo, N_SC["ple"] + KD)
            tile(S0["gate"], 0, 0)
            tile(S0["gate"] + 1, 1, 1)
            with pe.Fori(1, 7) as i:
                for j in range(2):
                    pe.wait_ge(g_scaled, 2 * i + j - 1)
                    tile(S0["gate"] + 2 * i + j, j, j)
            for half in range(2):
                t = slice(256 * half, 256 * half + 256)
                for j in range(2):
                    pe.wait_ge(lo_ready, S0["gate"] + 15 + j)
                    if half == 0:
                        pe.wait_ge(g_scaled, 13 + j)
                    for k in range(KD):
                        w = slice(k * P, (k + 1) * P)
                        ins = three(ps[:, 2 * half + j, t], wH[j][:, w], wL[j][:, w], aH[:, k, t], aL[:, k, t], k == 0, k == KD - 1)
                        if k == KD - 1:
                            ins.then_inc(tile_done, 1)
                        if (half, j, k) == (1, 0, 10):
                            row_sums("final", 16, 7, slice(0, 2))
                        if (half, j, k) == (1, 0, KD - 1):
                            row_spread_out(2, 7, slice(0, 2))
            row_sums("final", 18, 6, slice(2, 4))
            row_spread_out(3, 6, slice(2, 4))


OUT_ORDER = list(range(8, 16)) + list(range(8))


def kernel(**inputs):
    import numpy as np
    import concourse.bacc as bacc
    from concourse.bass_utils import run_bass_kernel_spmd

    v = {k: np.asarray(x) for k, x in inputs.items()}
    w_in = v["w_in"][0]
    off_kr, off_u, off_v = QL + KVL, QL + KVL + ROPE_D, QL + KVL + ROPE_D + 1024

    def tiles(w):
        k, m = w.shape
        return w.reshape(k // P, P, m // P, P).transpose(2, 1, 0, 3).reshape(m // P, P, k)

    def wide(w, cols):
        k, m = w.shape
        return w.reshape(k // P, P, m // cols, cols).transpose(2, 1, 0, 3).reshape(m // cols, P, k // P * cols)

    uq = v["w_uq"][0].reshape(QL, HEADS, 128 + ROPE_D)
    ukv = v["w_ukv"][0].reshape(KVL, HEADS, 256)
    kr = w_in[:, off_kr:off_u]
    cols = lambda g: g.reshape(-1, P).T
    arrays = {
        "x": v["x"][0].T.reshape(KD, P, T).transpose(1, 0, 2),
        "p": v["p"][0, 0].T.reshape(2, P, T).transpose(1, 0, 2),
        "pos": v["positions"].reshape(1, T),
        "gains": np.concatenate([cols(v[k].reshape(-1)) for k in ("g_mix", "g_ffn", "g_ple", "g_final", "g_out_attn", "g_out_sgu", "g_cq", "g_ckv")], axis=1),
        "rows": np.concatenate([v[k].reshape(1, 1024) for k in ("b_sgu", "g_ln_sgu", "b_ln_sgu")], axis=1),
        "ws": v["w_sgu"][0].transpose(2, 0, 1),
        "keys": np.stack([v["peer_k1"][0], v["peer_k2"][0]], axis=1).transpose(3, 0, 1, 2),
        "s_v": w_in[:, off_v:].reshape(4, 4, P, 2, 512).transpose(3, 0, 2, 1, 4).reshape(8, P, 2048),
        "s_u": tiles(w_in[:, off_u:off_v]),
        "s_c": tiles(np.concatenate([w_in[:, :off_kr], kr, kr], axis=1)),
        "s_uq": wide(np.concatenate([uq[:, :, :128].reshape(QL, -1), uq[:, :, 128:].reshape(QL, -1)], axis=1), 512),
        "s_ukv": wide(np.concatenate([ukv[:, :, :128].reshape(KVL, -1), ukv[:, :, 128:].reshape(KVL, -1)], axis=1), 1024),
        "s_out": tiles(v["w_out"][0]),
        "s_pq": tiles(v["w_peer_q"][0]),
        "s_pu": v["peer_u"][0].reshape(KEYS, KEYS, KD, P).transpose(1, 3, 2, 0).reshape(KEYS, P, 2048),
        "s_pv": v["peer_v"][0].reshape(KEYS, NGROUPS, GROUP, 4, 512).transpose(1, 3, 0, 2, 4).reshape(KEYS, P, 2048),
        "s_proj": wide(v["w_ple_proj"][0], 1024),
        "s_gate": tiles(v["w_ple_gate"][0]),
    }
    half = ROPE_D // 2
    consts = np.zeros((P, 386), np.float32)
    consts[:, 0:128] = np.eye(P, dtype=np.float32)
    consts[:, 128:256] = np.arange(P, dtype=np.float32)[None, :]
    for o in range(P):
        if o % ROPE_D < half:
            consts[o + half, 256 + o] = -1.0
        else:
            consts[o - half, 256 + o] = 1.0
    exponent = -np.arange(half, dtype=np.float32) / np.float32(half)
    consts[:, 384:386] = np.tile(np.power(np.float32(10000.0), exponent).astype(np.float32), 4)[:, None]
    arrays["consts"] = consts
    arrays = {k: np.ascontiguousarray(x) for k, x in arrays.items()}

    nc = bacc.Bacc("TRN2", target_bir_lowering=False, num_devices=1)
    aps = {k: nc.dram_tensor(k, x.shape, mybir.dt.from_np(x.dtype), kind="ExternalInput").ap() for k, x in arrays.items()}
    stream = {k[2:]: x for k, x in aps.items() if k.startswith("s_")}
    gates = nc.dram_tensor("gates", (NTB, KEYS, KEYS, TB), mybir.dt.float32, kind="Internal").ap()
    out = nc.dram_tensor("out", (P, KD, T), mybir.dt.float32, kind="ExternalOutput").ap()
    pre = nc.dram_tensor("pre", (NPRE, P, T), mybir.dt.float32, kind="Internal").ap()
    trunk_layer(nc, aps, stream, out, gates, pre)
    r = run_bass_kernel_spmd(nc, [arrays], core_ids=[0])
    return r.results[0]["out"].transpose(1, 0, 2).reshape(D, T).T.reshape(1, T, D)
```
